# Optimizing a Trainium2 kernel written in Bass

```python
import functools
import jax, jax.numpy as jnp
from jax import lax
import numpy as np

D_MODEL = 1024
BATCH = 1
SEQ = 512
DEPTH = 1
DEC_BATCH = 8
DEC_SEQ = 8
PAST_LEN = 1024
PAGE_SIZE = 128

HEAD_DIM = 64
RWKV_HEADS = 8
RWKV_WIDTH = RWKV_HEADS * HEAD_DIM
W_RANK = 64
A_RANK = 64
G_RANK = 128
RWKV_COLS = 3 * RWKV_WIDTH + W_RANK + A_RANK + G_RANK
RWKV_SPLITS = (RWKV_WIDTH, 2 * RWKV_WIDTH, 3 * RWKV_WIDTH, 3 * RWKV_WIDTH + W_RANK, 3 * RWKV_WIDTH + W_RANK + A_RANK)
GN_EPS = 64e-5
NSA_HEADS = 8
NSA_KV = 2
NSA_GROUP = NSA_HEADS // NSA_KV
NSA_WIDTH = NSA_HEADS * HEAD_DIM
KV_WIDTH = NSA_KV * HEAD_DIM
N_NSA_BRANCH = 3
NSA_COLS = NSA_WIDTH + N_NSA_BRANCH * 2 * KV_WIDTH + N_NSA_BRANCH * NSA_HEADS
CMP_BLOCK = 32
CMP_STRIDE = 16
CMP_RATIO = CMP_BLOCK // CMP_STRIDE
CMP_HIDDEN = 256
SEL_BLOCK = 64
N_SELECT = 16
WINDOW = 512
Q_BLOCK = 128
ROPE_THETA = 10000.0
IN_COLS = RWKV_COLS + NSA_COLS + 2 * D_MODEL
PEER_HEADS = 8
PEER_DK = 128
N_KEYS = 128
N_EXPERTS = N_KEYS * N_KEYS
PEER_TOPK = 16
PEER_BLOCK = 256
PLE_DIM = 256
RMS_EPS = 1e-6

kernel_name = 'rwkv7_nsa_peer_hybrid_step'

def rmsnorm(x, g):
    xf = x.astype(jnp.float32)
    y = xf * lax.rsqrt(jnp.mean(xf * xf, -1, keepdims=True) + RMS_EPS)
    return (y * g).astype(x.dtype)

def rope(x, pos):
    half = HEAD_DIM // 2
    inv = ROPE_THETA ** (-jnp.arange(half, dtype=jnp.float32) / half)
    ang = pos.astype(jnp.float32)[:, None] * inv
    cos, sin = jnp.cos(ang)[:, None, :], jnp.sin(ang)[:, None, :]
    xf = x.astype(jnp.float32)
    x1, x2 = xf[..., :half], xf[..., half:]
    return jnp.concatenate([x1 * cos - x2 * sin, x2 * cos + x1 * sin], -1).astype(x.dtype)

def masked_softmax(s, mask):
    s = jnp.where(mask, s.astype(jnp.float32), -jnp.inf)
    m = jnp.max(s, -1, keepdims=True)
    m = jnp.where(jnp.isfinite(m), m, 0.0)
    e = jnp.exp(s - m)
    return e / jnp.maximum(jnp.sum(e, -1, keepdims=True), 1e-30)

def rwkv_mix(zr, z_prev0, wkv0, lp):
    B, T, _ = zr.shape
    f32 = jnp.float32
    z_prev = jnp.concatenate([z_prev0[:, None, :].astype(zr.dtype), zr[:, :-1]], axis=1)
    xs = zr + (z_prev - zr) * lp['rwkv_mu']
    r, k, v, wl, al, gl = jnp.split(xs, RWKV_SPLITS, axis=-1)
    w = -jax.nn.softplus(-(lp['rwkv_w0'] + jnp.tanh(wl) @ lp['rwkv_w_up'])) - 0.5
    a = jax.nn.sigmoid(lp['rwkv_a0'] + al @ lp['rwkv_a_up'])
    g = jax.nn.sigmoid(gl) @ lp['rwkv_g_up']
    heads = lambda t: t.astype(f32).reshape(B, T, RWKV_HEADS, HEAD_DIM)
    kk = heads(k * lp['rwkv_k_k'])
    kk = kk / jnp.maximum(jnp.sqrt(jnp.sum(kk * kk, -1, keepdims=True)), 1e-12)
    k = k * (1.0 + (a - 1.0) * lp['rwkv_k_a'])
    r_h, k_h, v_h, a_h = heads(r), heads(k), heads(v), heads(a)
    decay = jnp.exp(-jnp.exp(heads(w)))

    def step(S, inp):
        r_t, k_t, v_t, d_t, kk_t, a_t = inp
        sa = jnp.einsum('bhvk,bhk->bhv', S, kk_t)
        S = S * d_t[:, :, None, :] - sa[..., None] * (kk_t * a_t)[:, :, None, :] + v_t[..., None] * k_t[:, :, None, :]
        return S, jnp.einsum('bhvk,bhk->bhv', S, r_t)

    seq = tuple(jnp.swapaxes(t, 0, 1) for t in (r_h, k_h, v_h, decay, kk, a_h))
    s_fin, out = lax.scan(step, wkv0.astype(f32), seq)
    out = jnp.swapaxes(out, 0, 1)
    mu = jnp.mean(out, -1, keepdims=True)
    var = jnp.mean(jnp.square(out - mu), -1, keepdims=True)
    on = ((out - mu) * lax.rsqrt(var + GN_EPS)).reshape(B, T, RWKV_WIDTH) * lp['rwkv_gn_w'] + lp['rwkv_gn_b']
    bonus = jnp.sum(r_h * k_h * lp['rwkv_r_k'], -1, keepdims=True) * v_h
    o = (on + bonus.reshape(B, T, RWKV_WIDTH)) * g
    return o.astype(zr.dtype), s_fin, zr[:, -1]

def nsa_project(zn, pos, lp):
    B, T, _ = zn.shape
    q = zn[..., :NSA_WIDTH].reshape(B, T, NSA_HEADS, HEAD_DIM)
    kv = zn[..., NSA_WIDTH:NSA_WIDTH + 6 * KV_WIDTH].reshape(B, T, N_NSA_BRANCH, 2, NSA_KV, HEAD_DIM)
    gates = jax.nn.sigmoid(zn[..., NSA_WIDTH + 6 * KV_WIDTH:].reshape(B, T, NSA_HEADS, N_NSA_BRANCH))
    qn = rmsnorm(q, lp['q_norm'])
    qr = rope(qn, pos)

    def prep(kvb, gk):
        return jnp.stack([rope(rmsnorm(kvb[:, :, 0], gk), pos), kvb[:, :, 1]], axis=2)

    return qn, qr, kv[:, :, 0], prep(kv[:, :, 1], lp['k_norm'][1]), prep(kv[:, :, 2], lp['k_norm'][2]), gates

def compress(kv_raw, lp):
    n_chunk = kv_raw.shape[0] // CMP_STRIDE
    nc = n_chunk - CMP_RATIO + 1
    chunks = kv_raw[:n_chunk * CMP_STRIDE].reshape(n_chunk, CMP_STRIDE, 2, NSA_KV, HEAD_DIM)
    w1 = lp['cmp_w1'].reshape(2, CMP_RATIO, CMP_STRIDE, HEAD_DIM, CMP_HIDDEN)
    part = jnp.einsum('csekd,ersdf->crekf', chunks, w1)
    hid = part[0:nc, 0]
    for r in range(1, CMP_RATIO):
        hid = hid + part[r:r + nc, r]
    pe_bias = jnp.einsum('esd,esdf->ef', lp['cmp_pe'], lp['cmp_w1'].reshape(2, CMP_BLOCK, HEAD_DIM, CMP_HIDDEN))
    hid = jax.nn.gelu(hid + pe_bias[None, :, None, :])
    out = jnp.einsum('nekf,efd->nekd', hid, lp['cmp_w2'])
    kc = rmsnorm(out[:, 0], lp['k_norm'][0])
    return kc, out[:, 1], jnp.arange(nc) * CMP_STRIDE + CMP_BLOCK - 1

def block_cover_matrix(nsb, nc):
    c0 = jnp.arange(nc) * CMP_STRIDE
    s0 = jnp.arange(nsb) * SEL_BLOCK
    cover = (c0[None, :] <= s0[:, None] + SEL_BLOCK - 1) & (c0[None, :] + CMP_BLOCK - 1 >= s0[:, None])
    return cover.astype(jnp.float32)

def nsa_core(qn, qr, q_pos, kc, vc, c_end, nsb, npb, gather_past, kv_new, kv_win, win_pos, gates):
    tq = qn.shape[0]
    scale = HEAD_DIM ** -0.5
    qn_g = qn.reshape(tq, NSA_KV, NSA_GROUP, HEAD_DIM)
    qr_g = qr.reshape(tq, NSA_KV, NSA_GROUP, HEAD_DIM)
    causal = q_pos[:, None] >= q_pos[None, :]
    p_c = masked_softmax(jnp.einsum('tkgd,nkd->kgtn', qn_g, kc) * scale, c_end[None, :] <= q_pos[:, None])
    o_c = jnp.einsum('kgtn,nkd->tkgd', p_c, vc)
    imp = jnp.einsum('kgtn,jn->ktj', p_c, block_cover_matrix(nsb, kc.shape[0]))
    blk = jnp.arange(nsb)[None, :]
    cur = (q_pos // SEL_BLOCK)[:, None]
    forced = (blk == cur) | (blk == cur - 1) | (blk == 0)
    imp = jnp.where(forced, jnp.inf, jnp.where(blk > cur, -jnp.inf, imp))
    n_sel = min(N_SELECT, nsb)
    sel = lax.top_k(imp, n_sel)[1]
    kv_p = gather_past(sel)
    m_len = n_sel * SEL_BLOCK
    k_p = kv_p[..., 0, :].reshape(NSA_KV, tq, m_len, HEAD_DIM)
    v_p = kv_p[..., 1, :].reshape(NSA_KV, tq, m_len, HEAD_DIM)
    s_sel = jnp.concatenate([jnp.einsum('tkgd,ktmd->kgtm', qr_g, k_p),
                             jnp.einsum('tkgd,skd->kgts', qr_g, kv_new[:, 0])], -1) * scale
    m_past = jnp.repeat(sel < npb, SEL_BLOCK, axis=-1)
    member = jnp.any(sel[..., None] == (q_pos // SEL_BLOCK), axis=-2)
    p_s = masked_softmax(s_sel, jnp.concatenate([m_past, member & causal], -1)[:, None])
    o_s = (jnp.einsum('kgtm,ktmd->tkgd', p_s[..., :m_len], v_p)
           + jnp.einsum('kgts,skd->tkgd', p_s[..., m_len:], kv_new[:, 1]))
    dist = q_pos[:, None] - win_pos[None, :]
    m_w = (dist >= 0) & (dist < WINDOW) & (win_pos >= 0)[None, :]
    p_w = masked_softmax(jnp.einsum('tkgd,skd->kgts', qr_g, kv_win[:, 0]) * scale, m_w)
    o_w = jnp.einsum('kgts,skd->tkgd', p_w, kv_win[:, 1])
    g = gates.reshape(tq, NSA_KV, NSA_GROUP, N_NSA_BRANCH)
    o = o_c * g[..., 0:1] + o_s * g[..., 1:2] + o_w * g[..., 2:3]
    return o.reshape(tq, NSA_WIDTH).astype(qn.dtype)

def nsa_prompt(qn, qr, kv_cmp, kv_sel, kv_win, gates, lp):
    S = qn.shape[1]
    nsb = S // SEL_BLOCK
    kv_idx = jnp.arange(NSA_KV)[:, None, None]

    def per_seq(args):
        qn1, qr1, kvc1, kvs1, kvw1, g1 = args
        kc, vc, c_end = compress(kvc1, lp)
        blocks = kvs1.reshape(nsb, SEL_BLOCK, 2, NSA_KV, HEAD_DIM)
        gather_past = lambda sel: blocks[sel, :, :, kv_idx]
        win_pad = jnp.pad(kvw1, ((WINDOW, 0), (0, 0), (0, 0), (0, 0)))

        def per_block(i):
            t0 = i * Q_BLOCK
            q_pos = t0 + jnp.arange(Q_BLOCK)
            sl = lambda a: lax.dynamic_slice_in_dim(a, t0, Q_BLOCK, 0)
            kw = lax.dynamic_slice_in_dim(win_pad, t0, WINDOW + Q_BLOCK, 0)
            w_pos = t0 - WINDOW + jnp.arange(WINDOW + Q_BLOCK)
            return nsa_core(sl(qn1), sl(qr1), q_pos, kc, vc, c_end, nsb, t0 // SEL_BLOCK,
                            gather_past, sl(kvs1), kw, w_pos, sl(g1))

        return lax.map(per_block, jnp.arange(S // Q_BLOCK)).reshape(S, NSA_WIDTH)

    return lax.map(per_seq, (qn, qr, kv_cmp, kv_sel, kv_win, gates))

def nsa_sample(qn, qr, kv_cmp, kv_sel, kv_win, gates, cache_cmp, cache_sel, page_table, state_win, lp):
    T = qn.shape[1]
    nsb = -(-(PAST_LEN + T) // SEL_BLOCK)
    npb = PAST_LEN // SEL_BLOCK
    bpp = PAGE_SIZE // SEL_BLOCK
    n_pages = PAST_LEN // PAGE_SIZE
    pool_blocks = cache_sel.reshape(cache_sel.shape[0] * bpp, SEL_BLOCK, 2, NSA_KV, HEAD_DIM)
    q_pos = PAST_LEN + jnp.arange(T)
    win_cache = state_win.shape[1]
    w_pos = PAST_LEN - win_cache + jnp.arange(win_cache + T)
    kv_idx = jnp.arange(NSA_KV)[:, None, None]

    def per_seq(args):
        qn1, qr1, kvc1, kvs1, kvw1, g1, pt, sw = args
        past_cmp = cache_cmp[pt].reshape(n_pages * PAGE_SIZE, 2, NSA_KV, HEAD_DIM).astype(kvc1.dtype)
        kc, vc, c_end = compress(jnp.concatenate([past_cmp, kvc1], 0), lp)

        def gather_past(sel):
            j = jnp.minimum(sel, npb - 1)
            return pool_blocks[pt[j // bpp] * bpp + j % bpp, :, :, kv_idx]

        kw = jnp.concatenate([sw.astype(kvw1.dtype), kvw1], 0)
        return nsa_core(qn1, qr1, q_pos, kc, vc, c_end, nsb, npb, gather_past, kvs1, kw, w_pos, g1)

    return lax.map(per_seq, (qn, qr, kv_cmp, kv_sel, kv_win, gates, page_table, state_win))

def peer_ffn(h, lp):
    lead = h.shape[:-1]
    ht = h.reshape(-1, D_MODEL)
    n = ht.shape[0]
    nb = -(-n // PEER_BLOCK)
    ht = jnp.pad(ht, ((0, nb * PEER_BLOCK - n), (0, 0))).reshape(nb, PEER_BLOCK, D_MODEL)

    def block(hb):
        q = (hb @ lp['peer_wq']).reshape(PEER_BLOCK, PEER_HEADS, 2, PEER_DK // 2)
        s = jnp.einsum('thcd,hcnd->thcn', q, lp['peer_keys']).astype(jnp.float32)
        sv, si = lax.top_k(s, PEER_TOPK)
        cand = (sv[:, :, 0, :, None] + sv[:, :, 1, None, :]).reshape(PEER_BLOCK, PEER_HEADS, PEER_TOPK * PEER_TOPK)
        cv, ci = lax.top_k(cand, PEER_TOPK)
        i1 = jnp.take_along_axis(si[:, :, 0], ci // PEER_TOPK, -1)
        i2 = jnp.take_along_axis(si[:, :, 1], ci % PEER_TOPK, -1)
        e = i1 * N_KEYS + i2
        gate = jax.nn.softmax(cv, -1)
        act = jax.nn.gelu(jnp.einsum('td,thkd->thk', hb, lp['peer_u'][e]).astype(jnp.float32))
        return jnp.einsum('thk,thkd->td', (gate * act).astype(hb.dtype), lp['peer_v'][e])

    out = lax.map(block, ht).reshape(nb * PEER_BLOCK, D_MODEL)[:n]
    return out.reshape(*lead, D_MODEL)

def layer_forward(x, p_l, pos, z_prev0, wkv0, attend, lp):
    h = rmsnorm(x, lp['attn_norm'])
    z = h @ lp['w_in']
    o_r, wkv, shift = rwkv_mix(z[..., :RWKV_COLS], z_prev0, wkv0, lp)
    qn, qr, kvc, kvs, kvw, gates = nsa_project(z[..., RWKV_COLS:RWKV_COLS + NSA_COLS], pos, lp)
    o_n = attend(qn, qr, kvc, kvs, kvw, gates)
    zg = z[..., RWKV_COLS + NSA_COLS:]
    merged = (jax.nn.sigmoid(zg[..., :D_MODEL]) * (o_r @ lp['w_rwkv_out'])
              + jax.nn.sigmoid(zg[..., D_MODEL:]) * (o_n @ lp['w_nsa_out']))
    x = x + merged @ lp['w_out']
    x = x + peer_ffn(rmsnorm(x, lp['ffn_norm']), lp)
    x = x + jax.nn.sigmoid(rmsnorm(x, lp['ple_norm']) @ lp['ple_w_gate']) * (p_l @ lp['ple_w_in'])
    return x, kvc, kvs, kvw, wkv, shift

def setup_inputs(seed: int = 0) -> dict:
    key = jax.random.key(seed)
    ks = iter(jax.random.split(key, 64))
    nrm = lambda shape, scale: jax.random.normal(next(ks), shape, jnp.float32) * scale
    gain = lambda shape: 1.0 + nrm(shape, 0.02)
    n_pages = PAST_LEN // PAGE_SIZE
    n_used = DEC_BATCH * n_pages
    n_phys = n_used + max(1, n_used // 4)
    win_cache = min(WINDOW, PAST_LEN)
    page_table = jax.random.permutation(next(ks), n_phys)[:n_used].reshape(DEC_BATCH, n_pages).astype(jnp.int32)
    L = DEPTH
    return {
        'x_prompt': nrm((BATCH, SEQ, D_MODEL), 1.0),
        'x_sample': nrm((DEC_BATCH, DEC_SEQ, D_MODEL), 1.0),
        'cache_cmp_kv': nrm((L, n_phys, PAGE_SIZE, 2, NSA_KV, HEAD_DIM), 1.0),
        'cache_sel_kv': nrm((L, n_phys, PAGE_SIZE, 2, NSA_KV, HEAD_DIM), 1.0),
        'state_win_kv': nrm((L, DEC_BATCH, win_cache, 2, NSA_KV, HEAD_DIM), 1.0),
        'state_wkv': nrm((L, DEC_BATCH, RWKV_HEADS, HEAD_DIM, HEAD_DIM), 0.3),
        'state_shift': nrm((L, DEC_BATCH, RWKV_COLS), 1.0),
        'page_table': page_table,
        'p_prompt': nrm((L, BATCH, SEQ, PLE_DIM), 1.0),
        'p_sample': nrm((L, DEC_BATCH, DEC_SEQ, PLE_DIM), 1.0),
        'attn_norm': gain((L, D_MODEL)),
        'w_in': nrm((L, D_MODEL, IN_COLS), D_MODEL ** -0.5),
        'rwkv_mu': jax.random.uniform(next(ks), (L, RWKV_COLS), jnp.float32),
        'rwkv_w0': jax.random.uniform(next(ks), (L, RWKV_WIDTH), jnp.float32, -3.0, 1.0),
        'rwkv_w_up': nrm((L, W_RANK, RWKV_WIDTH), 0.5 * W_RANK ** -0.5),
        'rwkv_a0': nrm((L, RWKV_WIDTH), 0.5),
        'rwkv_a_up': nrm((L, A_RANK, RWKV_WIDTH), 0.5 * A_RANK ** -0.5),
        'rwkv_g_up': nrm((L, G_RANK, RWKV_WIDTH), G_RANK ** -0.5),
        'rwkv_k_k': 0.85 + nrm((L, RWKV_WIDTH), 0.05),
        'rwkv_k_a': gain((L, RWKV_WIDTH)),
        'rwkv_r_k': nrm((L, RWKV_HEADS, HEAD_DIM), 0.1),
        'rwkv_gn_w': gain((L, RWKV_WIDTH)),
        'rwkv_gn_b': nrm((L, RWKV_WIDTH), 0.02),
        'w_rwkv_out': nrm((L, RWKV_WIDTH, D_MODEL), RWKV_WIDTH ** -0.5),
        'q_norm': gain((L, HEAD_DIM)),
        'k_norm': gain((L, N_NSA_BRANCH, HEAD_DIM)),
        'cmp_pe': nrm((L, 2, CMP_BLOCK, HEAD_DIM), 0.1),
        'cmp_w1': nrm((L, 2, CMP_BLOCK * HEAD_DIM, CMP_HIDDEN), (CMP_BLOCK * HEAD_DIM) ** -0.5),
        'cmp_w2': nrm((L, 2, CMP_HIDDEN, HEAD_DIM), CMP_HIDDEN ** -0.5),
        'w_nsa_out': nrm((L, NSA_WIDTH, D_MODEL), NSA_WIDTH ** -0.5),
        'w_out': nrm((L, D_MODEL, D_MODEL), D_MODEL ** -0.5),
        'ffn_norm': gain((L, D_MODEL)),
        'peer_wq': nrm((L, D_MODEL, PEER_HEADS * PEER_DK), D_MODEL ** -0.5),
        'peer_keys': nrm((L, PEER_HEADS, 2, N_KEYS, PEER_DK // 2), (PEER_DK // 2) ** -0.5),
        'peer_u': nrm((L, N_EXPERTS, D_MODEL), D_MODEL ** -0.5),
        'peer_v': nrm((L, N_EXPERTS, D_MODEL), 0.5),
        'ple_norm': gain((L, D_MODEL)),
        'ple_w_gate': nrm((L, D_MODEL, D_MODEL), D_MODEL ** -0.5),
        'ple_w_in': nrm((L, PLE_DIM, D_MODEL), PLE_DIM ** -0.5),
    }

def reference(x_prompt, x_sample, cache_cmp_kv, cache_sel_kv, state_win_kv, state_wkv, state_shift, page_table,
              p_prompt, p_sample, attn_norm, w_in, rwkv_mu, rwkv_w0, rwkv_w_up, rwkv_a0, rwkv_a_up, rwkv_g_up,
              rwkv_k_k, rwkv_k_a, rwkv_r_k, rwkv_gn_w, rwkv_gn_b, w_rwkv_out, q_norm, k_norm, cmp_pe, cmp_w1,
              cmp_w2, w_nsa_out, w_out, ffn_norm, peer_wq, peer_keys, peer_u, peer_v, ple_norm, ple_w_gate,
              ple_w_in):
    b_p, s_p = x_prompt.shape[:2]
    pos_p = jnp.arange(s_p)
    pos_s = PAST_LEN + jnp.arange(x_sample.shape[1])
    xp, xs = x_prompt, x_sample
    cmp_p, cmp_s, sel_p, sel_s, win_p, win_s = [], [], [], [], [], []
    wkv_p, wkv_s, sh_p, sh_s = [], [], [], []
    for l in range(DEPTH):
        lp = dict(attn_norm=attn_norm[l], w_in=w_in[l], rwkv_mu=rwkv_mu[l], rwkv_w0=rwkv_w0[l],
                  rwkv_w_up=rwkv_w_up[l], rwkv_a0=rwkv_a0[l], rwkv_a_up=rwkv_a_up[l], rwkv_g_up=rwkv_g_up[l],
                  rwkv_k_k=rwkv_k_k[l], rwkv_k_a=rwkv_k_a[l], rwkv_r_k=rwkv_r_k[l], rwkv_gn_w=rwkv_gn_w[l],
                  rwkv_gn_b=rwkv_gn_b[l], w_rwkv_out=w_rwkv_out[l], q_norm=q_norm[l], k_norm=k_norm[l],
                  cmp_pe=cmp_pe[l], cmp_w1=cmp_w1[l], cmp_w2=cmp_w2[l], w_nsa_out=w_nsa_out[l], w_out=w_out[l],
                  ffn_norm=ffn_norm[l], peer_wq=peer_wq[l], peer_keys=peer_keys[l], peer_u=peer_u[l],
                  peer_v=peer_v[l], ple_norm=ple_norm[l], ple_w_gate=ple_w_gate[l], ple_w_in=ple_w_in[l])
        attend_p = functools.partial(nsa_prompt, lp=lp)
        xp, kvc, kvs, kvw, wkv, sh = layer_forward(
            xp, p_prompt[l], pos_p, jnp.zeros((b_p, RWKV_COLS), xp.dtype),
            jnp.zeros((b_p, RWKV_HEADS, HEAD_DIM, HEAD_DIM), jnp.float32), attend_p, lp)
        cmp_p.append(kvc)
        sel_p.append(kvs)
        win_p.append(kvw[:, -min(WINDOW, s_p):])
        wkv_p.append(wkv)
        sh_p.append(sh)
        win_prev = state_win_kv[l]
        attend_s = functools.partial(nsa_sample, cache_cmp=cache_cmp_kv[l], cache_sel=cache_sel_kv[l],
                                     page_table=page_table, state_win=win_prev, lp=lp)
        xs, kvc, kvs, kvw, wkv, sh = layer_forward(xs, p_sample[l], pos_s, state_shift[l], state_wkv[l], attend_s, lp)
        cmp_s.append(kvc)
        sel_s.append(kvs)
        win_s.append(jnp.concatenate([win_prev.astype(kvw.dtype), kvw], 1)[:, -win_prev.shape[1]:])
        wkv_s.append(wkv)
        sh_s.append(sh)
    return (xp, xs, jnp.stack(cmp_p), jnp.stack(cmp_s), jnp.stack(sel_p), jnp.stack(sel_s),
            jnp.stack(win_p), jnp.stack(win_s), jnp.stack(wkv_p), jnp.stack(wkv_s), jnp.stack(sh_p), jnp.stack(sh_s))


_drawn_inputs = setup_inputs


def setup_inputs(seed=0):
    import zlib

    import numpy as np

    out = dict(_drawn_inputs(seed))
    spreads = {}
    factors = {'rwkv_k_k': 3.04,
     'rwkv_k_a': 2.944,
     'rwkv_gn_w': 2.86,
     'rwkv_gn_b': 3.111,
     'q_norm': 6.676,
     'k_norm': 3.558,
     'ple_norm': 45.386}
    for name, (base, spread) in spreads.items():
        noise = np.random.default_rng([zlib.crc32(name.encode()), seed]).standard_normal(out[name].shape)
        drawn = base * np.exp(spread * noise) if base else spread * noise
        out[name] = __import__('jax').numpy.asarray(drawn.astype(out[name].dtype))
    for name, factor in factors.items():
        out[name] = (out[name] * factor).astype(out[name].dtype)
    return out
```

```python
from contextlib import ExitStack

import numpy as np

import concourse.bass as bass
from concourse import mybir

ALU = mybir.AluOpType
ACT = mybir.ActivationFunctionType
AX = mybir.AxisListType
F32 = mybir.dt.float32
F32R = mybir.dt.float32r
U32 = mybir.dt.uint32

P = 128
D_MODEL = 1024
KD = D_MODEL // P
SEQ = 512
DEC_BATCH = 8
DEC_SEQ = 8
TS = DEC_BATCH * DEC_SEQ
T = SEQ + TS
TH = T // 2
PAST = 1024
PAGE = 128
PAGES = PAST // PAGE
HD = 64
HEADS = 8
RCOLS = 14
ZQ = 14
ZK = 18
NZ = 24
NGATE = 24
CMP_STRIDE = 16
CMP_HIDDEN = 256
SEL_BLOCK = 64
WINDOW = 512
CH = 64
TB = 32
NCH = SEQ // CH
N_KEYS = 128
TOPK = 16
PLE = 256
EPS = 1e-6
GN_EPS = 64e-5
DECAY = float(np.exp(-0.5))
SCALE = HD ** -0.5
NEG = -1e30

PARAMS = {}
for _name, _n in (("attn_norm", KD), ("ffn_norm", KD), ("ple_norm", KD), ("mu", RCOLS), ("w0", 4), ("a0", 4),
                  ("k_k", 4), ("k_a", 4), ("r_k", 4), ("gn_w", 4), ("gn_b", 4), ("q_norm", 1), ("k_norm", 3)):
    PARAMS[_name] = (sum(n for _, n in PARAMS.values()), _n)
NPARAM = sum(n for _, n in PARAMS.values())


class Tiles:
    pass


class Chain:

    def __init__(self, eng, sem, base=0):
        self.eng, self.sem, self.base, self.n = eng, sem, base, 0

    def link(self, ins):
        self.n += 1
        ins.then_inc(self.sem, 1)
        self.eng.wait_ge(self.sem, self.base + self.n)


class Steps:

    def __init__(self, sem, names, base=0):
        self.sem, self.names, self.base = sem, names.split(), base

    def at(self, name, i=0):
        return i * len(self.names) + self.base + self.names.index(name) + 1

    def before(self, i):
        return i * len(self.names) + self.base


class Core:

    def __init__(self, nc):
        self.nc = nc
        self.n = 0
        self.used = []

    def sb(self, ctx, name, shape, dt=F32):
        self.n += 1
        return ctx.enter_context(self.nc.sbuf_tensor(f"{name}_{self.n}", shape, dt))

    def sems(self, ctx, *names):
        self.n += 1
        made = [ctx.enter_context(self.nc.semaphore(f"{n}_{self.n}")) for n in names]
        self.used += made
        return made

    def clear_sems(self):
        numbers = sorted({s.num for s in self.used})
        self.used = []
        with self.nc.Block() as block:
            @block.gpsimd
            def _(pool):
                at = 0
                while at < len(numbers):
                    end = at + 1
                    while end < len(numbers) and numbers[end] == numbers[end - 1] + 1:
                        end += 1
                    pool.sem_clear(range(numbers[at], numbers[end - 1] + 1))
                    at = end

    def par(self, name, i=0, lo=0, hi=P):
        at, n = PARAMS[name]
        return self.params[lo:hi, at + i:at + i + 1]

    def bank(self, b, n=512):
        return self.ps[:, b, 0:n]

    def pair(self, b):
        return self.ps[:, b:b + 2, 0:TH]


def halves(ap):
    return ap.rearrange("p (h t) -> p h t", h=2)


def load_stage(k):
    nc = k.nc
    with ExitStack() as ctx:
        loaded, = k.sems(ctx, "loaded")
        pairs = [(k.x, k.d["x"]), (k.params, k.d["params"]), (k.ones, k.d["ones"]), (k.blocks, k.d["blocks"]),
                 (k.ident, k.d["ident"])]
        block = ctx.enter_context(nc.Block())

        @block.sync
        def _(sp):
            for dst, src in pairs:
                sp.dma_start(dst[:] if dst is not k.x else dst.rearrange("p c t -> p (c t)"), src).then_inc(loaded, 16)
            sp.wait_ge(loaded, 16 * len(pairs))


def norm_stage(k, gain, hi, lo):
    nc = k.nc
    with ExitStack() as ctx:
        sq = k.sb(ctx, "sq", [P, KD, T])
        rs = k.sb(ctx, "rs", [P, T])
        squared, summed, mean, rooted, chain, normed, rounded = k.sems(ctx, "squared", "summed", "mean", "rooted", "chain",
                                                                       "normed", "rounded")
        block = ctx.enter_context(nc.Block())

        @block.scalar
        def _(act):
            for c in range(KD):
                nc.scalar.activation(sq[:, c, :], k.x[:, c, :], ACT.Square).then_inc(squared, 1)
            act.wait_ge(mean, 1)
            nc.scalar.activation(rs[:], rs[:], ACT.Sqrt).then_inc(rooted, 1)
            for c in range(KD):
                act.wait_ge(normed, c + 1)
                nc.scalar.activation(hi[:, c, :], sq[:, c, :], ACT.Copy).then_inc(rounded, 1)

        @block.tensor
        def _(pe):
            for c in range(KD):
                pe.wait_ge(squared, c + 1)
                for h in range(2):
                    mm = nc.tensor.matmul(k.bank(h, TH), k.ones[:], sq[:, c, h * TH:(h + 1) * TH],
                                          start=c == 0, stop=c == KD - 1)
            mm.then_inc(summed, 1)

        @block.vector
        def _(dve):
            ch = Chain(dve, chain)
            dve.wait_ge(summed, 1)
            nc.vector.tensor_scalar(halves(rs[:]), k.pair(0), 1.0 / D_MODEL, EPS, ALU.mult, ALU.add).then_inc(mean, 1)
            dve.wait_ge(rooted, 1)
            ch.link(nc.vector.reciprocal(rs[:], rs[:]))
            for c in range(KD):
                nc.vector.scalar_tensor_tensor(out=sq[:, c, :], in0=k.x[:, c, :], scalar=k.par(gain, c),
                                               in1=rs[:], op0=ALU.mult, op1=ALU.mult).then_inc(normed, 1)
            for c in range(KD):
                dve.wait_ge(rounded, c + 1)
                last = nc.vector.tensor_tensor(lo[:, c, :], sq[:, c, :], hi[:, c, :].bitcast(F32), ALU.subtract)
            ch.link(last)


def three_passes(w_hi, w_lo, r_hi, r_lo):
    return (w_hi, r_hi), (w_hi, r_lo), (w_lo, r_hi)


def project_stage(k, w, ntiles, rhs, dst, gates=None):
    nc = k.nc
    ring = 4
    r_hi, r_lo = rhs
    with ExitStack() as ctx:
        wt = k.sb(ctx, "wt", [P, ring, KD, P])
        w_hi = k.sb(ctx, "w_hi", [P, 2, KD, P], F32R)
        w_lo = k.sb(ctx, "w_lo", [P, 2, KD, P], F32R)
        arrived = k.sems(ctx, *[f"arrived{b}" for b in range(ring)])
        rounded, parted, multiplied, taken, gate_w, gate_mm = k.sems(ctx, "rounded", "parted", "multiplied", "taken",
                                                                     "gate_w", "gate_mm")
        block = ctx.enter_context(nc.Block())

        @block.sync
        def _(sp):
            if gates is not None:
                sp.dma_start(gates[1].rearrange("p c n -> p (c n)"), gates[0]).then_inc(gate_w, 16)
            with sp.Fori(0, ntiles // ring) as i:
                for b in range(ring):
                    sp.wait_ge(parted, i * ring + b + 1)
                    sp.dma_start(wt[:, b].rearrange("p c n -> p (c n)"), w[i * ring + b]).then_inc(arrived[b], 16)

        @block.vector
        def _(dve):
            dve.sem_inc(parted, ring)
            with dve.Fori(0, ntiles // ring) as i:
                for b in range(ring):
                    dve.wait_ge(arrived[b], i * 16 + 16)
                    dve.wait_ge(multiplied, i * ring + b + 1)
                    nc.vector.tensor_copy(w_hi[:, b % 2], wt[:, b]).then_inc(rounded, 1)
                    dve.wait_ge(rounded, i * ring + b + 1)
                    nc.vector.tensor_tensor(w_lo[:, b % 2], wt[:, b], w_hi[:, b % 2].bitcast(F32),
                                            ALU.subtract).then_inc(parted, 1)

        @block.tensor
        def _(pe):
            pe.sem_inc(multiplied, 2)
            with pe.Fori(0, ntiles // ring) as i:
                for b in range(ring):
                    pe.wait_ge(parted, i * ring + ring + b + 1)
                    pe.wait_ge(taken, i * ring + b + 1)
                    for c in range(KD):
                        for n, (lhs, r) in enumerate(three_passes(w_hi[:, b % 2, c, :], w_lo[:, b % 2, c, :], r_hi, r_lo)):
                            for h in range(2):
                                mm = nc.tensor.matmul(k.bank(2 * b + h, TH), lhs, r[:, c, h * TH:(h + 1) * TH],
                                                      start=c == 0 and n == 0, stop=c == KD - 1 and n == 2)
                    mm.then_inc(multiplied, 1)
            if gates is not None:
                pe.wait_ge(gate_w, 16)
                pe.wait_ge(taken, ntiles + ring)
                for tt in range(5):
                    n = min(P, T - tt * P)
                    for c in range(KD):
                        for r in (r_hi, r_lo):
                            mm = nc.tensor.matmul(k.ps[0:n, 0, tt * NGATE:(tt + 1) * NGATE],
                                                  r[:, c, tt * P:tt * P + n].bitcast(F32), gates[1][:, c, :],
                                                  start=c == 0 and r is r_hi, stop=c == KD - 1 and r is r_lo)
                mm.then_inc(gate_mm, 1)

        @block.scalar
        def _(act):
            act.sem_inc(taken, ring)
            with act.Fori(0, ntiles // ring) as i:
                for b in range(ring):
                    act.wait_ge(multiplied, i * ring + b + 3)
                    out = dst[:, bass.ds(i * 4 + b, 1), :].rearrange("p o (h t) -> p (o h) t", h=2)
                    nc.scalar.activation(out, k.pair(2 * b), ACT.Copy).then_inc(taken, 1)
            if gates is not None:
                act.wait_ge(gate_mm, 1)
                nc.scalar.activation(gates[2][:, 0:4, :].rearrange("p a n -> p (a n)"), k.ps[:, 0, 0:4 * NGATE],
                                     ACT.Sigmoid)
                nc.scalar.activation(gates[2][0:TS, 4, :], k.ps[0:TS, 0, 4 * NGATE:5 * NGATE], ACT.Sigmoid)


def rwkv_prepare_stage(k):
    nc = k.nc
    Z, r = k.z, k.r
    with ExitStack() as ctx:
        xs = r.xs
        last9 = k.sb(ctx, "last9", [P, RCOLS, 9])
        prev = k.sb(ctx, "prev", [P, RCOLS, DEC_BATCH])
        up = k.sb(ctx, "up", [P, 2, 512])
        keep = k.sb(ctx, "keep", [P, T])
        V = Steps(None, "last shifted_low shifted keys2 cum a_used normed prods bonus done")
        S = Steps(None, "low sw aa gg rooted decays")
        E = Steps(None, "w a g keysum bonussum")
        v_at, s_at, e_at, loaded, stored, chain, schain = k.sems(ctx, "dve_step", "act_step", "pe_step", "loaded",
                                                                "stored", "chain", "schain")
        sw, cum, tmp = Z[:, 0:4, :], Z[:, 4:8, :], Z[:, 8:12, :]
        kk = r.kt
        block = ctx.enter_context(nc.Block())

        @block.sync
        def _(sp):
            sp.dma_start(prev.rearrange("p c s -> p (c s)"), k.d["shift"]).then_inc(loaded, 16)
            sp.dma_start(up.rearrange("p c s -> p (c s)"), k.d["up"]).then_inc(loaded, 16)
            sp.dma_start(keep[:], k.d["keep"]).then_inc(loaded, 16)
            sp.wait_ge(v_at, V.at("last"))
            sp.dma_start(k.d["out_shift"], last9.rearrange("p c s -> p (c s)")).then_inc(stored, 16)
            sp.wait_ge(stored, 16)

        @block.vector
        def _(dve):
            ch = Chain(dve, chain)
            nc.vector.tensor_copy(last9[:], Z[:, 0:RCOLS, SEQ - 1:T:DEC_SEQ]).then_inc(v_at, 1)
            nc.vector.tensor_scalar(xs[:, :, 0:1], Z[:, 0:RCOLS, 0:1], -1.0, None, ALU.mult)
            ch.link(nc.vector.tensor_tensor(xs[:, :, 1:T], Z[:, 0:RCOLS, 0:T - 1], Z[:, 0:RCOLS, 1:T], ALU.subtract))
            dve.wait_ge(loaded, 48)
            ch.link(nc.vector.tensor_tensor(xs[:, :, SEQ:T:DEC_SEQ], prev[:], Z[:, 0:RCOLS, SEQ:T:DEC_SEQ], ALU.subtract))
            for n in (12, 13, *range(12)):
                ins = nc.vector.scalar_tensor_tensor(out=xs[:, n, :], in0=xs[:, n, :], scalar=k.par("mu", n),
                                                     in1=Z[:, n, :], op0=ALU.mult, op1=ALU.add)
                if n == 13:
                    ins.then_inc(v_at, 1)
            ins.then_inc(v_at, 1)
            dve.wait_ge(v_at, V.at("shifted"))
            for n in range(4):
                last = nc.vector.tensor_scalar(kk[:, n, :], xs[:, 4 + n, :], k.par("k_k", n), None, ALU.mult)
            ch.link(last)
            nc.vector.tensor_tensor(tmp, kk[:], kk[:], ALU.mult).then_inc(v_at, 1)
            dve.wait_ge(s_at, S.at("sw"))
            for n in range(4):
                last = nc.vector.tensor_tensor_scan(cum[:, n, :], keep[:], sw[:, n, :], 0.0, ALU.mult, ALU.add)
            ch.link(last)
            nc.vector.tensor_tensor(sw, cum, sw, ALU.subtract).then_inc(v_at, 1)
            dve.wait_ge(s_at, S.at("aa"))
            for n in range(4):
                last = nc.vector.tensor_scalar(r.bonus[:, n, :], r.bt[:, n, :], -1.0, k.par("k_a", n), ALU.add, ALU.mult)
            ch.link(last)
            nc.vector.scalar_tensor_tensor(out=r.ht, in0=r.bonus[:], scalar=1.0, in1=xs[:, 4:8, :],
                                           op0=ALU.add, op1=ALU.mult).then_inc(v_at, 1)
            dve.wait_ge(s_at, S.at("rooted"))
            ch.link(nc.vector.tensor_scalar(tmp, tmp, 1e-12, None, ALU.max))
            ch.link(nc.vector.reciprocal(tmp, tmp))
            ch.link(nc.vector.tensor_tensor(kk[:], kk[:], tmp, ALU.mult))
            nc.vector.tensor_tensor(r.bt[:], r.bt[:], kk[:], ALU.mult).then_inc(v_at, 1)
            dve.wait_ge(v_at, V.at("normed"))
            for n in range(4):
                last = nc.vector.scalar_tensor_tensor(out=tmp[:, n, :], in0=xs[:, n, :], scalar=k.par("r_k", n),
                                                      in1=r.ht[:, n, :], op0=ALU.mult, op1=ALU.mult)
            last.then_inc(v_at, 1)
            dve.wait_ge(e_at, E.at("bonussum"))
            for n in range(4):
                last = nc.vector.tensor_tensor(halves(r.bonus[:, n, :]), k.pair(2 * n), halves(xs[:, 8 + n, :]), ALU.mult)
            last.then_inc(v_at, 1)
            dve.wait_ge(s_at, S.at("decays"))
            nc.vector.tensor_copy(r.ends[:, :, 0:NCH], tmp[:, :, CH - 1:SEQ:CH])
            nc.vector.tensor_copy(r.ends[:, :, NCH:], tmp[:, :, SEQ + DEC_SEQ - 1:T:DEC_SEQ])
            nc.vector.tensor_tensor(r.rt, r.rt, tmp, ALU.mult)
            nc.vector.tensor_tensor(kk[:], kk[:], sw, ALU.mult)
            nc.vector.tensor_tensor(r.bt[:], r.bt[:], cum, ALU.mult)
            nc.vector.tensor_tensor(r.ht, r.ht, cum, ALU.mult).then_inc(v_at, 1)
            dve.wait_ge(v_at, V.at("done"))

        @block.scalar
        def _(act):
            act.wait_ge(v_at, V.at("shifted_low"))
            nc.scalar.activation(xs[0:64, 12, :], xs[0:64, 12, :], ACT.Tanh)
            nc.scalar.activation(xs[:, 13, :], xs[:, 13, :], ACT.Sigmoid).then_inc(s_at, 1)
            act.wait_ge(v_at, V.at("shifted"))
            for name, dst, bias in (("w", sw, "w0"), ("a", r.bt, "a0"), ("g", r.g, None)):
                act.wait_ge(e_at, E.at(name))
                for n in range(4):
                    if bias:
                        last = nc.scalar.activation(halves(dst[:, n, :]), k.pair(2 * n), ACT.Sigmoid, bias=k.par(bias, n))
                    else:
                        last = nc.scalar.activation(halves(dst[:, n, :]), k.pair(2 * n), ACT.Copy)
                last.then_inc(s_at, 1)
            act.wait_ge(e_at, E.at("keysum"))
            for n in range(4):
                last = nc.scalar.activation(halves(tmp[:, n, :]), k.pair(2 * n), ACT.Sqrt)
            last.then_inc(s_at, 1)
            act.wait_ge(e_at, E.at("bonussum"))
            nc.scalar.activation(tmp, cum, ACT.Exp, scale=-DECAY).then_inc(schain, 1)
            nc.scalar.activation(sw, sw, ACT.Exp, scale=-DECAY)
            act.wait_ge(schain, 1)
            nc.scalar.activation(cum, cum, ACT.Exp, scale=DECAY).then_inc(s_at, 1)

        @block.tensor
        def _(pe):
            pe.wait_ge(loaded, 48)
            pe.wait_ge(s_at, S.at("low"))
            for name, lhs, rhs in (("w", up[0:64, 0], xs[0:64, 12, :]), ("a", up[64:128, 0], xs[64:128, 12, :]),
                                   ("g", up[:, 1], xs[:, 13, :])):
                if name != "w":
                    pe.wait_ge(s_at, S.at({"a": "sw", "g": "aa"}[name]))
                for n in range(4):
                    for h in range(2):
                        mm = nc.tensor.matmul(k.bank(2 * n + h, TH), lhs[:, n * P:(n + 1) * P],
                                              rhs[:, h * TH:(h + 1) * TH], start=True, stop=True)
                mm.then_inc(e_at, 1)
            for name, ready, freed in (("keysum", "keys2", "gg"), ("bonussum", "prods", "rooted")):
                pe.wait_ge(v_at, V.at(ready))
                pe.wait_ge(s_at, S.at(freed))
                for n in range(4):
                    for h in range(2):
                        mm = nc.tensor.matmul(k.bank(2 * n + h, TH), k.blocks[:], tmp[:, n, h * TH:(h + 1) * TH],
                                              start=True, stop=True)
                mm.then_inc(e_at, 1)


def chunk_round(k, c, t0, i, eng, which, sample):
    nc = k.nc
    V, S, E = c.V, c.S, c.E
    hs = range(HEADS)
    bank = lambda b: k.ps[0:CH, b, :].rearrange("p (h t) -> p h t", h=HEADS)
    mask = lambda m: c.masks[:, 6 * sample + m:6 * sample + m + 1, :].broadcast_to([CH, HEADS, CH])

    def product(b, lhs, rhs, start=True, stop=True):
        for h in hs:
            mm = nc.tensor.matmul(bank(b)[:, h, :], lhs[:, h, :], rhs[:, h, :], start=start, stop=stop)
        return mm

    def products(b, *pairs):
        for h in hs:
            for n, (lhs, rhs) in enumerate(pairs):
                rhs_h = rhs[:, h, :] if rhs is not k.ident else k.ident[0:CH, 0:CH]
                lhs_h = lhs[:, h, :] if lhs is not k.ident else k.ident[0:CH, 0:CH]
                mm = nc.tensor.matmul(bank(b)[:, h, :], lhs_h, rhs_h, start=n == 0, stop=n == len(pairs) - 1)
        return mm

    sources = ((c.r0, k.r.rt), (c.k0, k.r.kt), (c.b0, k.r.bt), (c.h0, k.r.ht), (c.v0, k.r.vt))
    def wait(steps, value):
        eng.wait_ge(steps.sem, value)
        if which == "tensor":
            eng.sem_inc(c.passed, 1)

    v = lambda name: wait(V, V.at(name, i))
    s = lambda name: wait(S, S.at(name, i))
    e = lambda name: wait(E, E.at(name, i))

    if which == "tensor":
        v("even")
        s("odd")
        product(0, c.k0, c.b0)
        product(1, c.b0, c.k0)
        product(2, c.h0, c.k0)
        product(3, c.h0, c.r0)
        product(4, c.b0, c.r0).then_inc(E.sem, 1)
        for b, src in ((5, c.v0), (6, c.h0), (7, c.b0)):
            for h in hs:
                mm = nc.tensor.transpose(bank(b)[:, h, :], src[:, h, :], k.ident[0:CH, 0:CH])
        mm.then_inc(E.sem, 1)
        v("masked")
        product(0, c.nt, c.n)
        product(1, c.n, c.nt).then_inc(E.sem, 1)
        for j in range(1, 4):
            v(f"square{j}")
            s(f"square{j}")
            n, nt = (c.n2, c.n2t) if j % 2 else (c.n, c.nt)
            product(2, nt, c.t)
            mm = product(3, n, c.tt)
            if j < 3:
                product(0, nt, n)
                mm = product(1, n, nt)
            mm.then_inc(E.sem, 1)
        v("inverse")
        product(0, c.below, c.tt)
        product(1, c.tt, c.below).then_inc(E.sem, 1)
        v("q")
        s("q")
        product(2, c.qt, c.q)
        product(3, c.t, c.q)
        product(4, c.q, c.t).then_inc(E.sem, 1)
        v("r")
        s("q2")
        product(5, c.rt, c.q2).then_inc(E.sem, 1)
        s("turned")
        if sample:
            for h in hs:
                for n in range(DEC_BATCH):
                    cols = slice(n * DEC_SEQ, (n + 1) * DEC_SEQ)
                    mm = nc.tensor.matmul(bank(6)[:, h, cols], c.states[:, h, n, :], c.k0[:, h, cols],
                                          start=True, stop=True)
            mm.then_inc(E.sem, 1)
            s("seen")
            products(7, (c.seen, k.ident), (c.ak, c.v1)).then_inc(E.sem, 1)
        else:
            wait(V, V.before(i))
            products(7, (c.k0, c.state), (c.ak, c.v1)).then_inc(E.sem, 1)
        v("inverse_done")
        s("x")
        product(6, c.ti, c.x).then_inc(E.sem, 1)
        v("u")
        if sample:
            for h in hs:
                nc.tensor.matmul(bank(0)[:, h, :], c.v1[:, h, :], c.rk[:, h, :], start=True, stop=False)
                for n in range(DEC_BATCH):
                    cols = slice(n * DEC_SEQ, (n + 1) * DEC_SEQ)
                    nc.tensor.matmul(bank(0)[:, h, cols], c.states[:, h, n, :], c.r0[:, h, cols],
                                     start=False, stop=False)
                mm = nc.tensor.matmul(bank(0)[:, h, :], c.u[:, h, :], c.rb[:, h, :], start=False, stop=True)
            mm.then_inc(E.sem, 1)
            for h in hs:
                eng.wait_ge(c.spread, h + 1)
                b = 1 + h % 2
                if h >= 2:
                    eng.wait_ge(c.taken, h - 1)
                nc.tensor.matmul(k.ps[0:CH, b, :], k.ident[0:CH, 0:CH],
                                 c.states[:, h].rearrange("p n v -> p (n v)"), start=True, stop=False)
                nc.tensor.matmul(k.ps[0:CH, b, :], c.h1[:, h, :], c.vm[:, h % 2].rearrange("p n v -> p (n v)"),
                                 start=False, stop=False)
                nc.tensor.matmul(k.ps[0:CH, b, :], c.b1[:, h, :], c.um[:, h % 2].rearrange("p n v -> p (n v)"),
                                 start=False, stop=True).then_inc(c.updated, 1)
        else:
            products(0, (c.state, c.r0), (c.v1, c.rk), (c.u, c.rb)).then_inc(E.sem, 1)
            products(1, (k.ident, c.state), (c.h1, c.v1), (c.b1, c.u)).then_inc(E.sem, 1)

    if which == "vector":
        for dst, src in sources:
            last = nc.vector.tensor_copy(dst[:, 0::2, :], src[0:CH, :, bass.ds(t0, CH)])
        last.then_inc(V.sem, 1)
        ch = Chain(eng, c.chain, i * c.links)
        e("grams")
        ch.link(nc.vector.tensor_tensor(c.n[:], bank(0), mask(0), ALU.mult))
        ch.link(nc.vector.tensor_tensor(c.nt[:], bank(1), mask(1), ALU.mult))
        nc.vector.tensor_tensor(c.below[:], bank(0), mask(2), ALU.mult).then_inc(V.sem, 1)
        nc.vector.tensor_tensor(c.ak[:], bank(2), mask(3), ALU.mult)
        nc.vector.tensor_tensor(c.rk[:], bank(3), mask(4), ALU.mult)
        nc.vector.tensor_tensor(c.rb[:], bank(4), mask(5), ALU.mult)
        ident = k.ident[0:CH, 0:CH].rearrange("p (o t) -> p o t", o=1).broadcast_to([CH, HEADS, CH])
        nc.vector.tensor_tensor(c.t[:], c.n[:], ident, ALU.add)
        ch.link(nc.vector.tensor_tensor(c.tt[:], c.nt[:], ident, ALU.add))
        for j in range(1, 4):
            e(("square1", "prods1", "prods2")[j - 1])
            nc.vector.tensor_copy((c.n2 if j % 2 else c.n)[:], bank(0)).then_inc(V.sem, 1)
            e(f"prods{j}")
            ch.link(nc.vector.tensor_tensor(c.t[:], bank(2), c.t[:], ALU.add))
            ins = nc.vector.tensor_tensor(c.tt[:], bank(3), c.tt[:], ALU.add)
            if j < 3:
                ch.link(ins)
            else:
                ins.then_inc(V.sem, 1)
        e("q")
        nc.vector.tensor_copy(c.q[:], bank(0)).then_inc(V.sem, 1)
        e("q2")
        ch.link(nc.vector.tensor_tensor(c.rr[:], bank(3), c.tt[:], ALU.add))
        nc.vector.tensor_tensor(c.rt[:], bank(4), c.t[:], ALU.add).then_inc(V.sem, 1)
        e("inverse")
        nc.vector.tensor_tensor(c.ti[:], bank(5), c.rr[:], ALU.add).then_inc(V.sem, 1)
        e("u")
        nc.vector.tensor_copy(c.u[:], bank(6)).then_inc(V.sem, 1)
        if sample:
            eng.wait_ge(V.sem, V.at("u", i))
            m = c.seqmask.rearrange("p (n o) -> p n o", o=1).broadcast_to([CH, DEC_BATCH, HD])
            for h in hs:
                if h >= 2:
                    eng.wait_ge(c.updated, h - 1)
                rep = lambda x: x[:, h:h + 1, :].broadcast_to([CH, DEC_BATCH, HD])
                nc.vector.tensor_tensor(c.vm[:, h % 2], rep(c.v1), m, ALU.mult)
                nc.vector.tensor_tensor(c.um[:, h % 2], rep(c.u), m, ALU.mult).then_inc(c.spread, 1)
                if h >= 1:
                    take_state(k, c, eng, h - 1)
            take_state(k, c, eng, HEADS - 1)
        else:
            e("state")
            dc = c.dc.rearrange("p (h o) -> p h o", o=1).broadcast_to([CH, HEADS, HD])
            nc.vector.tensor_tensor(c.state[:], bank(1), dc, ALU.mult).then_inc(V.sem, 1)
        assert ch.n == c.links, ch.n

    if which == "scalar":
        if not sample:
            eng.wait_ge(V.sem, V.before(i))
        for dst, src in sources:
            last = nc.scalar.activation(dst[:, 1::2, :], src[CH:P, :, bass.ds(t0, CH)], ACT.Copy)
        if not sample:
            for half in range(2):
                last = nc.scalar.activation(c.dc.rearrange("p (h a) -> p h a", a=2)[:, :, half:half + 1],
                                            k.r.ends[half * CH:half * CH + CH, :, bass.ds(i, 1)], ACT.Copy)
        last.then_inc(S.sem, 1)
        e("turned")
        nc.scalar.activation(c.v1[:], bank(5), ACT.Copy)
        nc.scalar.activation(c.h1[:], bank(6), ACT.Copy)
        nc.scalar.activation(c.b1[:], bank(7), ACT.Copy, scale=-1.0).then_inc(S.sem, 1)
        for j in range(1, 4):
            e(("square1", "prods1", "prods2")[j - 1])
            nc.scalar.activation((c.n2t if j % 2 else c.nt)[:], bank(1), ACT.Copy).then_inc(S.sem, 1)
        e("q")
        nc.scalar.activation(c.qt[:], bank(1), ACT.Copy).then_inc(S.sem, 1)
        e("q2")
        nc.scalar.activation(c.q2[:], bank(2), ACT.Copy).then_inc(S.sem, 1)
        if sample:
            e("seen")
            nc.scalar.activation(c.seen[:], bank(6), ACT.Copy).then_inc(S.sem, 1)
        e("x")
        nc.scalar.activation(c.x[:], bank(7), ACT.Copy).then_inc(S.sem, 1)
        e("out")
        for half in range(2):
            last = nc.scalar.activation(k.r.o[half * CH:half * CH + CH, :, bass.ds(t0, CH)], bank(0)[:, half::2, :], ACT.Copy)
        last.then_inc(S.sem, 1)


def take_state(k, c, eng, h):
    eng.wait_ge(c.updated, h + 1)
    ps = k.ps[0:CH, 1 + h % 2, :].rearrange("p (n v) -> p n v", n=DEC_BATCH)
    dc = c.dcs[:, h, :].rearrange("p (n o) -> p n o", o=1).broadcast_to([CH, DEC_BATCH, HD])
    k.nc.vector.tensor_tensor(c.states[:, h], ps, dc, ALU.mult).then_inc(c.taken, 1)


def rwkv_chunks_stage(k, sample):
    nc = k.nc
    with ExitStack() as ctx:
        spare = k.z[0:CH, 0:4, :].rearrange("p a t -> p (a t)")
        names = "r0 k0 b0 h0 v0 n nt n2 n2t t tt below ak rk rb v1 h1 b1 q qt q2 rr rt" + ("" if sample else " state")
        tiles = [k.sb(ctx, name, [CH, HEADS, CH])[:] if m >= 4 else
                 spare[:, m * 512:(m + 1) * 512].rearrange("p (h t) -> p h t", h=HEADS)
                 for m, name in enumerate(names.split())]
        c = Tiles()
        (c.r0, c.k0, c.b0, c.h0, c.v0, c.n, c.nt, c.n2, c.n2t, c.t, c.tt, c.below, c.ak, c.rk, c.rb, c.v1, c.h1, c.b1,
         c.q, c.qt, c.q2, c.rr, c.rt) = tiles[:23]
        if not sample:
            c.state = tiles[23]
        c.x, c.u, c.seen, c.ti = c.n, c.nt, c.n2, c.n2t
        c.masks = k.sb(ctx, "masks", [CH, 12, CH])
        c.dc = k.sb(ctx, "dc", [CH, HEADS])
        c.links = 9
        v_at, s_at, e_at, c.chain, loaded, stored, c.passed = k.sems(ctx, "dve_step", "act_step", "pe_step", "chain",
                                                                     "loaded", "stored", "passed")
        c.V = Steps(v_at, "even masked square1 square2 square3 inverse q r inverse_done u" + ("" if sample else " ready"),
                    base=1)
        c.S = Steps(s_at, "odd turned square1 square2 square3 q q2 " + ("seen " if sample else "") + "x out")
        c.E = Steps(e_at, "grams turned square1 prods1 prods2 prods3 q q2 inverse " + ("seen " if sample else "")
                    + "x u out" + ("" if sample else " state"))
        if sample:
            c.states = k.sb(ctx, "states", [CH, HEADS, DEC_BATCH, HD])
            more = k.z[0:CH, 8:12, :].rearrange("p a t -> p (a t)")
            c.vm, c.um = (more[:, m * 1024:(m + 1) * 1024].rearrange("p (b n v) -> p b n v", b=2, v=HD) for m in range(2))
            c.seqmask = k.sb(ctx, "seqmask", [CH, DEC_BATCH])
            c.dcs = k.sb(ctx, "dcs", [CH, HEADS, DEC_BATCH])
            c.spread, c.updated, c.taken = k.sems(ctx, "spread", "updated", "taken")
        n_loads = 3 if sample else 1
        block = ctx.enter_context(nc.Block())

        def rounds(eng, which):
            if sample:
                chunk_round(k, c, SEQ, 0, eng, which, 1)
            else:
                with eng.Fori(0, NCH) as i:
                    chunk_round(k, c, i * CH, i, eng, which, 0)

        @block.sync
        def _(sp):
            sp.dma_start(c.masks.rearrange("p m t -> p (m t)"), k.d["masks"]).then_inc(loaded, 16)
            if sample:
                sp.dma_start(c.states.rearrange("p h n v -> p (h n v)"), k.d["states"]).then_inc(loaded, 16)
                sp.dma_start(c.seqmask[:], k.d["seqmask"]).then_inc(loaded, 16)
                sp.wait_ge(c.taken, HEADS)
                sp.dma_start(k.d["out_states"], c.states.rearrange("p h n v -> p (h n v)")).then_inc(stored, 16)
            else:
                sp.wait_ge(v_at, c.V.before(NCH))
                sp.dma_start(k.d["out_state"], c.state.rearrange("p h v -> p (h v)")).then_inc(stored, 16)
            sp.wait_ge(stored, 16)

        @block.tensor
        def _(pe):
            pe.wait_ge(loaded, 16 * n_loads)
            rounds(pe, "tensor")

        @block.vector
        def _(dve):
            if sample:
                for half in range(2):
                    last = nc.vector.tensor_copy(
                        c.dcs.rearrange("p (h a) n -> p h a n", a=2)[:, :, half, :],
                        k.r.ends[half * CH:half * CH + CH, :, NCH:])
                last.then_inc(v_at, 1)
            else:
                nc.vector.memset(c.state[:], 0.0).then_inc(v_at, 1)
            dve.wait_ge(loaded, 16 * n_loads)
            dve.wait_ge(v_at, 1)
            rounds(dve, "vector")

        @block.scalar
        def _(act):
            rounds(act, "scalar")


def rwkv_finish_stage(k):
    nc = k.nc
    o, r = k.r.o, k.r
    with ExitStack() as ctx:
        sq = k.sb(ctx, "sq", [P, 4, T])
        V = Steps(None, "centred mean")
        v_at, squared, rooted, summed, chain = k.sems(ctx, "dve_step", "squared", "rooted", "summed", "chain")
        block = ctx.enter_context(nc.Block())

        @block.tensor
        def _(pe):
            for src, ready in ((o, None), (sq, squared)):
                if ready is not None:
                    pe.wait_ge(ready, 1)
                for n in range(4):
                    for h in range(2):
                        mm = nc.tensor.matmul(k.bank(2 * n + h, TH), k.blocks[:], src[:, n, h * TH:(h + 1) * TH],
                                              start=True, stop=True)
                mm.then_inc(summed, 1)

        @block.vector
        def _(dve):
            ch = Chain(dve, chain)
            dve.wait_ge(summed, 1)
            for n in range(4):
                last = nc.vector.scalar_tensor_tensor(out=halves(o[:, n, :]), in0=k.pair(2 * n), scalar=-1.0 / HD,
                                                      in1=halves(o[:, n, :]), op0=ALU.mult, op1=ALU.add)
            last.then_inc(v_at, 1)
            dve.wait_ge(summed, 2)
            for n in range(4):
                last = nc.vector.tensor_scalar(halves(sq[:, n, :]), k.pair(2 * n), 1.0 / HD, GN_EPS, ALU.mult, ALU.add)
            last.then_inc(v_at, 1)
            dve.wait_ge(rooted, 1)
            ch.link(nc.vector.reciprocal(sq[:], sq[:]))
            ch.link(nc.vector.tensor_tensor(o[:], o[:], sq[:], ALU.mult))
            for n in range(4):
                last = nc.vector.tensor_scalar(o[:, n, :], o[:, n, :], k.par("gn_w", n), k.par("gn_b", n),
                                               ALU.mult, ALU.add)
            ch.link(last)
            ch.link(nc.vector.tensor_tensor(o[:], o[:], r.bonus[:], ALU.add))
            ch.link(nc.vector.tensor_tensor(o[:], o[:], r.g[:], ALU.mult))

        @block.scalar
        def _(act):
            act.wait_ge(v_at, V.at("centred"))
            nc.scalar.activation(sq[:], o[:], ACT.Square).then_inc(squared, 1)
            act.wait_ge(v_at, V.at("mean"))
            nc.scalar.activation(sq[:], sq[:], ACT.Sqrt).then_inc(rooted, 1)


def nsa_prepare_stage(k):
    nc = k.nc
    Z = k.z
    groups = [([ZQ, ZQ + 1, ZQ + 2, ZQ + 3], ["q_norm"] * 4, [0] * 4), ([ZK + 2, ZK + 4], ["k_norm"] * 2, [1, 2])]
    with ExitStack() as ctx:
        sq = k.sb(ctx, "sq", [P, 4, T])
        tab = k.sb(ctx, "rope", [P, 2, T])
        rot = k.sb(ctx, "rot", [P, P])
        V = Steps(None, "mean normed roped")
        E = Steps(None, "summed turned")
        v_at, e_at, squared, rooted, vt_ready, vt_out, loaded, stored, chain = k.sems(
            ctx, "dve_step", "pe_step", "squared", "rooted", "vt_ready", "vt_out", "loaded", "stored", "chain")
        block = ctx.enter_context(nc.Block())

        @block.sync
        def _(sp):
            sp.dma_start(tab.rearrange("p m t -> p (m t)"), k.d["rope"]).then_inc(loaded, 16)
            sp.dma_start(rot[:], k.d["rot"]).then_inc(loaded, 16)
            sp.dma_start(k.d["out_win"], k.d["win_rows"]).then_inc(stored, 16)
            sp.wait_ge(v_at, V.at("roped", 1))
            sp.dma_start(k.d["out_kv"], Z[:, ZK:NZ, :].rearrange("p c t -> p (c t)")).then_inc(stored, 16)
            sp.wait_ge(stored, 32)

        @block.scalar
        def _(act):
            for g, (tiles, _, _) in enumerate(groups):
                if g:
                    act.wait_ge(v_at, V.at("roped", g - 1))
                for n, z in enumerate(tiles):
                    last = nc.scalar.activation(sq[:, n, :], Z[:, z, :], ACT.Square)
                last.then_inc(squared, 1)
                act.wait_ge(v_at, V.at("mean", g))
                nc.scalar.activation(sq[:, 0:len(tiles), :], sq[:, 0:len(tiles), :], ACT.Sqrt).then_inc(rooted, 1)

        @block.tensor
        def _(pe):
            pe.wait_ge(loaded, 32)
            for g, (tiles, _, _) in enumerate(groups):
                pe.wait_ge(squared, g + 1)
                for n in range(len(tiles)):
                    for h in range(2):
                        mm = nc.tensor.matmul(k.bank(2 * n + h, TH), k.blocks[:], sq[:, n, h * TH:(h + 1) * TH],
                                              start=True, stop=True)
                mm.then_inc(e_at, 1)
                pe.wait_ge(v_at, V.at("normed", g))
                for n, z in enumerate(tiles):
                    for h in range(2):
                        mm = nc.tensor.matmul(k.bank(2 * n + h, TH), rot[:], Z[:, z, h * TH:(h + 1) * TH],
                                              start=True, stop=True)
                mm.then_inc(e_at, 1)
            for b, z in enumerate((ZK + 3, ZK + 5)):
                for tt in range(5):
                    n = min(P, T - tt * P)
                    mm = nc.tensor.transpose(k.ps[0:n, 4 + 2 * b + tt // 4, (tt % 4) * P:(tt % 4) * P + P],
                                             Z[:, z, tt * P:tt * P + n], k.ident[:])
            mm.then_inc(vt_ready, 1)

        @block.vector
        def _(dve):
            ch = Chain(dve, chain)
            dve.wait_ge(loaded, 32)
            for g, (tiles, gains, which) in enumerate(groups):
                m = len(tiles)
                dve.wait_ge(e_at, E.at("summed", g))
                for n in range(m):
                    last = nc.vector.tensor_scalar(halves(sq[:, n, :]), k.pair(2 * n), 1.0 / HD, EPS, ALU.mult, ALU.add)
                last.then_inc(v_at, 1)
                dve.wait_ge(rooted, g + 1)
                ch.link(nc.vector.reciprocal(sq[:, 0:m, :], sq[:, 0:m, :]))
                for n, z in enumerate(tiles):
                    last = nc.vector.scalar_tensor_tensor(out=Z[:, z, :], in0=Z[:, z, :], scalar=k.par(gains[n], which[n]),
                                                          in1=sq[:, n, :], op0=ALU.mult, op1=ALU.mult)
                last.then_inc(v_at, 1)
                dve.wait_ge(e_at, E.at("turned", g))
                for n in range(m):
                    last = nc.vector.tensor_tensor(halves(sq[:, n, :]), k.pair(2 * n), halves(tab[:, 1, :]), ALU.mult)
                dst = [k.qr[:, n, :] if g == 0 else Z[:, z, :] for n, z in enumerate(tiles)]
                for n, z in enumerate(tiles):
                    last = nc.vector.tensor_tensor(dst[n], Z[:, z, :], tab[:, 0, :], ALU.mult)
                ch.link(last)
                for n in range(m):
                    last = nc.vector.tensor_tensor(dst[n], dst[n], sq[:, n, :], ALU.add)
                last.then_inc(v_at, 1)
            dve.wait_ge(vt_ready, 1)
            for b, dst in enumerate((k.vs, k.vw)):
                nc.vector.tensor_copy(dst[:, 0:4, :].rearrange("p a c -> p (a c)"), k.bank(4 + 2 * b))
                last = nc.vector.tensor_copy(dst[0:TS, 4, :], k.ps[0:TS, 5 + 2 * b, 0:P])
            ch.link(last)


def compress_stage(k):
    nc = k.nc
    Z = k.z
    jobs = [("cache", 4, CH), ("cache", 4, CH), ("prompt", 1, 32)]
    with ExitStack() as ctx:
        w1 = k.sb(ctx, "w1", [P, 8, 2, 2, CMP_HIDDEN])
        w2 = k.sb(ctx, "w2", [P, 2, 2, HD])
        pos = k.sb(ctx, "pos", [P, 8, 2, 2])
        pages = k.sb(ctx, "pages", [P, 4 * PAGES, 8, 2, 2, 8])
        xp = k.sb(ctx, "xp", [P, 8, 2, 2, 32])
        bias = k.sb(ctx, "bias", [P, 4])
        second = k.sb(ctx, "second", [P, 512])
        hid = k.sb(ctx, "hid", [P, 2, 2, 512])
        sq = k.sb(ctx, "sq", [P, 256])
        rs = k.sb(ctx, "rs", [P, 256])
        weights, table, landed, parted, biased, bias_out, moved, summed, gelued, heads, squared, mean, rooted, out, chain, sums, kept \
            = k.sems(ctx, "weights", "table", "landed", "parted", "biased", "bias_out", "moved", "summed", "gelued",
                     "heads", "squared", "mean", "rooted", "out", "chain", "sums", "kept")
        block = ctx.enter_context(nc.Block())

        @block.sync
        def _(sp):
            sp.dma_start(k.table[:], k.d["page_table"]).then_inc(table, 16)
            sp.dma_start(w1.rearrange("p j e r f -> p (j e r f)"), k.d["cmp_w1"]).then_inc(weights, 16)
            sp.dma_start(w2.rearrange("p e h d -> p (e h d)"), k.d["cmp_w2"]).then_inc(weights, 16)
            sp.dma_start(pos.rearrange("p j e r -> p (j e r)"), k.d["cmp_pe"]).then_inc(weights, 16)
            sp.wait_ge(table, 16)
            for n in range(2):
                if n:
                    sp.wait_ge(parted, 4 * n)
                with sp.Fori(0, 4 * PAGES) as i:
                    page = sp.value_load(k.table[0:1, bass.ds(n * 4 * PAGES + i, 1)], min_val=0, max_val=k.n_phys - 1)
                    sp.dma_start(pages[:, bass.ds(i, 1)].rearrange("p o j e k c -> p (o j e k c)"),
                                 k.d["cmp_pages"][bass.ds(page, 1)].rearrange("o p n -> (o p) n")).then_inc(landed, 16)

        @block.tensor
        def _(pe):
            pe.wait_ge(weights, 48)
            for e in range(2):
                for f in range(2):
                    for j in range(8):
                        for r in range(2):
                            mm = nc.tensor.matmul(k.ps[:, 0, 2 * e + f:2 * e + f + 1], w1[:, j, e, r, f * P:(f + 1) * P],
                                                  pos[:, j, e, r:r + 1], start=j == 0 and r == 0, stop=j == 7 and r == 1)
            mm.then_inc(biased, 1)
            pe.wait_ge(bias_out, 1)
            for n, (kind, ns, cols) in enumerate(jobs):
                w = ns * 2 * cols
                if kind == "cache":
                    pe.wait_ge(landed, 16 * 4 * PAGES * (n + 1))
                else:
                    pe.wait_ge(moved, 1)
                for e in range(2):
                    for f in range(2):
                        b = 2 * (2 * e + f)
                        if n:
                            pe.wait_ge(out, 2 * n)
                        for r in range(2):
                            for j in range(8):
                                if kind == "cache":
                                    rhs = pages[:, :, j, e]
                                    dst = k.bank(b + r).rearrange("p (k s c) -> p s k c", k=2, c=8)
                                else:
                                    rhs = xp[:, j, e].rearrange("p k c -> p (k c)")
                                    dst = k.bank(b + r, w)
                                mm = nc.tensor.matmul(dst, w1[:, j, e, r, f * P:(f + 1) * P], rhs,
                                                      start=j == 0, stop=j == 7)
                        mm.then_inc(parted, 1)
                pe.wait_ge(gelued, 4 * (n + 1))
                half = w // 2
                for kv in range(2):
                    for f in range(2):
                        mm = nc.tensor.matmul(k.ps[kv * HD:kv * HD + HD, 0, 0:half], w2[:, 0, f, :],
                                              hid[:, 0, f, kv * half:(kv + 1) * half], start=f == 0, stop=f == 1)
                for s in range(ns):
                    for kv in range(2):
                        for f in range(2):
                            at = kv * half + s * cols
                            mm = nc.tensor.matmul(k.ps[0:cols, 1, s * P + kv * HD:s * P + kv * HD + HD],
                                                  hid[:, 1, f, at:at + cols], w2[:, 1, f, :], start=f == 0, stop=f == 1)
                mm.then_inc(heads, 1)
                pe.wait_ge(squared, n + 1)
                nc.tensor.matmul(k.bank(2, half), k.blocks[:], sq[:, 0:half], start=True, stop=True).then_inc(sums, 1)

        @block.scalar
        def _(act):
            for e in range(2):
                for kv in range(2):
                    for odd in range(2):
                        last = nc.scalar.activation(
                            xp[odd * HD:odd * HD + HD, :, e, kv, :].rearrange("p j c -> p c j"),
                            Z[kv * HD:kv * HD + HD, ZK + e, odd:SEQ:2].rearrange("p (c j) -> p c j", j=8), ACT.Copy)
            last.then_inc(moved, 1)
            act.wait_ge(bias_out, 1)
            for n, (kind, ns, cols) in enumerate(jobs):
                w = ns * 2 * cols
                for m in range(4):
                    act.wait_ge(parted, 4 * n + m + 1)
                    if 4 * n + m:
                        act.wait_ge(summed, 4 * n + m)
                    nc.scalar.activation(second[:, 0:w], k.bank(2 * m + 1, w), ACT.Identity,
                                         bias=bias[:, m:m + 1]).then_inc(kept, 1)
                    act.wait_ge(summed, 4 * n + m + 1)
                    nc.scalar.activation(hid[:, m // 2, m % 2, 0:w], hid[:, m // 2, m % 2, 0:w],
                                         ACT.Gelu_apprx_tanh).then_inc(gelued, 1)
                act.wait_ge(heads, n + 1)
                nc.scalar.activation(sq[:, 0:w // 2], k.bank(0, w // 2), ACT.Square).then_inc(squared, 1)
                act.wait_ge(mean, n + 1)
                nc.scalar.activation(rs[:, 0:w // 2], rs[:, 0:w // 2], ACT.Sqrt).then_inc(rooted, 1)

        @block.vector
        def _(dve):
            ch = Chain(dve, chain)
            dve.wait_ge(biased, 1)
            nc.vector.tensor_copy(bias[:], k.ps[:, 0, 0:4]).then_inc(bias_out, 1)
            for n, (kind, ns, cols) in enumerate(jobs):
                w = ns * 2 * cols
                for m in range(4):
                    if n and m == 0:
                        dve.wait_ge(heads, n)
                    dst = hid[:, m // 2, m % 2, 0:w].rearrange("p (s c) -> p s c", c=cols)
                    nc.vector.memset(dst[:, :, cols - 1:cols], 0.0)
                    dve.wait_ge(kept, 4 * n + m + 1)
                    nc.vector.tensor_tensor(
                        dst[:, :, 0:cols - 1], k.bank(2 * m, w).rearrange("p (s c) -> p s c", c=cols)[:, :, 0:cols - 1],
                        second[:, 0:w].rearrange("p (s c) -> p s c", c=cols)[:, :, 1:cols], ALU.add).then_inc(summed, 1)
                half = w // 2
                dve.wait_ge(heads, n + 1)
                if kind == "cache":
                    dst = k.vc[:, 4 * n:4 * n + 4, :].rearrange("p s d -> p (s d)")
                    nc.vector.tensor_copy(dst, k.ps[0:cols, 1, 0:ns * P]).then_inc(out, 1)
                else:
                    nc.vector.tensor_copy(k.vcp[:], k.ps[0:cols, 1, 0:P]).then_inc(out, 1)
                dve.wait_ge(sums, n + 1)
                nc.vector.tensor_scalar(rs[:, 0:half], k.bank(2, half), 1.0 / HD, EPS, ALU.mult, ALU.add).then_inc(mean, 1)
                dve.wait_ge(rooted, n + 1)
                ch.link(nc.vector.reciprocal(rs[:, 0:half], rs[:, 0:half]))
                dst = k.kc[:, 4 * n:4 * n + 4, :].rearrange("p s c -> p (s c)") if kind == "cache" else k.kcp[:]
                nc.vector.scalar_tensor_tensor(out=dst, in0=k.bank(0, half), scalar=k.par("k_norm", 0),
                                               in1=rs[:, 0:half], op0=ALU.mult, op1=ALU.mult).then_inc(out, 1)


def prompt_attention_stage(k):
    nc = k.nc
    Z = k.z
    units = [(qt, kv, i) for qt in range(SEQ // P) for kv in range(2) for i in range(4)]
    n_units = len(units)
    chunks = [2 * (qt + 1) + 1 for qt, _, _ in units]
    pieces = [-(-c // 4) for c in chunks]
    before = [sum(pieces[:u]) for u in range(n_units + 1)]
    CMP = 32
    with ExitStack() as ctx:
        E = k.sb(ctx, "probs", [P, 2, 2 * SEQ + CMP])
        PT = k.sb(ctx, "probs_t", [P, 2, 12, P])
        tri = k.sb(ctx, "tri", [P, P])
        cmask = k.sb(ctx, "cmask", [P, 4, CMP])
        cs = k.sb(ctx, "cmp_scores", [P, 8, CMP])
        mx = k.sb(ctx, "mx", [P, 2, 3])
        nm = k.sb(ctx, "nm", [P, 2, 3])
        sums = k.sb(ctx, "sums", [P, 2, 3])
        wts = k.sb(ctx, "wts", [P, 2, 3])
        loaded, scored, cmp_half, cmp_scored, cmp_masked, maxed, exped, weighted, turned, laid, mixed, out, chain = k.sems(
            ctx, "loaded", "scored", "cmp_half", "cmp_scored", "cmp_masked", "maxed", "exped", "weighted", "turned", "laid", "mixed",
            "out", "chain")

        def scores(u):
            qt = units[u][0]
            nk = (qt + 1) * P
            return k.bank(2 * (u % 2), nk), k.bank(2 * (u % 2) + 1, nk), cs[:, u % 8, :]

        def probs(u):
            nk = (units[u][0] + 1) * P
            return E[:, u % 2, 0:nk], E[:, u % 2, nk:2 * nk], E[:, u % 2, 2 * nk:2 * nk + CMP]

        block = ctx.enter_context(nc.Block())

        @block.sync
        def _(sp):
            sp.dma_start(tri[:], k.d["tri"]).then_inc(loaded, 16)
            sp.dma_start(cmask.rearrange("p a n -> p (a n)"), k.d["cmask"]).then_inc(loaded, 16)

        @block.tensor
        def _(pe):
            for step in range(n_units + 2):
                if step < n_units:
                    u = step
                    qt, kv, i = units[u]
                    half = slice(kv * HD, kv * HD + HD)
                    q = slice(qt * P, qt * P + P)
                    nk = (qt + 1) * P
                    if u % 8 == 0:
                        if qt:
                            pe.wait_ge(cmp_masked, qt)
                        for m in range(8):
                            mh = slice(m // 4 * HD, m // 4 * HD + HD)
                            mm = nc.tensor.matmul(k.ps[:, 4, m * CMP:(m + 1) * CMP], Z[mh, ZQ + m % 4, q], k.kcp[mh, :],
                                                  start=True, stop=True)
                            if m == 3:
                                mm.then_inc(cmp_half, 1)
                                pe.wait_ge(cmp_half, qt + 1)
                        mm.then_inc(cmp_scored, 1)
                    if u >= 2:
                        pe.wait_ge(exped, u - 1)
                    sel, win, _ = scores(u)
                    nc.tensor.matmul(sel, k.qr[half, i, q], Z[half, ZK + 2, 0:nk], start=True, stop=True)
                    nc.tensor.matmul(win, k.qr[half, i, q], Z[half, ZK + 4, 0:nk], start=True, stop=True).then_inc(scored, 1)
                if 1 <= step <= n_units:
                    u = step - 1
                    pe.wait_ge(weighted, u + 1)
                    for n in range(pieces[u]):
                        at = before[u] + n
                        if at >= 2:
                            pe.wait_ge(laid, at - 1)
                        for c in range(4 * n, min(4 * n + 4, chunks[u])):
                            w = P if c < chunks[u] - 1 else CMP
                            mm = nc.tensor.transpose(k.ps[0:w, 6 + at % 2, (c % 4) * P:(c % 4) * P + P],
                                                     E[:, u % 2, c * P:c * P + w], k.ident[:])
                        mm.then_inc(turned, 1)
                if step >= 2:
                    u = step - 2
                    qt, kv, i = units[u]
                    pe.wait_ge(laid, before[u + 1])
                    if u >= 1:
                        pe.wait_ge(out, u)
                    for c in range(chunks[u]):
                        if c == chunks[u] - 1:
                            lhs, rhs = k.vcp[:], PT[0:CMP, u % 2, c, :]
                        else:
                            v = k.vs if c <= qt else k.vw
                            lhs, rhs = v[:, c % (qt + 1), :], PT[:, u % 2, c, :]
                        mm = nc.tensor.matmul(k.bank(5, P), lhs, rhs, start=c == 0, stop=c == chunks[u] - 1)
                    mm.then_inc(mixed, 1)

        @block.scalar
        def _(act):
            for step in range(n_units + 1):
                if step < n_units:
                    u = step
                    act.wait_ge(maxed, u + 1)
                    if u >= 2:
                        act.wait_ge(turned, before[u - 1])
                    for b, (src, dst) in enumerate(zip(scores(u), probs(u))):
                        last = nc.scalar.activation(dst, src, ACT.Exp, bias=nm[:, u % 2, b:b + 1], scale=SCALE,
                                                    accum_out=sums[:, u % 2, b:b + 1])
                    last.then_inc(exped, 1)
                if step >= 1:
                    u = step - 1
                    for n in range(pieces[u]):
                        at = before[u] + n
                        act.wait_ge(turned, at + 1)
                        if n == 0 and u >= 2:
                            act.wait_ge(mixed, u - 1)
                        full = min(4, chunks[u] - 1 - 4 * n)
                        if full:
                            last = nc.scalar.activation(PT[:, u % 2, 4 * n:4 * n + full, :],
                                                        k.ps[:, 6 + at % 2, 0:full * P].rearrange("p (c q) -> p c q", q=P),
                                                        ACT.Copy)
                        if n == pieces[u] - 1:
                            last = nc.scalar.activation(PT[0:CMP, u % 2, chunks[u] - 1, :],
                                                        k.ps[0:CMP, 6 + at % 2, full * P:full * P + P], ACT.Copy)
                        last.then_inc(laid, 1)

        @block.vector
        def _(dve):
            ch = Chain(dve, chain)
            dve.wait_ge(loaded, 32)
            for step in range(n_units + 2):
                if step < n_units:
                    u = step
                    qt = units[u][0]
                    if u % 8 == 0:
                        dve.wait_ge(cmp_scored, qt + 1)
                        if u:
                            dve.wait_ge(exped, u)
                        nc.vector.tensor_tensor(cs[:], k.bank(4, 8 * CMP).rearrange("p (m n) -> p m n", n=CMP),
                                                cmask[:, qt:qt + 1, :].broadcast_to([P, 8, CMP]), ALU.add).then_inc(cmp_masked, 1)
                        dve.wait_ge(cmp_masked, qt + 1)
                    dve.wait_ge(scored, u + 1)
                    sel, win, cmp = scores(u)
                    last_keys = slice(qt * P, qt * P + P)
                    nc.vector.tensor_tensor(sel[:, last_keys], sel[:, last_keys], tri[:], ALU.add)
                    ch.link(nc.vector.tensor_tensor(win[:, last_keys], win[:, last_keys], tri[:], ALU.add))
                    for b, src in enumerate((sel, win, cmp)):
                        last = nc.vector.tensor_reduce(mx[:, u % 2, b:b + 1], src, AX.X, ALU.max)
                    ch.link(last)
                    nc.vector.tensor_scalar(nm[:, u % 2, :], mx[:, u % 2, :], NEG * 1e-10, -SCALE, ALU.max,
                                            ALU.mult).then_inc(maxed, 1)
                if 1 <= step <= n_units:
                    u = step - 1
                    qt, kv, i = units[u]
                    dve.wait_ge(exped, u + 1)
                    ch.link(nc.vector.tensor_scalar(wts[:, u % 2, :], sums[:, u % 2, :], 1e-30, None, ALU.max))
                    ch.link(nc.vector.reciprocal(wts[:, u % 2, :], wts[:, u % 2, :]))
                    g = 3 * (4 * kv + i)
                    nc.vector.tensor_tensor(wts[:, u % 2, 0:2], wts[:, u % 2, 0:2], k.gates[:, qt, g + 1:g + 3], ALU.mult)
                    ch.link(nc.vector.tensor_tensor(wts[:, u % 2, 2:3], wts[:, u % 2, 2:3], k.gates[:, qt, g:g + 1],
                                                    ALU.mult))
                    for b, dst in enumerate(probs(u)):
                        last = nc.vector.tensor_scalar(dst, dst, wts[:, u % 2, b:b + 1], None, ALU.mult)
                    last.then_inc(weighted, 1)
                if step >= 2:
                    u = step - 2
                    qt, kv, i = units[u]
                    half = slice(kv * HD, kv * HD + HD)
                    dve.wait_ge(mixed, u + 1)
                    nc.vector.tensor_copy(k.on[half, i, qt * P:qt * P + P], k.ps[half, 5, 0:P]).then_inc(out, 1)


def sample_attention_stage(k):
    nc = k.nc
    Z = k.z
    NG = DEC_BATCH // 2
    NSEL = PAST // SEL_BLOCK
    KEYS = dict(sel=(0, PAST), win=(PAST, WINDOW), seln=(PAST + WINDOW, TS), winn=(PAST + WINDOW + TS, TS),
                cmp=(PAST + WINDOW + 2 * TS, CH - 1))
    with ExitStack() as ctx:
        kv_pages = k.sb(ctx, "kv_pages", [P, 2, 2 * PAGES, 2 * P])
        wk = k.sb(ctx, "win_k", [P, 2, 2, WINDOW])
        wv = k.sb(ctx, "win_v", [P, 2, 2, 4, P])
        E = k.sb(ctx, "probs", [P, PAST + WINDOW + 2 * TS + CH])
        PT = k.sb(ctx, "probs_t", [P, 15, P])
        newmask = k.sb(ctx, "newmask", [P, NG, TS])
        winmask = k.sb(ctx, "winmask", [P, DEC_SEQ])
        pick = k.sb(ctx, "pick", [TS, NG, P])
        headmask = k.sb(ctx, "headmask", [P, NGATE])
        same = k.sb(ctx, "same", [P, P])
        iota = k.sb(ctx, "iota", [P, 14])
        mx = k.sb(ctx, "mx", [P, 5])
        nm = k.sb(ctx, "nm", [P, 3])
        sums = k.sb(ctx, "sums", [P, 5])
        wts = k.sb(ctx, "wts", [P, 3])
        pc = k.sb(ctx, "pc", [P, CH])
        imp = k.sb(ctx, "imp", [P, 14])
        pen = k.sb(ctx, "pen", [P, 14])
        one = k.sb(ctx, "one", [P, 2])
        gsel = k.sb(ctx, "gsel", [P, NGATE])
        gr = k.sb(ctx, "gr", [P, 3])
        qs = k.sb(ctx, "qs", [P, 2, DEC_BATCH, 4 * DEC_SEQ])
        V = Steps(None, "cmpmax pc maxes weighted out")
        S = Steps(None, "cmpexp exps laid1 laid2")
        PE = Steps(None, "scores imp turned1 turned2 mixed")
        v_at, s_at, e_at, loaded, landed0, landed1, chain, packed = k.sems(
            ctx, "dve_step", "act_step", "pe_step", "loaded", "landed0", "landed1", "chain", "packed")
        landed = (landed0, landed1)
        tables = [(newmask.rearrange("p g t -> p (g t)"), "newmask"), (winmask[:], "winmask"),
                  (pick.rearrange("p g t -> p (g t)"), "pick"), (headmask[:], "headmask"), (same[:], "same"),
                  (iota[:], "iota14")]
        past = k.ps[:, 0:2, :].rearrange("p b n -> p (b n)")
        win, small = k.bank(2), k.bank(3)
        near = k.sb(ctx, "near", [P, 3 * CH])
        parts = lambda t: (t[:, 0:CH - 1], t[:, CH:2 * CH], t[:, 2 * CH:3 * CH])
        cmp, seln, winn = parts(near)
        isum, grow, mix = k.ps[:, 4, 0:CH - 1], k.ps[:, 4, 128:128 + NGATE], k.ps[:, 4, 256:256 + P]
        probs = lambda name: E[:, KEYS[name][0]:KEYS[name][0] + KEYS[name][1]]
        block = ctx.enter_context(nc.Block())

        @block.sync
        def _(sp):
            for dst, name in tables:
                sp.dma_start(dst, k.d[name]).then_inc(loaded, 16)
            for g in range(NG):
                b = g % 2
                if g >= 2:
                    sp.wait_ge(e_at, PE.at("mixed", g - 2))
                with sp.Fori(0, 2 * PAGES) as i:
                    page = sp.value_load(k.table[0:1, bass.ds(g * 2 * PAGES + i, 1)], min_val=0, max_val=k.n_phys - 1)
                    sp.dma_start(kv_pages[:, b, bass.ds(i, 1), :].rearrange("p o n -> p (o n)"),
                                 k.d["sel_pages"][bass.ds(page, 1)].rearrange("o p n -> (o p) n")).then_inc(landed[b], 16)
                sp.dma_start(wk[:, b].rearrange("p s n -> p (s n)"), k.d["win_k"][g]).then_inc(landed[b], 16)
                sp.dma_start(wv[:, b].rearrange("p s c n -> p (s c n)"), k.d["win_v"][g]).then_inc(landed[b], 16)

        @block.tensor
        def _(pe):
            pe.wait_ge(loaded, 16 * len(tables))
            pe.wait_ge(packed, 2)
            for g in range(NG):
                b = g % 2
                pe.wait_ge(landed[b], (g // 2 + 1) * 16 * (2 * PAGES + 2))
                if g:
                    pe.wait_ge(s_at, S.at("exps", g - 1))
                    pe.wait_ge(v_at, V.at("out", g - 1))
                for s in range(2):
                    seq = 2 * g + s
                    for kv in range(2):
                        half = slice(kv * HD, kv * HD + HD)
                        rows = slice(32 * (2 * s + kv), 32 * (2 * s + kv) + 32)
                        qr, qn = qs[half, 0, seq, :], qs[half, 1, seq, :]
                        for n in range(2):
                            nc.tensor.matmul(past[rows, n * 512:(n + 1) * 512], qr,
                                             kv_pages[half, b, PAGES * s + 4 * n:PAGES * s + 4 * n + 4, 0:P],
                                             start=True, stop=True)
                        nc.tensor.matmul(win[rows, :], qr, wk[half, b, s, :], start=True, stop=True)
                        pcmp, pseln, pwinn = parts(small)
                        nc.tensor.matmul(pcmp[rows, :], qn, k.kc[half, seq, 0:CH - 1], start=True, stop=True)
                        nc.tensor.matmul(pseln[rows, :], qr, Z[half, ZK + 2, SEQ:T], start=True, stop=True)
                        nc.tensor.matmul(pwinn[rows, :], qr, Z[half, ZK + 4, SEQ:T], start=True, stop=True)
                nc.tensor.matmul(grow, pick[:, g, :], k.gates[0:TS, 4, :], start=True, stop=True).then_inc(e_at, 1)
                pe.wait_ge(v_at, V.at("pc", g))
                nc.tensor.matmul(isum, same[:], pc[:, 0:CH - 1], start=True, stop=True).then_inc(e_at, 1)
                pe.wait_ge(v_at, V.at("weighted", g))
                for n in range(12):
                    mm = nc.tensor.transpose(k.ps[:, 5 + n // 4, (n % 4) * P:(n % 4) * P + P], E[:, n * P:(n + 1) * P],
                                             k.ident[:])
                mm.then_inc(e_at, 1)
                pe.wait_ge(s_at, S.at("laid1", g))
                for n, name in enumerate(("seln", "winn", "cmp")):
                    mm = nc.tensor.transpose(k.ps[0:KEYS[name][1], 5, n * P:n * P + P], probs(name), k.ident[:])
                mm.then_inc(e_at, 1)
                pe.wait_ge(s_at, S.at("laid2", g))
                for s in range(2):
                    seq = 2 * g + s
                    cols = slice(CH * s, CH * s + CH)
                    terms = [(kv_pages[:, b, PAGES * s + n, P:2 * P], PT[:, n, cols]) for n in range(PAGES)]
                    terms += [(wv[:, b, s, n, :], PT[:, PAGES + n, cols]) for n in range(4)]
                    terms += [(k.vs[0:TS, 4, :], PT[0:TS, 12, cols]), (k.vw[0:TS, 4, :], PT[0:TS, 13, cols]),
                              (k.vc[0:CH - 1, seq, :], PT[0:CH - 1, 14, cols])]
                    for n, (lhs, rhs) in enumerate(terms):
                        mm = nc.tensor.matmul(mix[:, cols], lhs, rhs, start=n == 0, stop=n == len(terms) - 1)
                mm.then_inc(e_at, 1)

        @block.scalar
        def _(act):
            for g in range(NG):
                act.wait_ge(v_at, V.at("cmpmax", g))
                if g:
                    act.wait_ge(e_at, PE.at("turned2", g - 1))
                nc.scalar.activation(probs("cmp"), cmp, ACT.Exp, bias=nm[:, 0:1], scale=SCALE,
                                     accum_out=sums[:, 0:1]).then_inc(s_at, 1)
                act.wait_ge(v_at, V.at("maxes", g))
                for n, (name, src, b) in enumerate((("sel", past, 1), ("seln", seln, 1), ("win", win, 2),
                                                    ("winn", winn, 2))):
                    last = nc.scalar.activation(probs(name), src, ACT.Exp, bias=nm[:, b:b + 1], scale=SCALE,
                                                accum_out=sums[:, 1 + n:2 + n])
                last.then_inc(s_at, 1)
                act.wait_ge(e_at, PE.at("turned1", g))
                last = nc.scalar.activation(PT[:, 0:12, :].rearrange("p c q -> p (c q)"),
                                            k.ps[:, 5:8, :].rearrange("p b n -> p (b n)"), ACT.Copy)
                last.then_inc(s_at, 1)
                act.wait_ge(e_at, PE.at("turned2", g))
                nc.scalar.activation(PT[0:TS, 12:14, :].rearrange("p c q -> p (c q)"), k.ps[0:TS, 5, 0:2 * P], ACT.Copy)
                nc.scalar.activation(PT[0:CH - 1, 14, :], k.ps[0:CH - 1, 5, 2 * P:3 * P], ACT.Copy).then_inc(s_at, 1)

        @block.vector
        def _(dve):
            ch = Chain(dve, chain)
            for m, src in enumerate((k.qr, Z[:, ZQ:ZQ + 4, :])):
                for i in range(4):
                    last = nc.vector.tensor_copy(qs[:, m].rearrange("p s (i t) -> p s i t", i=4)[:, :, i, :],
                                                 src[:, i, SEQ:T].rearrange("p (s t) -> p s t", t=DEC_SEQ))
                last.then_inc(packed, 1)
            dve.wait_ge(loaded, 16 * len(tables))
            for g in range(NG):
                dve.wait_ge(e_at, PE.at("scores", g))
                for dst, src in zip(parts(near), parts(small)):
                    last = nc.vector.tensor_copy(dst, src)
                ch.link(last)
                ch.link(nc.vector.tensor_reduce(mx[:, 0:1], cmp, AX.X, ALU.max))
                nc.vector.tensor_scalar(nm[:, 0:1], mx[:, 0:1], -SCALE, None, ALU.mult).then_inc(v_at, 1)
                nc.vector.tensor_tensor(seln, seln, newmask[:, g, :], ALU.add)
                nc.vector.tensor_tensor(winn, winn, newmask[:, g, :], ALU.add)
                nc.vector.tensor_tensor(win[:, 0:DEC_SEQ], win[:, 0:DEC_SEQ], winmask[:], ALU.add)
                ch.link(nc.vector.tensor_tensor(gsel[:], grow, headmask[:], ALU.mult))
                nc.vector.tensor_reduce(gr[:], gsel.rearrange("p (h b) -> p b h", b=3), AX.X, ALU.add)
                nc.vector.tensor_reduce(mx[:, 1:2], seln, AX.X, ALU.max)
                nc.vector.tensor_reduce(mx[:, 2:3], win, AX.X, ALU.max)
                ch.link(nc.vector.tensor_reduce(mx[:, 3:4], winn, AX.X, ALU.max))
                dve.wait_ge(s_at, S.at("cmpexp", g))
                ch.link(nc.vector.tensor_scalar(wts[:, 0:1], sums[:, 0:1], 1e-30, None, ALU.max))
                ch.link(nc.vector.reciprocal(wts[:, 0:1], wts[:, 0:1]))
                nc.vector.tensor_scalar(pc[:, 0:CH - 1], probs("cmp"), wts[:, 0:1], None, ALU.mult).then_inc(v_at, 1)
                dve.wait_ge(e_at, PE.at("imp", g))
                ch.link(nc.vector.tensor_copy(pc[:, 0:CH - 1], isum))
                windows = pc[:, 3:3 + 4 * 14].rearrange("p (j c) -> p j c", c=4)
                ch.link(nc.vector.tensor_reduce(imp[:], windows, AX.X, ALU.add))
                ch.link(nc.vector.tensor_tensor(imp[:], imp[:], pc[:, 7:7 + 4 * 14:4], ALU.add))
                ch.link(nc.vector.tensor_reduce(one[:, 0:1], imp[:], AX.X, ALU.min))
                ch.link(nc.vector.tensor_scalar(pen[:], imp[:], one[:, 0:1], None, ALU.is_le))
                ch.link(nc.vector.tensor_tensor(pen[:], pen[:], iota[:], ALU.mult))
                ch.link(nc.vector.tensor_reduce(one[:, 1:2], pen[:], AX.X, ALU.max))
                ch.link(nc.vector.tensor_scalar(pen[:], iota[:], one[:, 1:2], NEG, ALU.is_equal, ALU.mult))
                blocks = past[:, SEL_BLOCK:15 * SEL_BLOCK].rearrange("p (j c) -> p j c", c=SEL_BLOCK)
                ch.link(nc.vector.tensor_tensor(blocks, blocks, pen.rearrange("p (j o) -> p j o", o=1)
                                                .broadcast_to([P, 14, SEL_BLOCK]), ALU.add))
                ch.link(nc.vector.tensor_reduce(mx[:, 4:5], past, AX.X, ALU.max))
                ch.link(nc.vector.tensor_tensor(mx[:, 0:1], mx[:, 4:5], mx[:, 1:2], ALU.max))
                ch.link(nc.vector.tensor_tensor(mx[:, 1:2], mx[:, 2:3], mx[:, 3:4], ALU.max))
                nc.vector.tensor_scalar(nm[:, 1:3], mx[:, 0:2], -SCALE, None, ALU.mult).then_inc(v_at, 1)
                dve.wait_ge(s_at, S.at("exps", g))
                nc.vector.tensor_tensor(wts[:, 1:2], sums[:, 1:2], sums[:, 2:3], ALU.add)
                ch.link(nc.vector.tensor_tensor(wts[:, 2:3], sums[:, 3:4], sums[:, 4:5], ALU.add))
                ch.link(nc.vector.tensor_scalar(wts[:, 1:3], wts[:, 1:3], 1e-30, None, ALU.max))
                ch.link(nc.vector.reciprocal(wts[:, 1:3], wts[:, 1:3]))
                ch.link(nc.vector.tensor_tensor(wts[:], wts[:], gr[:], ALU.mult))
                for name, b in (("sel", 1), ("seln", 1), ("win", 2), ("winn", 2), ("cmp", 0)):
                    last = nc.vector.tensor_scalar(probs(name), probs(name), wts[:, b:b + 1], None, ALU.mult)
                last.then_inc(v_at, 1)
                dve.wait_ge(e_at, PE.at("mixed", g))
                for kv in range(2):
                    half = slice(kv * HD, kv * HD + HD)
                    for s in range(2):
                        at = SEQ + (2 * g + s) * DEC_SEQ
                        src = mix[half, CH * s + 32 * kv:CH * s + 32 * kv + 32].rearrange("p (i t) -> p i t", i=4)
                        last = nc.vector.tensor_copy(k.on[half, :, at:at + DEC_SEQ], src)
                last.then_inc(v_at, 1)


def merge_stage(k, m_hi, m_lo):
    nc = k.nc
    out = k.z[:, 8:16, :]
    ring = 4
    with ExitStack() as ctx:
        wt = k.sb(ctx, "wt", [P, ring, KD, P])
        tmp = k.sb(ctx, "tmp", [P, T])
        arrived = k.sems(ctx, *[f"arrived{b}" for b in range(ring)])
        multiplied, gated, merged, rounded, chain = k.sems(ctx, "multiplied", "gated", "merged", "rounded", "chain")
        block = ctx.enter_context(nc.Block())

        @block.sync
        def _(sp):
            for n in range(KD):
                if n >= ring:
                    sp.wait_ge(multiplied, n - ring + 1)
                sp.dma_start(wt[:, n % ring].rearrange("p c n -> p (c n)"), k.d["w_merge"][n]).then_inc(arrived[n % ring], 16)

        @block.tensor
        def _(pe):
            for n in range(KD):
                pe.wait_ge(arrived[n % ring], 16 * (n // ring + 1))
                if n >= 2:
                    pe.wait_ge(merged, n - 1)
                for branch, src in enumerate((k.r.o, k.on)):
                    for c in range(4):
                        for h in range(2):
                            mm = nc.tensor.matmul(k.bank(4 * (n % 2) + 2 * branch + h, TH), wt[:, n % ring, 4 * branch + c, :],
                                                  src[:, c, h * TH:(h + 1) * TH], start=c == 0, stop=c == 3)
                mm.then_inc(multiplied, 1)

        @block.scalar
        def _(act):
            for n in range(KD):
                nc.scalar.activation(k.zg[:, n, :], k.zg[:, n, :], ACT.Sigmoid)
                nc.scalar.activation(k.zg[:, KD + n, :], k.zg[:, KD + n, :], ACT.Sigmoid).then_inc(gated, 1)
            for n in range(KD):
                act.wait_ge(merged, n + 1)
                nc.scalar.activation(m_hi[:, n, :], out[:, n, :], ACT.Copy).then_inc(rounded, 1)

        @block.vector
        def _(dve):
            ch = Chain(dve, chain)
            for n in range(KD):
                dve.wait_ge(gated, n + 1)
                dve.wait_ge(multiplied, n + 1)
                if n:
                    dve.wait_ge(merged, n)
                b = 4 * (n % 2)
                nc.vector.tensor_tensor(halves(out[:, n, :]), k.pair(b), halves(k.zg[:, n, :]), ALU.mult)
                ch.link(nc.vector.tensor_tensor(halves(tmp[:]), k.pair(b + 2), halves(k.zg[:, KD + n, :]), ALU.mult))
                nc.vector.tensor_tensor(out[:, n, :], out[:, n, :], tmp[:], ALU.add).then_inc(merged, 1)
            for n in range(KD):
                dve.wait_ge(rounded, n + 1)
                last = nc.vector.tensor_tensor(m_lo[:, n, :], out[:, n, :], m_hi[:, n, :].bitcast(F32), ALU.subtract)
            ch.link(last)


def choose_stage(k, q, picked):
    nc = k.nc
    NP = P
    tiles = [(tt * P, min(P, T - tt * P)) for tt in range(5)]
    HC = 2 * HEADS
    with ExitStack() as ctx:
        keys = k.sb(ctx, "keys", [P, HEADS, N_KEYS])
        sc = k.sb(ctx, "sc", [P, 2, HC, N_KEYS])
        sv = k.sb(ctx, "sv", [P, HC, TOPK])
        si = k.sb(ctx, "si", [P, HC, TOPK], U32)
        sif = k.sb(ctx, "sif", [P, HC, TOPK])
        cand = k.sb(ctx, "cand", [P, HEADS, TOPK, TOPK])
        cv = k.sb(ctx, "cv", [P, HEADS, TOPK])
        ci = k.sb(ctx, "ci", [P, HEADS, TOPK], U32)
        cj = k.sb(ctx, "cj", [P, 2, HEADS * TOPK], U32)
        cjf = k.sb(ctx, "cjf", [P, 2, HEADS * TOPK])
        hot = k.sb(ctx, "hot", [P, HEADS * TOPK, TOPK])
        num = k.sb(ctx, "num", [P, 3, HEADS * TOPK])
        ex = k.sb(ctx, "ex", [P, HEADS, TOPK])
        tot = k.sb(ctx, "tot", [P, HEADS])
        iota = k.sb(ctx, "iota", [P, TOPK])
        loaded, scored, copied, lowered, exped, chosen, turned, laid, chain = k.sems(
            ctx, "loaded", "scored", "copied", "lowered", "exped", "chosen", "turned", "laid", "chain")
        block = ctx.enter_context(nc.Block())

        @block.sync
        def _(sp):
            sp.dma_start(keys.rearrange("p h n -> p (h n)"), k.d["keys"]).then_inc(loaded, 16)
            sp.dma_start(iota[:], k.d["iota16"]).then_inc(loaded, 16)

        @block.tensor
        def _(pe):
            pe.wait_ge(loaded, 32)
            for n, (at, rows) in enumerate(tiles):
                if n:
                    pe.wait_ge(copied, n)
                for h in range(HEADS):
                    for c in range(2):
                        half = slice(c * HD, c * HD + HD)
                        mm = nc.tensor.matmul(k.ps[0:rows, 2 * c + h // 4, (h % 4) * N_KEYS:(h % 4 + 1) * N_KEYS],
                                              q[half, h, at:at + rows], keys[half, h, :], start=True, stop=True)
                mm.then_inc(scored, 1)
                pe.wait_ge(chosen, n + 1)
                if n:
                    pe.wait_ge(laid, n)
                for m in range(3):
                    mm = nc.tensor.transpose(k.ps[:, 4, m * P:m * P + rows], num[0:rows, m, :], k.ident[0:rows, 0:rows])
                mm.then_inc(turned, 1)

        @block.scalar
        def _(act):
            for n, (at, rows) in enumerate(tiles):
                act.wait_ge(scored, n + 1)
                if n:
                    act.wait_ge(lowered, n)
                nc.scalar.activation(sc[0:rows, 0].rearrange("p a n -> p (a n)"),
                                     k.ps[0:rows, 0:4, :].rearrange("p b n -> p (b n)"), ACT.Copy).then_inc(copied, 1)
                act.wait_ge(lowered, n + 1)
                nc.scalar.activation(ex[0:rows], ex[0:rows], ACT.Exp).then_inc(exped, 1)
                act.wait_ge(turned, n + 1)
                nc.scalar.activation(picked[:, :, at:at + rows],
                                     k.ps[:, 4, 0:3 * P].rearrange("p (m t) -> p m t", m=3)[:, :, 0:rows],
                                     ACT.Copy).then_inc(laid, 1)

        @block.vector
        def _(dve):
            ch = Chain(dve, chain)
            dve.wait_ge(loaded, 32)

            def top16(src, spare, val, idx, count, rows):
                for n in range(count):
                    last = nc.vector.max(val[0:rows, n, 0:8], src(n))
                ch.link(last)
                for n in range(count):
                    nc.vector.max_index(idx[0:rows, n, 0:8], val[0:rows, n, 0:8], src(n))
                    last = nc.vector.match_replace(spare(n), val[0:rows, n, 0:8], src(n), NEG)
                ch.link(last)
                for n in range(count):
                    last = nc.vector.max(val[0:rows, n, 8:16], spare(n))
                ch.link(last)
                for n in range(count):
                    last = nc.vector.max_index(idx[0:rows, n, 8:16], val[0:rows, n, 8:16], spare(n))
                ch.link(last)

            for n, (at, rows) in enumerate(tiles):
                r = slice(0, rows)
                dve.wait_ge(copied, n + 1)
                top16(lambda m: sc[r, 0, m, :], lambda m: sc[r, 1, m, :], sv, si, HC, rows)
                nc.vector.tensor_copy(sif[r], si[r])
                first = sv[r, 0:HEADS, :].rearrange("p h (j o) -> p h j o", o=1).broadcast_to([rows, HEADS, TOPK, TOPK])
                second = sv[r, HEADS:, :].rearrange("p h (o j) -> p h o j", o=1).broadcast_to([rows, HEADS, TOPK, TOPK])
                ch.link(nc.vector.tensor_tensor(cand[r], first, second, ALU.add))
                spare = sc[:, 1].rearrange("p a n -> p (a n)").rearrange("p (h m) -> p h m", h=HEADS)
                top16(lambda m: cand[r, m].rearrange("p a b -> p (a b)"), lambda m: spare[r, m, :], cv, ci, HEADS, rows)
                nc.vector.tensor_scalar(cj[r, 0], ci[r].rearrange("p h j -> p (h j)"), 4, None, ALU.logical_shift_right)
                nc.vector.tensor_scalar(cj[r, 1], ci[r].rearrange("p h j -> p (h j)"), 15, None, ALU.bitwise_and)
                ch.link(nc.vector.tensor_tensor(ex[r], cv[r], cv[r, :, 0:1].broadcast_to([rows, HEADS, TOPK]),
                                                ALU.subtract))
                nc.vector.tensor_copy(cjf[r], cj[r]).then_inc(lowered, 1)
                dve.wait_ge(lowered, n + 1)
                for c in range(2):
                    place = cjf[r, c, :].rearrange("p (a o) -> p a o", o=1).broadcast_to([rows, P, TOPK])
                    slot = iota[r].rearrange("p (o j) -> p o j", o=1).broadcast_to([rows, P, TOPK])
                    ch.link(nc.vector.tensor_tensor(hot[r], place, slot, ALU.is_equal))
                    which = sif[r, c * HEADS:(c + 1) * HEADS, :].rearrange("p h (o j) -> p h o j", o=1) \
                        .broadcast_to([rows, HEADS, TOPK, TOPK])
                    hot4 = hot[r].rearrange("p (h a) j -> p h a j", h=HEADS)
                    ch.link(nc.vector.tensor_tensor(hot4, hot4, which, ALU.mult))
                    if c == 0 and n:
                        dve.wait_ge(turned, n)
                    ch.link(nc.vector.tensor_reduce(num[r, c, :], hot[r], AX.X, ALU.add))
                dve.wait_ge(exped, n + 1)
                ch.link(nc.vector.tensor_reduce(tot[r], ex[r], AX.X, ALU.add))
                ch.link(nc.vector.reciprocal(tot[r], tot[r]))
                nc.vector.tensor_tensor(num[r, 2, :].rearrange("p (h j) -> p h j", h=HEADS), ex[r],
                                        tot[r].rearrange("p (h o) -> p h o", o=1).broadcast_to([rows, HEADS, TOPK]),
                                        ALU.mult).then_inc(chosen, 1)


def gate_matrix_stage(k, picked):
    nc = k.nc
    Q = 4
    rounds = T // (2 * TB)
    with ExitStack() as ctx:
        a = k.sb(ctx, "a", [P, TB, N_KEYS])
        b = k.sb(ctx, "b", [P, TB, N_KEYS])
        nq = TB // Q
        cur = k.sb(ctx, "cur", [P, 2, 3, TB])
        G = k.sb(ctx, "g", [P, 2, N_KEYS, TB])
        iota = k.sb(ctx, "iota", [P, N_KEYS])
        loaded, current, a_made, b_made, spread, taken, stored0, stored1, passed = k.sems(
            ctx, "loaded", "current", "a_made", "b_made", "spread", "taken", "stored0", "stored1", "passed")
        stored = (stored0, stored1)
        block = ctx.enter_context(nc.Block())

        @block.sync
        def _(sp):
            sp.dma_start(iota[:], k.d["iota128"]).then_inc(loaded, 16)
            with sp.Fori(0, rounds) as i:
                for s in range(2):
                    sp.wait_ge(taken, (i * 2 + s) * nq + nq + nq)
                    sp.dma_start(k.g_dram[bass.ds(i * 2 + s, 1)].rearrange("o p n -> (o p) n"),
                                 G[:, s].rearrange("p n t -> p (n t)")).then_inc(stored[s], 16)
            for s in range(2):
                sp.wait_ge(stored[s], 16 * (rounds + 1))

        @block.vector
        def _(dve):
            dve.sem_inc(spread, nq)
            dve.wait_ge(loaded, 16)
            with dve.Fori(0, rounds) as i:
                for s in range(2):
                    dve.wait_ge(spread, (i * 2 + s) * nq + 1)
                    nc.vector.tensor_copy(cur[:, s], picked[:, :, bass.ds(i * 2 * TB + s * TB, TB)]).then_inc(current, 1)
                    dve.wait_ge(current, i * 2 + s + 1)
                    for q in range(nq):
                        dve.wait_ge(spread, (i * 2 + s) * nq + q + 1)
                        for t in range(Q * q, Q * q + Q):
                            last = nc.vector.tensor_scalar(a[:, t, :], iota[:], cur[:, s, 0, t:t + 1], cur[:, s, 2, t:t + 1],
                                                           ALU.is_equal, ALU.mult)
                        last.then_inc(a_made, 1)

        @block.gpsimd
        def _(pool):
            pool.wait_ge(loaded, 16)
            with pool.Fori(0, rounds) as i:
                for s in range(2):
                    pool.wait_ge(current, i * 2 + s + 1)
                    for q in range(nq):
                        pool.wait_ge(spread, (i * 2 + s) * nq + q + 1)
                        pool.sem_inc(passed, 1)
                        for t in range(Q * q, Q * q + Q):
                            last = nc.gpsimd.tensor_scalar(b[:, t, :], iota[:], cur[:, s, 1, t:t + 1], None, ALU.is_equal)
                        last.then_inc(b_made, 1)

        @block.tensor
        def _(pe):
            with pe.Fori(0, rounds) as i:
                for s in range(2):
                    for q in range(nq):
                        pe.wait_ge(a_made, (i * 2 + s) * nq + q + 1)
                        pe.wait_ge(b_made, (i * 2 + s) * nq + q + 1)
                        pe.wait_ge(taken, (i * 2 + s) * nq + q + 1)
                        for t in range(Q * q, Q * q + Q):
                            mm = nc.tensor.matmul(k.ps[:, q, (t % Q) * P:(t % Q + 1) * P], b[:, t, :], a[:, t, :],
                                                  start=True, stop=True)
                        mm.then_inc(spread, 1)

        @block.scalar
        def _(act):
            act.sem_inc(taken, nq)
            for s in range(2):
                act.sem_inc(stored[s], 16)
            with act.Fori(0, rounds) as i:
                for s in range(2):
                    act.wait_ge(stored[s], i * 16 + 16)
                    for q in range(nq):
                        act.wait_ge(spread, (i * 2 + s) * nq + nq + q + 1)
                        nc.scalar.activation(G[:, s, :, Q * q:Q * q + Q].rearrange("p n t -> p t n"),
                                             k.bank(q).rearrange("p (t n) -> p t n", t=Q), ACT.Copy).then_inc(taken, 1)


def experts_stage(k, h, y):
    nc = k.nc
    EG = 4
    groups = N_KEYS // EG
    h_hi, h_lo = h
    with ExitStack() as ctx:
        u_raw = k.sb(ctx, "u_raw", [P, EG, KD, P])
        u_hi = k.sb(ctx, "u_hi", [P, 2, KD, P], F32R)
        u_lo = k.sb(ctx, "u_lo", [P, 2, KD, P], F32R)
        v_raw = k.sb(ctx, "v_raw", [P, 2, D_MODEL])
        v_hi = k.sb(ctx, "v_hi", [P, EG, D_MODEL], F32R)
        v_lo = k.sb(ctx, "v_lo", [P, EG, D_MODEL], F32R)
        G = k.sb(ctx, "g", [P, T // TB, EG, TB])
        act_t = k.sb(ctx, "act", [P, 2, T])
        w = k.sb(ctx, "w", [P, T])
        w_hi = k.sb(ctx, "w_hi", [P, EG, T], F32R)
        w_lo = k.sb(ctx, "w_lo", [P, EG, T], F32R)
        u_in = k.sems(ctx, *[f"u_in{e}" for e in range(EG)])
        v_in = k.sems(ctx, "v_in0", "v_in1")
        (g_in, u_rounded, u_parted, v_rounded, v_parted, up, gelued, gated, w_rounded, weighed, down, added,
         cleared) = k.sems(ctx, "g_in", "u_rounded", "u_parted", "v_rounded", "v_parted", "up", "gelued", "gated",
                           "w_rounded", "weighed", "down", "added", "cleared")
        U0, V0, UP0, GE0, WE0, DN0, AD0 = EG, 2, 0, 2, 2, KD, 2
        block = ctx.enter_context(nc.Block())

        @block.sync
        def _(sp):
            with sp.Fori(0, groups) as i:
                for e in range(EG):
                    sp.wait_ge(u_parted, i * EG + e + 1)
                    sp.dma_start(u_raw[:, e].rearrange("p c n -> p (c n)"),
                                 k.d["peer_u"][bass.ds(i * EG + e, 1)].rearrange("o p n -> (o p) n")).then_inc(u_in[e], 16)
                sp.wait_ge(weighed, i * EG + WE0)
                sp.dma_start(G.rearrange("p c e t -> p c (e t)"),
                             k.g_dram.rearrange("c p n -> p c n")[:, :, bass.ds(i * (EG * TB), EG * TB)]).then_inc(g_in, 16)
                for e in range(EG):
                    sp.wait_ge(v_parted, i * EG + e + 1)
                    sp.dma_start(v_raw[:, e % 2],
                                 k.d["peer_v"][bass.ds(i * EG + e, 1)].rearrange("o p n -> (o p) n")).then_inc(v_in[e % 2], 16)

        @block.tensor
        def _(pe):
            pe.sem_inc(down, DN0)
            with pe.Fori(0, groups) as i:
                for e in range(EG):
                    pe.wait_ge(u_parted, i * EG + U0 + e + 1)
                    pe.wait_ge(gelued, i * EG + e + 1)
                    for c in range(KD):
                        for n, (lhs, r) in enumerate(three_passes(u_hi[:, e % 2, c, :], u_lo[:, e % 2, c, :], h_hi, h_lo)):
                            for s in range(2):
                                mm = nc.tensor.matmul(k.bank(2 * (e % 2) + s, TH), lhs, r[:, c, s * TH:(s + 1) * TH],
                                                      start=c == 0 and n == 0, stop=c == KD - 1 and n == 2)
                    mm.then_inc(up, 1)
                pe.wait_ge(v_parted, i * EG + V0 + EG)
                for d in range(KD):
                    pe.wait_ge(added, i * KD + d + 1)
                    for e in range(EG):
                        if d == 0 and e in (0, EG - 1):
                            pe.wait_ge(weighed, i * EG + WE0 + (EG if e else EG - 1))
                        for n, (lhs, r) in enumerate(three_passes(v_hi[:, e, d * P:(d + 1) * P], v_lo[:, e, d * P:(d + 1) * P],
                                                                  w_hi, w_lo)):
                            for s in range(2):
                                mm = nc.tensor.matmul(k.bank(4 + 2 * (d % 2) + s, TH), lhs, r[:, e, s * TH:(s + 1) * TH],
                                                      start=e == 0 and n == 0, stop=e == EG - 1 and n == 2)
                    mm.then_inc(down, 1)

        def parts_ahead(last):
            return () if last else (0, 1)

        @block.scalar
        def _(act):
            def round_u(i, e, first=False):
                act.wait_ge(u_in[e], i * 16 + 16)
                if not first:
                    act.wait_ge(up, i * EG + e - 1)
                nc.scalar.activation(u_hi[:, e % 2], u_raw[:, e], ACT.Copy).then_inc(u_rounded, 1)

            def round_group(i, last):
                for e in range(EG):
                    act.wait_ge(v_in[e % 2], i * 32 + 16 * (e // 2 + 1))
                    act.wait_ge(down, i * KD + DN0)
                    nc.scalar.activation(v_hi[:, e, :], v_raw[:, e % 2, :], ACT.Copy).then_inc(v_rounded, 1)
                    act.wait_ge(up, i * EG + e + 1)
                    act.wait_ge(weighed, i * EG + e + 1)
                    nc.scalar.activation(halves(act_t[:, e % 2, :]), k.pair(2 * (e % 2)), ACT.Gelu_apprx_tanh).then_inc(gelued, 1)
                    if e < EG - 2:
                        round_u(i, e + 2)
                for e in parts_ahead(last):
                    round_u(i + 1, e)

            act.sem_inc(gelued, GE0)
            for e in range(2):
                round_u(0, e, first=True)
            with act.Fori(0, groups - 1) as i:
                round_group(i, False)
            round_group(groups - 1, True)

        @block.vector
        def _(dve):
            def part_u(i, e):
                dve.wait_ge(u_rounded, i * EG + e + 1)
                nc.vector.tensor_tensor(u_lo[:, e % 2], u_raw[:, e], u_hi[:, e % 2].bitcast(F32),
                                        ALU.subtract).then_inc(u_parted, 1)

            def round_group(i, last):
                dve.wait_ge(g_in, i * 16 + 16)
                for e in range(EG):
                    dve.wait_ge(v_rounded, i * EG + e + 1)
                    nc.vector.tensor_tensor(v_lo[:, e, :], v_raw[:, e % 2, :], v_hi[:, e, :].bitcast(F32),
                                            ALU.subtract).then_inc(v_parted, 1)
                    dve.wait_ge(gelued, i * EG + GE0 + e + 1)
                    dve.wait_ge(weighed, i * EG + WE0 + e)
                    nc.vector.tensor_tensor(w.rearrange("p (c t) -> p c t", t=TB),
                                            act_t[:, e % 2, :].rearrange("p (c t) -> p c t", t=TB), G[:, :, e, :],
                                            ALU.mult).then_inc(gated, 1)
                    dve.wait_ge(gated, i * EG + e + 1)
                    nc.vector.tensor_copy(w_hi[:, e, :], w[:]).then_inc(w_rounded, 1)
                    dve.wait_ge(w_rounded, i * EG + e + 1)
                    nc.vector.tensor_tensor(w_lo[:, e, :], w[:], w_hi[:, e, :].bitcast(F32), ALU.subtract).then_inc(weighed, 1)
                    if e < EG - 2:
                        part_u(i, e + 2)
                for e in parts_ahead(last):
                    part_u(i + 1, e)
                for d in range(KD):
                    dve.wait_ge(down, i * KD + DN0 + d + 1)
                    nc.vector.tensor_tensor(halves(y[:, d, :]), k.pair(4 + 2 * (d % 2)), halves(y[:, d, :]),
                                            ALU.add).then_inc(added, 1)

            dve.sem_inc(u_parted, U0)
            dve.sem_inc(v_parted, V0)
            dve.sem_inc(weighed, WE0)
            dve.sem_inc(added, AD0)
            nc.vector.memset(y[:], 0.0).then_inc(cleared, 1)
            dve.wait_ge(cleared, 1)
            for e in range(2):
                part_u(0, e)
            with dve.Fori(0, groups - 1) as i:
                round_group(i, False)
            round_group(groups - 1, True)


def embed_stage(k, h):
    nc = k.nc
    ring = 4
    kt = KD + 2
    with ExitStack() as ctx:
        wt = k.sb(ctx, "wt", [P, ring, kt, P])
        w_hi = k.sb(ctx, "w_hi", [P, 2, KD, P], F32R)
        w_lo = k.sb(ctx, "w_lo", [P, 2, KD, P], F32R)
        p = k.sb(ctx, "p", [P, 2, T])
        sig = k.sb(ctx, "sig", [P, 2, T])
        arrived = k.sems(ctx, *[f"arrived{b}" for b in range(ring)])
        loaded, rounded, parted, multiplied, gated, made, stored, chain = k.sems(
            ctx, "loaded", "rounded", "parted", "multiplied", "gated", "made", "stored", "chain")
        block = ctx.enter_context(nc.Block())

        @block.sync
        def _(sp):
            for n in range(KD):
                if n >= ring:
                    sp.wait_ge(multiplied, n - ring + 1)
                sp.dma_start(wt[:, n % ring].rearrange("p c n -> p (c n)"), k.d["w_ple"][n]).then_inc(arrived[n % ring], 16)
                if n == 0:
                    sp.dma_start(p.rearrange("p c t -> p (c t)"), k.d["p"]).then_inc(loaded, 16)
            for n in range(KD):
                sp.wait_ge(made, n + 1)
                sp.dma_start(k.d["out_y"][n], k.x[:, n, :]).then_inc(stored, 16)
            sp.wait_ge(stored, 16 * KD)

        @block.tensor
        def _(pe):
            pe.wait_ge(loaded, 16)
            for n in range(KD):
                pe.wait_ge(parted, n + 1)
                if n >= 2:
                    pe.wait_ge(made, n - 1)
                for c in range(KD):
                    for m, (lhs, r) in enumerate(three_passes(w_hi[:, n % 2, c, :], w_lo[:, n % 2, c, :], *h)):
                        for s in range(2):
                            mm = nc.tensor.matmul(k.bank(4 * (n % 2) + s, TH), lhs, r[:, c, s * TH:(s + 1) * TH],
                                                  start=c == 0 and m == 0, stop=c == KD - 1 and m == 2)
                for c in range(2):
                    for s in range(2):
                        mm = nc.tensor.matmul(k.bank(4 * (n % 2) + 2 + s, TH), wt[:, n % ring, KD + c, :],
                                              p[:, c, s * TH:(s + 1) * TH], start=c == 0, stop=c == 1)
                mm.then_inc(multiplied, 1)

        @block.scalar
        def _(act):
            for n in range(KD + 1):
                if n < KD:
                    act.wait_ge(arrived[n % ring], 16 * (n // ring + 1))
                    if n >= 2:
                        act.wait_ge(multiplied, n - 1)
                    nc.scalar.activation(w_hi[:, n % 2], wt[:, n % ring, 0:KD, :], ACT.Copy).then_inc(rounded, 1)
                if n:
                    act.wait_ge(multiplied, n)
                    if n >= 3:
                        act.wait_ge(made, n - 2)
                    nc.scalar.activation(halves(sig[:, (n - 1) % 2, :]), k.pair(4 * ((n - 1) % 2)), ACT.Sigmoid).then_inc(gated, 1)

        @block.vector
        def _(dve):
            ch = Chain(dve, chain)
            for n in range(KD + 1):
                if n < KD:
                    dve.wait_ge(rounded, n + 1)
                    nc.vector.tensor_tensor(w_lo[:, n % 2], wt[:, n % ring, 0:KD, :], w_hi[:, n % 2].bitcast(F32),
                                            ALU.subtract).then_inc(parted, 1)
                if n:
                    m = n - 1
                    dve.wait_ge(gated, m + 1)
                    ch.link(nc.vector.tensor_tensor(halves(sig[:, m % 2, :]), halves(sig[:, m % 2, :]),
                                                    k.pair(4 * (m % 2) + 2), ALU.mult))
                    nc.vector.tensor_tensor(k.x[:, m, :], k.x[:, m, :], sig[:, m % 2, :], ALU.add).then_inc(made, 1)


def add_stage(k, y):
    nc = k.nc
    with ExitStack() as ctx:
        added, = k.sems(ctx, "added")
        block = ctx.enter_context(nc.Block())

        @block.vector
        def _(dve):
            nc.vector.tensor_tensor(k.x[:], k.x[:], y[:, :, :], ALU.add).then_inc(added, 1)
            dve.wait_ge(added, 1)


def layer_program(nc, d, n_phys, last=99):
    k = Core(nc)
    k.d, k.n_phys = d, n_phys
    with ExitStack() as whole:
        k.ps = whole.enter_context(nc.psum_tensor("ps", [P, 8, 512], F32))
        k.x = k.sb(whole, "x", [P, KD, T])
        k.params = k.sb(whole, "params", [P, NPARAM])
        k.ones = k.sb(whole, "ones", [P, P])
        k.blocks = k.sb(whole, "blocks", [P, P])
        k.ident = k.sb(whole, "ident", [P, P])
        k.gates = k.sb(whole, "gates", [P, 5, NGATE])
        k.table = k.sb(whole, "table", [1, DEC_BATCH * PAGES], mybir.dt.int32)
        load_stage(k)
        with ExitStack() as mixing:
            k.z = k.sb(mixing, "z", [P, NZ, T])
            k.r = Tiles()
            k.r.o = k.z[:, 4:8, :]
            with ExitStack() as ctx:
                h = [k.sb(ctx, name, [P, KD, T], F32R) for name in ("h_hi", "h_lo")]
                wg = k.sb(ctx, "wg", [P, KD, NGATE])
                norm_stage(k, "attn_norm", *h)
                project_stage(k, d["w_in"], NZ, h, k.z, gates=(d["w_gates"], wg, k.gates))
            with ExitStack() as ctx:
                xs = k.sb(ctx, "xs", [P, RCOLS, T])
                k.r.kt, k.r.bt, k.r.bonus, k.r.g = (k.sb(ctx, name, [P, 4, T]) for name in ("kt", "bt", "bonus", "g"))
                k.r.ends = k.sb(ctx, "ends", [P, 4, NCH + DEC_BATCH])
                k.r.xs, k.r.rt, k.r.ht, k.r.vt = xs, xs[:, 0:4, :], xs[:, 4:8, :], xs[:, 8:12, :]
                rwkv_prepare_stage(k)
                rwkv_chunks_stage(k, sample=False)
                rwkv_chunks_stage(k, sample=True)
                rwkv_finish_stage(k)
            k.on = k.sb(mixing, "on", [P, 4, T])
            with ExitStack() as ctx:
                k.qr = k.sb(ctx, "qr", [P, 4, T])
                k.vs = k.sb(ctx, "vs", [P, 5, P])
                k.vw = k.sb(ctx, "vw", [P, 5, P])
                k.kc = k.sb(ctx, "kc", [P, DEC_BATCH, CH])
                k.vc = k.sb(ctx, "vc", [CH, DEC_BATCH, P])
                k.kcp = k.sb(ctx, "kcp", [P, 32])
                k.vcp = k.sb(ctx, "vcp", [32, P])
                compress_stage(k)
                nsa_prepare_stage(k)
                prompt_attention_stage(k)
                sample_attention_stage(k)
            k.zg = k.sb(mixing, "zg", [P, 2 * KD, T])
            with ExitStack() as ctx:
                h = [k.sb(ctx, name, [P, KD, T], F32R) for name in ("h_hi", "h_lo")]
                norm_stage(k, "attn_norm", *h)
                project_stage(k, d["w_zg"], 2 * KD, h, k.zg)
            with ExitStack() as ctx:
                m = [k.sb(ctx, name, [P, KD, T], F32R) for name in ("m_hi", "m_lo")]
                merge_stage(k, *m)
                project_stage(k, d["w_out"], KD, m, k.z[:, 8:16, :])
                add_stage(k, k.z[:, 8:16, :])
        k.clear_sems()
        k.g_dram = nc.dram_tensor("gate_matrix", (T // TB, P, N_KEYS * TB), F32).ap()
        with ExitStack() as ffn:
            h = [k.sb(ffn, name, [P, KD, T], F32R) for name in ("h_hi", "h_lo")]
            norm_stage(k, "ffn_norm", *h)
            with ExitStack() as ctx:
                picked = k.sb(ctx, "picked", [P, 3, T])
                q = k.sb(ctx, "q", [P, KD, T])
                project_stage(k, d["peer_wq"], KD, h, q)
                choose_stage(k, q, picked)
                gate_matrix_stage(k, picked)
            with ExitStack() as ctx:
                y = k.sb(ctx, "y", [P, KD, T])
                experts_stage(k, h, y)
                add_stage(k, y)
            norm_stage(k, "ple_norm", *h)
            embed_stage(k, h)



def _tiles(w):
    kk, n = w.shape
    return w.reshape(kk // P, P, n // P, P).transpose(2, 1, 0, 3).reshape(n // P, P, kk // P * P)


def _rows(w):
    c, t = w.shape
    return w.reshape(c // P, P, t).transpose(1, 0, 2).reshape(P, c // P * t)


def _constants():
    f = np.float32
    out = {}
    out["ones"] = np.ones((P, P), f)
    out["blocks"] = np.kron(np.eye(2), np.ones((HD, HD))).astype(f)
    out["ident"] = np.eye(P, dtype=f)
    keep = np.ones((P, T), f)
    keep[:, 0:SEQ:CH] = 0
    keep[:, SEQ::DEC_SEQ] = 0
    out["keep"] = keep
    t = np.arange(CH)
    masks = []
    for inner, outer in ((16, CH), (DEC_SEQ, DEC_SEQ)):
        near = t[:, None] // inner == t[None, :] // inner
        within = t[:, None] // outer == t[None, :] // outer
        lower = t[:, None] > t[None, :]
        masks += [-1.0 * (near & lower), -1.0 * (near & lower.T), -1.0 * (within & ~near & lower),
                  1.0 * (within & lower.T), 1.0 * (within & ~lower), -1.0 * (within & ~lower)]
    out["masks"] = np.stack(masks, 1).reshape(CH, 12 * CH).astype(f)
    out["seqmask"] = (t[:, None] // DEC_SEQ == np.arange(DEC_BATCH)[None, :]).astype(f)
    pos = np.concatenate([np.arange(SEQ), np.tile(PAST + np.arange(DEC_SEQ), DEC_BATCH)]).astype(f)
    half = HD // 2
    inv = np.power(f(10000.0), -np.arange(half, dtype=f) / f(half)).astype(f)
    ang = (pos[None, :] * inv[:, None]).astype(f).astype(np.float64)
    out["rope"] = np.concatenate([np.tile(np.cos(ang), (4, 1)), np.tile(np.sin(ang), (4, 1))], 1).astype(f)
    rot = np.zeros((P, P), f)
    for base in range(0, P, HD):
        for j in range(half):
            rot[base + half + j, base + j] = -1
            rot[base + j, base + half + j] = 1
    out["rot"] = rot
    q = np.arange(P)
    out["tri"] = np.where(q[:, None] >= q[None, :], 0, NEG).astype(f)
    n = np.arange(32)
    cm = [np.where((CMP_STRIDE * n[None, :] + 31 <= qt * P + q[:, None]) & (n[None, :] < 31), 0, NEG) for qt in range(4)]
    out["cmask"] = np.concatenate(cm, 1).astype(f)
    row = np.arange(P)
    rs, rkv, ri, rt = row // 64, row // 32 % 2, row // 8 % 4, row % 8
    col = np.arange(TS)
    out["newmask"] = np.concatenate([np.where((col[None, :] // 8 == 2 * g + rs[:, None]) & (col[None, :] % 8 <= rt[:, None]),
                                              0, NEG) for g in range(4)], 1).astype(f)
    out["winmask"] = np.where(np.arange(8)[None, :] <= rt[:, None], NEG, 0).astype(f)
    out["pick"] = np.concatenate([col[:, None] == (8 * (2 * g + rs) + rt)[None, :] for g in range(4)], 1).astype(f)
    out["headmask"] = (np.arange(NGATE)[None, :] // 3 == (4 * rkv + ri)[:, None]).astype(f)
    key = rs * 100 + rkv * 10 + rt
    out["same"] = (key[:, None] == key[None, :]).astype(f)
    out["iota14"] = np.tile(np.arange(1, 15, dtype=f), (P, 1))
    out["iota16"] = np.tile(np.arange(16, dtype=f), (P, 1))
    out["iota128"] = np.tile(np.arange(128, dtype=f), (P, 1))
    return out


def _lay_out(x_prompt, x_sample, cache_cmp_kv, cache_sel_kv, state_win_kv, state_wkv, state_shift, page_table,
             p_prompt, p_sample, attn_norm, w_in, rwkv_mu, rwkv_w0, rwkv_w_up, rwkv_a0, rwkv_a_up, rwkv_g_up,
             rwkv_k_k, rwkv_k_a, rwkv_r_k, rwkv_gn_w, rwkv_gn_b, w_rwkv_out, q_norm, k_norm, cmp_pe, cmp_w1,
             cmp_w2, w_nsa_out, w_out, ffn_norm, peer_wq, peer_keys, peer_u, peer_v, ple_norm, ple_w_gate, ple_w_in):
    d = _constants()
    n_phys = cache_cmp_kv.shape[1]
    d["x"] = _rows(np.concatenate([x_prompt[0], x_sample.reshape(TS, D_MODEL)], 0).T)
    d["p"] = _rows(np.concatenate([p_prompt[0, 0], p_sample[0].reshape(TS, PLE)], 0).T)
    params = dict(attn_norm=attn_norm[0], ffn_norm=ffn_norm[0], ple_norm=ple_norm[0], mu=rwkv_mu[0], w0=rwkv_w0[0],
                  a0=rwkv_a0[0], k_k=rwkv_k_k[0], k_a=rwkv_k_a[0], r_k=rwkv_r_k[0].reshape(-1), gn_w=rwkv_gn_w[0],
                  gn_b=rwkv_gn_b[0], q_norm=np.tile(q_norm[0], 2), k_norm=np.tile(k_norm[0], (1, 2)).reshape(-1))
    d["params"] = np.concatenate([params[n].reshape(-1, P).T for n in PARAMS], 1)
    order = np.concatenate([np.r_[i * HD:(i + 1) * HD, (4 + i) * HD:(5 + i) * HD] for i in range(4)])
    r0 = RCOLS * P
    kv_end = r0 + 512 + 6 * P
    w = w_in[0]
    d["w_in"] = _tiles(np.concatenate([w[:, :r0], w[:, r0:r0 + 512][:, order], w[:, r0 + 512:kv_end]], 1))
    d["w_zg"] = _tiles(w[:, kv_end + NGATE:])
    d["w_gates"] = _rows(w[:, kv_end:kv_end + NGATE])
    d["up"] = np.concatenate([np.concatenate([rwkv_w_up[0], rwkv_a_up[0]], 0), rwkv_g_up[0]], 1)
    d["shift"] = _rows(state_shift[0].T)
    d["states"] = state_wkv[0].transpose(3, 1, 0, 2).reshape(HD, -1)
    pages = cache_cmp_kv[0].reshape(n_phys, 8, 8, 2, 2, 2, HD)
    d["cmp_pages"] = pages.transpose(0, 3, 6, 2, 4, 5, 1).reshape(n_phys, P, 256)
    sel = cache_sel_kv[0].reshape(n_phys, PAGE, 2, P)
    d["sel_pages"] = np.concatenate([sel[:, :, 0].transpose(0, 2, 1), sel[:, :, 1]], 2)
    win = state_win_kv[0].reshape(DEC_BATCH // 2, 2, WINDOW, 2, P)
    d["win_k"] = win[:, :, :, 0].transpose(0, 3, 1, 2).reshape(4, P, 2 * WINDOW)
    d["win_v"] = win[:, :, :, 1].reshape(4, 2, 4, P, P).transpose(0, 3, 1, 2, 4).reshape(4, P, 2 * 4 * P)
    d["win_rows"] = state_win_kv[0][:, DEC_SEQ:].reshape(DEC_BATCH, -1)
    d["page_table"] = page_table.reshape(1, -1)
    d["cmp_w1"] = cmp_w1[0].reshape(2, 2, 8, 2, HD, CMP_HIDDEN).transpose(3, 4, 2, 0, 1, 5).reshape(P, -1)
    d["cmp_pe"] = cmp_pe[0].reshape(2, 2, 8, 2, HD).transpose(3, 4, 2, 0, 1).reshape(P, -1)
    d["cmp_w2"] = cmp_w2[0].reshape(2, 2, P, HD).transpose(2, 0, 1, 3).reshape(P, -1)
    d["w_merge"] = np.concatenate([_tiles(w_rwkv_out[0]), _tiles(w_nsa_out[0][order])], 2)
    d["w_out"] = _tiles(w_out[0])
    d["peer_wq"] = _tiles(peer_wq[0])
    d["keys"] = peer_keys[0].transpose(1, 3, 0, 2).reshape(P, -1)
    d["peer_u"] = peer_u[0].reshape(N_KEYS, P, KD, P).transpose(0, 3, 2, 1).reshape(N_KEYS, P, KD * P)
    d["peer_v"] = peer_v[0].reshape(N_KEYS, P, D_MODEL)
    d["w_ple"] = np.concatenate([_tiles(ple_w_gate[0]), _tiles(ple_w_in[0])], 2)
    return {n: np.ascontiguousarray(a) for n, a in d.items()}, n_phys


_OUTS = dict(out_y=(KD, P, T), out_kv=(P, 6 * T), out_win=(DEC_BATCH, (WINDOW - DEC_SEQ) * 2 * P),
             out_state=(HD, HEADS * HD), out_states=(HD, HEADS * DEC_BATCH * HD), out_shift=(P, RCOLS * 9))


def kernel(**inputs):
    import concourse.bacc as _bacc
    from concourse import mybir as _mybir
    from concourse.bass_utils import run_bass_kernel_spmd as _run

    arrays, n_phys = _lay_out(**{n: np.asarray(a) for n, a in inputs.items()})
    nc = _bacc.Bacc("TRN2", target_bir_lowering=False, num_devices=1)
    d = {n: nc.dram_tensor(f"in_{n}", a.shape, _mybir.dt.from_np(a.dtype), kind="ExternalInput").ap()
         for n, a in arrays.items()}
    for n, shape in _OUTS.items():
        d[n] = nc.dram_tensor(n, shape, F32, kind="ExternalOutput").ap()
    layer_program(nc, d, n_phys)
    r = _run(nc, [{f"in_{n}": a for n, a in arrays.items()}], core_ids=[0]).results[0]

    y = r["out_y"].reshape(D_MODEL, T).T
    kv = r["out_kv"].reshape(2, HD, 3, 2, T).transpose(2, 4, 3, 0, 1)
    prompt = [np.ascontiguousarray(kv[b, :SEQ])[None, None] for b in range(3)]
    new = [np.ascontiguousarray(kv[b, SEQ:]).reshape(1, DEC_BATCH, DEC_SEQ, 2, 2, HD) for b in range(3)]
    win = np.concatenate([r["out_win"].reshape(1, DEC_BATCH, WINDOW - DEC_SEQ, 2, 2, HD), new[2]], 2)
    state = r["out_state"].reshape(HD, HEADS, HD).transpose(1, 2, 0)[None, None]
    states = r["out_states"].reshape(HD, HEADS, DEC_BATCH, HD).transpose(2, 1, 3, 0)[None]
    shift = r["out_shift"].reshape(P, RCOLS, 9).transpose(2, 1, 0).reshape(9, RCOLS * P)
    out = (y[:SEQ][None], y[SEQ:].reshape(DEC_BATCH, DEC_SEQ, D_MODEL), prompt[0], new[0], prompt[1], new[1],
           prompt[2], win, state, states, shift[None, 0:1], shift[None, 1:])
    return tuple(np.ascontiguousarray(a) for a in out)
```

```python
from contextlib import ExitStack

import numpy as np

import concourse.bass as bass
from concourse import mybir

ALU = mybir.AluOpType
ACT = mybir.ActivationFunctionType
AX = mybir.AxisListType
F32 = mybir.dt.float32
F32R = mybir.dt.float32r
U32 = mybir.dt.uint32

P = 128
D_MODEL = 1024
KD = D_MODEL // P
SEQ = 512
DEC_BATCH = 8
DEC_SEQ = 8
TS = DEC_BATCH * DEC_SEQ
T = SEQ + TS
TH = T // 2
PAST = 1024
PAGE = 128
PAGES = PAST // PAGE
HD = 64
HEADS = 8
RCOLS = 14
ZQ = 14
ZK = 18
NZ = 24
NGATE = 24
CMP_STRIDE = 16
CMP_HIDDEN = 256
SEL_BLOCK = 64
WINDOW = 512
CH = 64
TB = 32
NCH = SEQ // CH
N_KEYS = 128
TOPK = 16
PLE = 256
EPS = 1e-6
GN_EPS = 64e-5
DECAY = float(np.exp(-0.5))
SCALE = HD ** -0.5
NEG = -1e30

PARAMS = {}
for _name, _n in (("attn_norm", KD), ("ffn_norm", KD), ("ple_norm", KD), ("mu", RCOLS), ("w0", 4), ("a0", 4),
                  ("k_k", 4), ("k_a", 4), ("r_k", 4), ("gn_w", 4), ("gn_b", 4), ("q_norm", 1), ("k_norm", 3)):
    PARAMS[_name] = (sum(n for _, n in PARAMS.values()), _n)
NPARAM = sum(n for _, n in PARAMS.values())


class Tiles:
    pass


class Chain:

    def __init__(self, eng, sem, base=0):
        self.eng, self.sem, self.base, self.n = eng, sem, base, 0

    def link(self, ins):
        self.n += 1
        ins.then_inc(self.sem, 1)
        self.eng.wait_ge(self.sem, self.base + self.n)


class Steps:

    def __init__(self, sem, names, base=0):
        self.sem, self.names, self.base = sem, names.split(), base

    def at(self, name, i=0):
        return i * len(self.names) + self.base + self.names.index(name) + 1

    def before(self, i):
        return i * len(self.names) + self.base


class Core:

    def __init__(self, nc):
        self.nc = nc
        self.n = 0
        self.used = []

    def sb(self, ctx, name, shape, dt=F32):
        self.n += 1
        return ctx.enter_context(self.nc.sbuf_tensor(f"{name}_{self.n}", shape, dt))

    def sems(self, ctx, *names):
        self.n += 1
        made = [ctx.enter_context(self.nc.semaphore(f"{n}_{self.n}")) for n in names]
        self.used += made
        return made

    def clear_sems(self):
        numbers = sorted({s.num for s in self.used})
        self.used = []
        with self.nc.Block() as block:
            @block.gpsimd
            def _(pool):
                at = 0
                while at < len(numbers):
                    end = at + 1
                    while end < len(numbers) and numbers[end] == numbers[end - 1] + 1:
                        end += 1
                    pool.sem_clear(range(numbers[at], numbers[end - 1] + 1))
                    at = end

    def par(self, name, i=0, lo=0, hi=P):
        at, n = PARAMS[name]
        return self.params[lo:hi, at + i:at + i + 1]

    def bank(self, b, n=512):
        return self.ps[:, b, 0:n]

    def pair(self, b):
        return self.ps[:, b:b + 2, 0:TH]


def halves(ap):
    return ap.rearrange("p (h t) -> p h t", h=2)


def load_stage(k):
    nc = k.nc
    with ExitStack() as ctx:
        loaded, = k.sems(ctx, "loaded")
        pairs = [(k.x, k.d["x"]), (k.params, k.d["params"]), (k.ones, k.d["ones"]), (k.blocks, k.d["blocks"]),
                 (k.ident, k.d["ident"])]
        block = ctx.enter_context(nc.Block())

        @block.sync
        def _(sp):
            for dst, src in pairs:
                sp.dma_start(dst[:] if dst is not k.x else dst.rearrange("p c t -> p (c t)"), src).then_inc(loaded, 16)
            sp.wait_ge(loaded, 16 * len(pairs))


def norm_stage(k, gain, hi, lo):
    nc = k.nc
    with ExitStack() as ctx:
        sq = k.sb(ctx, "sq", [P, KD, T])
        rs = k.sb(ctx, "rs", [P, T])
        squared, summed, mean, rooted, chain, normed, rounded = k.sems(ctx, "squared", "summed", "mean", "rooted", "chain",
                                                                       "normed", "rounded")
        block = ctx.enter_context(nc.Block())

        @block.scalar
        def _(act):
            for c in range(KD):
                nc.scalar.activation(sq[:, c, :], k.x[:, c, :], ACT.Square).then_inc(squared, 1)
            act.wait_ge(mean, 1)
            nc.scalar.activation(rs[:], rs[:], ACT.Sqrt).then_inc(rooted, 1)
            for c in range(KD):
                act.wait_ge(normed, c + 1)
                nc.scalar.activation(hi[:, c, :], sq[:, c, :], ACT.Copy).then_inc(rounded, 1)

        @block.tensor
        def _(pe):
            for c in range(KD):
                pe.wait_ge(squared, c + 1)
                for h in range(2):
                    mm = nc.tensor.matmul(k.bank(h, TH), k.ones[:], sq[:, c, h * TH:(h + 1) * TH],
                                          start=c == 0, stop=c == KD - 1)
            mm.then_inc(summed, 1)

        @block.vector
        def _(dve):
            ch = Chain(dve, chain)
            dve.wait_ge(summed, 1)
            nc.vector.tensor_scalar(halves(rs[:]), k.pair(0), 1.0 / D_MODEL, EPS, ALU.mult, ALU.add).then_inc(mean, 1)
            dve.wait_ge(rooted, 1)
            ch.link(nc.vector.reciprocal(rs[:], rs[:]))
            for c in range(KD):
                nc.vector.scalar_tensor_tensor(out=sq[:, c, :], in0=k.x[:, c, :], scalar=k.par(gain, c),
                                               in1=rs[:], op0=ALU.mult, op1=ALU.mult).then_inc(normed, 1)
            for c in range(KD):
                dve.wait_ge(rounded, c + 1)
                last = nc.vector.tensor_tensor(lo[:, c, :], sq[:, c, :], hi[:, c, :].bitcast(F32), ALU.subtract)
            ch.link(last)


def three_passes(w_hi, w_lo, r_hi, r_lo):
    return (w_hi, r_hi), (w_hi, r_lo), (w_lo, r_hi)


def project_stage(k, w, ntiles, rhs, dst, gates=None):
    nc = k.nc
    ring = 4
    r_hi, r_lo = rhs
    with ExitStack() as ctx:
        wt = k.sb(ctx, "wt", [P, ring, KD, P])
        w_hi = k.sb(ctx, "w_hi", [P, 2, KD, P], F32R)
        w_lo = k.sb(ctx, "w_lo", [P, 2, KD, P], F32R)
        arrived = k.sems(ctx, *[f"arrived{b}" for b in range(ring)])
        rounded, parted, multiplied, taken, gate_w, gate_mm = k.sems(ctx, "rounded", "parted", "multiplied", "taken",
                                                                     "gate_w", "gate_mm")
        block = ctx.enter_context(nc.Block())

        @block.sync
        def _(sp):
            if gates is not None:
                sp.dma_start(gates[1].rearrange("p c n -> p (c n)"), gates[0]).then_inc(gate_w, 16)
            with sp.Fori(0, ntiles // ring) as i:
                for b in range(ring):
                    sp.wait_ge(parted, i * ring + b + 1)
                    sp.dma_start(wt[:, b].rearrange("p c n -> p (c n)"), w[i * ring + b]).then_inc(arrived[b], 16)

        @block.vector
        def _(dve):
            dve.sem_inc(parted, ring)
            with dve.Fori(0, ntiles // ring) as i:
                for b in range(ring):
                    dve.wait_ge(arrived[b], i * 16 + 16)
                    dve.wait_ge(multiplied, i * ring + b + 1)
                    nc.vector.tensor_copy(w_hi[:, b % 2], wt[:, b]).then_inc(rounded, 1)
                    dve.wait_ge(rounded, i * ring + b + 1)
                    nc.vector.tensor_tensor(w_lo[:, b % 2], wt[:, b], w_hi[:, b % 2].bitcast(F32),
                                            ALU.subtract).then_inc(parted, 1)

        @block.tensor
        def _(pe):
            pe.sem_inc(multiplied, 2)
            with pe.Fori(0, ntiles // ring) as i:
                for b in range(ring):
                    pe.wait_ge(parted, i * ring + ring + b + 1)
                    pe.wait_ge(taken, i * ring + b + 1)
                    for c in range(KD):
                        for n, (lhs, r) in enumerate(three_passes(w_hi[:, b % 2, c, :], w_lo[:, b % 2, c, :], r_hi, r_lo)):
                            for h in range(2):
                                mm = nc.tensor.matmul(k.bank(2 * b + h, TH), lhs, r[:, c, h * TH:(h + 1) * TH],
                                                      start=c == 0 and n == 0, stop=c == KD - 1 and n == 2)
                    mm.then_inc(multiplied, 1)
            if gates is not None:
                pe.wait_ge(gate_w, 16)
                pe.wait_ge(taken, ntiles + ring)
                for tt in range(5):
                    n = min(P, T - tt * P)
                    for c in range(KD):
                        for r in (r_hi, r_lo):
                            mm = nc.tensor.matmul(k.ps[0:n, 0, tt * NGATE:(tt + 1) * NGATE],
                                                  r[:, c, tt * P:tt * P + n].bitcast(F32), gates[1][:, c, :],
                                                  start=c == 0 and r is r_hi, stop=c == KD - 1 and r is r_lo)
                mm.then_inc(gate_mm, 1)

        @block.scalar
        def _(act):
            act.sem_inc(taken, ring)
            with act.Fori(0, ntiles // ring) as i:
                for b in range(ring):
                    act.wait_ge(multiplied, i * ring + b + 3)
                    out = dst[:, bass.ds(i * 4 + b, 1), :].rearrange("p o (h t) -> p (o h) t", h=2)
                    nc.scalar.activation(out, k.pair(2 * b), ACT.Copy).then_inc(taken, 1)
            if gates is not None:
                act.wait_ge(gate_mm, 1)
                nc.scalar.activation(gates[2][:, 0:4, :].rearrange("p a n -> p (a n)"), k.ps[:, 0, 0:4 * NGATE],
                                     ACT.Sigmoid)
                nc.scalar.activation(gates[2][0:TS, 4, :], k.ps[0:TS, 0, 4 * NGATE:5 * NGATE], ACT.Sigmoid)


def rwkv_prepare_stage(k):
    nc = k.nc
    Z, r = k.z, k.r
    with ExitStack() as ctx:
        xs = r.xs
        last9 = k.sb(ctx, "last9", [P, RCOLS, 9])
        prev = k.sb(ctx, "prev", [P, RCOLS, DEC_BATCH])
        up = k.sb(ctx, "up", [P, 2, 512])
        keep = k.sb(ctx, "keep", [P, T])
        V = Steps(None, "last shifted_low shifted keys2 cum a_used normed prods bonus done")
        S = Steps(None, "low sw aa gg rooted decays")
        E = Steps(None, "w a g keysum bonussum")
        v_at, s_at, e_at, loaded, stored, chain, schain = k.sems(ctx, "dve_step", "act_step", "pe_step", "loaded",
                                                                "stored", "chain", "schain")
        sw, cum, tmp = Z[:, 0:4, :], Z[:, 4:8, :], Z[:, 8:12, :]
        kk = r.kt
        block = ctx.enter_context(nc.Block())

        @block.sync
        def _(sp):
            sp.dma_start(prev.rearrange("p c s -> p (c s)"), k.d["shift"]).then_inc(loaded, 16)
            sp.dma_start(up.rearrange("p c s -> p (c s)"), k.d["up"]).then_inc(loaded, 16)
            sp.dma_start(keep[:], k.d["keep"]).then_inc(loaded, 16)
            sp.wait_ge(v_at, V.at("last"))
            sp.dma_start(k.d["out_shift"], last9.rearrange("p c s -> p (c s)")).then_inc(stored, 16)
            sp.wait_ge(stored, 16)

        @block.vector
        def _(dve):
            ch = Chain(dve, chain)
            nc.vector.tensor_copy(last9[:], Z[:, 0:RCOLS, SEQ - 1:T:DEC_SEQ]).then_inc(v_at, 1)
            nc.vector.tensor_scalar(xs[:, :, 0:1], Z[:, 0:RCOLS, 0:1], -1.0, None, ALU.mult)
            ch.link(nc.vector.tensor_tensor(xs[:, :, 1:T], Z[:, 0:RCOLS, 0:T - 1], Z[:, 0:RCOLS, 1:T], ALU.subtract))
            dve.wait_ge(loaded, 48)
            ch.link(nc.vector.tensor_tensor(xs[:, :, SEQ:T:DEC_SEQ], prev[:], Z[:, 0:RCOLS, SEQ:T:DEC_SEQ], ALU.subtract))
            for n in (12, 13, *range(12)):
                ins = nc.vector.scalar_tensor_tensor(out=xs[:, n, :], in0=xs[:, n, :], scalar=k.par("mu", n),
                                                     in1=Z[:, n, :], op0=ALU.mult, op1=ALU.add)
                if n == 13:
                    ins.then_inc(v_at, 1)
            ins.then_inc(v_at, 1)
            dve.wait_ge(v_at, V.at("shifted"))
            for n in range(4):
                last = nc.vector.tensor_scalar(kk[:, n, :], xs[:, 4 + n, :], k.par("k_k", n), None, ALU.mult)
            ch.link(last)
            nc.vector.tensor_tensor(tmp, kk[:], kk[:], ALU.mult).then_inc(v_at, 1)
            dve.wait_ge(s_at, S.at("sw"))
            for n in range(4):
                last = nc.vector.tensor_tensor_scan(cum[:, n, :], keep[:], sw[:, n, :], 0.0, ALU.mult, ALU.add)
            ch.link(last)
            nc.vector.tensor_tensor(sw, cum, sw, ALU.subtract).then_inc(v_at, 1)
            dve.wait_ge(s_at, S.at("aa"))
            for n in range(4):
                last = nc.vector.tensor_scalar(r.bonus[:, n, :], r.bt[:, n, :], -1.0, k.par("k_a", n), ALU.add, ALU.mult)
            ch.link(last)
            nc.vector.scalar_tensor_tensor(out=r.ht, in0=r.bonus[:], scalar=1.0, in1=xs[:, 4:8, :],
                                           op0=ALU.add, op1=ALU.mult).then_inc(v_at, 1)
            dve.wait_ge(s_at, S.at("rooted"))
            ch.link(nc.vector.tensor_scalar(tmp, tmp, 1e-12, None, ALU.max))
            ch.link(nc.vector.reciprocal(tmp, tmp))
            ch.link(nc.vector.tensor_tensor(kk[:], kk[:], tmp, ALU.mult))
            nc.vector.tensor_tensor(r.bt[:], r.bt[:], kk[:], ALU.mult).then_inc(v_at, 1)
            dve.wait_ge(v_at, V.at("normed"))
            for n in range(4):
                last = nc.vector.scalar_tensor_tensor(out=tmp[:, n, :], in0=xs[:, n, :], scalar=k.par("r_k", n),
                                                      in1=r.ht[:, n, :], op0=ALU.mult, op1=ALU.mult)
            last.then_inc(v_at, 1)
            dve.wait_ge(e_at, E.at("bonussum"))
            for n in range(4):
                last = nc.vector.tensor_tensor(halves(r.bonus[:, n, :]), k.pair(2 * n), halves(xs[:, 8 + n, :]), ALU.mult)
            last.then_inc(v_at, 1)
            dve.wait_ge(s_at, S.at("decays"))
            nc.vector.tensor_copy(r.ends[:, :, 0:NCH], tmp[:, :, CH - 1:SEQ:CH])
            nc.vector.tensor_copy(r.ends[:, :, NCH:], tmp[:, :, SEQ + DEC_SEQ - 1:T:DEC_SEQ])
            nc.vector.tensor_tensor(r.rt, r.rt, tmp, ALU.mult)
            nc.vector.tensor_tensor(kk[:], kk[:], sw, ALU.mult)
            nc.vector.tensor_tensor(r.bt[:], r.bt[:], cum, ALU.mult)
            nc.vector.tensor_tensor(r.ht, r.ht, cum, ALU.mult).then_inc(v_at, 1)
            dve.wait_ge(v_at, V.at("done"))

        @block.scalar
        def _(act):
            act.wait_ge(v_at, V.at("shifted_low"))
            nc.scalar.activation(xs[0:64, 12, :], xs[0:64, 12, :], ACT.Tanh)
            nc.scalar.activation(xs[:, 13, :], xs[:, 13, :], ACT.Sigmoid).then_inc(s_at, 1)
            act.wait_ge(v_at, V.at("shifted"))
            for name, dst, bias in (("w", sw, "w0"), ("a", r.bt, "a0"), ("g", r.g, None)):
                act.wait_ge(e_at, E.at(name))
                for n in range(4):
                    if bias:
                        last = nc.scalar.activation(halves(dst[:, n, :]), k.pair(2 * n), ACT.Sigmoid, bias=k.par(bias, n))
                    else:
                        last = nc.scalar.activation(halves(dst[:, n, :]), k.pair(2 * n), ACT.Copy)
                last.then_inc(s_at, 1)
            act.wait_ge(e_at, E.at("keysum"))
            for n in range(4):
                last = nc.scalar.activation(halves(tmp[:, n, :]), k.pair(2 * n), ACT.Sqrt)
            last.then_inc(s_at, 1)
            act.wait_ge(e_at, E.at("bonussum"))
            nc.scalar.activation(tmp, cum, ACT.Exp, scale=-DECAY).then_inc(schain, 1)
            nc.scalar.activation(sw, sw, ACT.Exp, scale=-DECAY)
            act.wait_ge(schain, 1)
            nc.scalar.activation(cum, cum, ACT.Exp, scale=DECAY).then_inc(s_at, 1)

        @block.tensor
        def _(pe):
            pe.wait_ge(loaded, 48)
            pe.wait_ge(s_at, S.at("low"))
            for name, lhs, rhs in (("w", up[0:64, 0], xs[0:64, 12, :]), ("a", up[64:128, 0], xs[64:128, 12, :]),
                                   ("g", up[:, 1], xs[:, 13, :])):
                if name != "w":
                    pe.wait_ge(s_at, S.at({"a": "sw", "g": "aa"}[name]))
                for n in range(4):
                    for h in range(2):
                        mm = nc.tensor.matmul(k.bank(2 * n + h, TH), lhs[:, n * P:(n + 1) * P],
                                              rhs[:, h * TH:(h + 1) * TH], start=True, stop=True)
                mm.then_inc(e_at, 1)
            for name, ready, freed in (("keysum", "keys2", "gg"), ("bonussum", "prods", "rooted")):
                pe.wait_ge(v_at, V.at(ready))
                pe.wait_ge(s_at, S.at(freed))
                for n in range(4):
                    for h in range(2):
                        mm = nc.tensor.matmul(k.bank(2 * n + h, TH), k.blocks[:], tmp[:, n, h * TH:(h + 1) * TH],
                                              start=True, stop=True)
                mm.then_inc(e_at, 1)


def accumulate(nc, out, *pairs):
    for m in range(out.shape[1]):
        for n, (lhs, rhs) in enumerate(pairs):
            for half in range(2):
                part = slice(half * HD, half * HD + HD)
                mm = nc.tensor.matmul(out[part, m, :], lhs[part, m, :], rhs[part, m, :], start=n == 0,
                                      stop=n == len(pairs) - 1)
    return mm


def accumulate_open(nc, out, lhs, rhs, first=False, last=False):
    blocks = out.shape[1]
    for m in range(blocks):
        for half in range(2):
            part = slice(half * HD, half * HD + HD)
            mm = nc.tensor.matmul(out[part, m, :], lhs[part, m, :], rhs[part, m, :], start=first and m == 0,
                                  stop=last and m == blocks - 1)
    return mm


def chunk_inverse(k, c, t0, i, eng, which, sample):
    nc = k.nc
    mask = lambda m: c.masks[:, 6 * sample + m:6 * sample + m + 1, :].broadcast_to([P, c.blocks, CH])
    product = lambda b, lhs, rhs: accumulate(nc, c.bank(b), (lhs, rhs))
    v = lambda name: c.wait(eng, which, c.V, c.V.at(name, i))
    s = lambda name: c.wait(eng, which, c.S, c.S.at(name, i))
    e = lambda name: c.wait(eng, which, c.E, c.E.at(name, i))
    power = lambda j: (c.n2, c.n2t) if j % 2 else (c.n, c.nt)

    if which == "tensor":
        v("copied")
        s("copied")
        product(0, c.k0, c.b0)
        product(1, c.b0, c.k0)
        product(2, c.h0, c.k0)
        product(3, c.h0, c.r0)
        product(4, c.b0, c.r0).then_inc(c.E.sem, 1)
        identity = c.ident2.rearrange("p (o t) -> p o t", o=1).broadcast_to([P, c.blocks, CH])
        product(5, c.v0, identity)
        product(6, c.h0, identity)
        product(7, c.b0, identity).then_inc(c.E.sem, 1)
        v("masked")
        product(0, c.nt, c.n)
        product(1, c.n, c.nt).then_inc(c.E.sem, 1)
        for j in range(1, 4):
            n, nt = power(j)
            v(f"square{j}")
            s(f"square{j}")
            if j < 3:
                product(0, nt, n)
                product(1, n, nt).then_inc(c.E.sem, 1)
            v(f"times{j}")
            product(2, nt, c.t)
            product(3, n, c.tt).then_inc(c.E.sem, 1)
        v("inverse")
        product(0, c.below, c.tt)
        product(1, c.tt, c.below).then_inc(c.E.sem, 1)
        v("q")
        s("q")
        product(2, c.qt, c.q)
        product(3, c.t, c.q)
        product(4, c.q, c.t).then_inc(c.E.sem, 1)
        v("r")
        s("q2")
        product(5, c.rt, c.q2).then_inc(c.E.sem, 1)

    if which == "vector":
        for dst, src in ((c.k0, k.r.kt), (c.b0, k.r.bt), (c.h0, k.r.ht), (c.r0, k.r.rt)):
            last = nc.vector.tensor_copy(c.chunks(dst), c.source(src, t0))
        last.then_inc(c.V.sem, 1)
        e("grams")
        nc.vector.tensor_tensor(c.n, c.bank(0), mask(0), ALU.mult)
        nc.vector.tensor_tensor(c.nt, c.bank(1), mask(1), ALU.mult)
        nc.vector.tensor_tensor(c.below, c.bank(0), mask(2), ALU.mult).then_inc(c.V.sem, 1)
        v("masked")
        ident = c.ident2.rearrange("p (o t) -> p o t", o=1).broadcast_to([P, c.blocks, CH])
        nc.vector.tensor_tensor(c.t, c.n, ident, ALU.add)
        nc.vector.tensor_tensor(c.tt, c.nt, ident, ALU.add)
        for j in range(1, 4):
            e(f"square{j}")
            nc.vector.tensor_copy(power(j)[0], c.bank(0)).then_inc(c.V.sem, 1)
            if j == 1:
                nc.vector.tensor_tensor(c.ak, c.bank(2), mask(3), ALU.mult)
                nc.vector.tensor_tensor(c.rk, c.bank(3), mask(4), ALU.mult)
                nc.vector.tensor_tensor(c.rb, c.bank(4), mask(5), ALU.mult).then_inc(c.V.sem, 1)
            else:
                e(f"prods{j - 1}")
                v(f"times{j - 1}")
                nc.vector.tensor_tensor(c.t, c.bank(2), c.t, ALU.add)
                nc.vector.tensor_tensor(c.tt, c.bank(3), c.tt, ALU.add).then_inc(c.V.sem, 1)
        e("prods3")
        v("times3")
        nc.vector.tensor_tensor(c.t, c.bank(2), c.t, ALU.add)
        nc.vector.tensor_tensor(c.tt, c.bank(3), c.tt, ALU.add).then_inc(c.V.sem, 1)
        e("q")
        nc.vector.tensor_copy(c.q, c.bank(0)).then_inc(c.V.sem, 1)
        e("q2")
        v("inverse")
        nc.vector.tensor_tensor(c.rr, c.bank(3), c.tt, ALU.add)
        nc.vector.tensor_tensor(c.rt, c.bank(4), c.t, ALU.add).then_inc(c.V.sem, 1)
        e("inverse")
        v("r")
        nc.vector.tensor_tensor(c.ti, c.bank(5), c.rr, ALU.add).then_inc(c.V.sem, 1)

    if which == "scalar":
        if not sample:
            c.wait(eng, which, c.V, c.V.before(i))
        nc.scalar.activation(c.chunks(c.v0), c.source(k.r.vt, t0), ACT.Copy).then_inc(c.S.sem, 1)
        e("turned")
        nc.scalar.activation(c.v1, c.bank(5), ACT.Copy)
        nc.scalar.activation(c.h1, c.bank(6), ACT.Copy)
        nc.scalar.activation(c.b1, c.bank(7), ACT.Copy, scale=-1.0)
        for j in range(1, 4):
            e(f"square{j}")
            nc.scalar.activation(power(j)[1], c.bank(1), ACT.Copy).then_inc(c.S.sem, 1)
        e("q")
        nc.scalar.activation(c.qt, c.bank(1), ACT.Copy).then_inc(c.S.sem, 1)
        e("q2")
        nc.scalar.activation(c.q2, c.bank(2), ACT.Copy).then_inc(c.S.sem, 1)


def prompt_states(k, c, t0, i, eng, which):
    nc = k.nc
    v = lambda name: c.wait(eng, which, c.V, c.V.at(name, i))
    e = lambda name: c.wait(eng, which, c.E, c.E.at(name, i))
    banks = [[c.bank(b)[:, 0:4, :] for b in four] for four in ((7, 6, 0, 1), (2, 3, 4, 5))]
    part_of = lambda tile, j: tile[:, 4 * j:4 * j + 4, :]

    def early(j):
        x, _, out, new = banks[j]
        accumulate_open(nc, x, part_of(c.ak, j), part_of(c.v1, j), first=True)
        accumulate_open(nc, out, part_of(c.v1, j), part_of(c.rk, j), first=True)
        accumulate_open(nc, new, part_of(c.h1, j), part_of(c.v1, j), first=True)

    if which == "tensor":
        early(0)
        v("inverse_done")
        for j in range(2):
            x, u, out, new = banks[j]
            if j:
                v("state0")
            accumulate_open(nc, x, part_of(c.k0, j), c.state, last=True).then_inc(c.E.sem, 1)
            accumulate_open(nc, out, c.state, part_of(c.r0, j))
            accumulate_open(nc, new, c.identity4, c.state)
            if j == 0:
                early(1)
            v(f"x{j}")
            accumulate(nc, u, (part_of(c.ti, j), c.x)).then_inc(c.E.sem, 1)
            v(f"u{j}")
            accumulate_open(nc, new, part_of(c.b1, j), c.u, last=True).then_inc(c.E.sem, 1)
            accumulate_open(nc, out, c.u, part_of(c.rb, j), last=True).then_inc(c.E.sem, 1)

    if which == "vector":
        for j in range(2):
            x, u, out, new = banks[j]
            e(f"x{j}")
            nc.vector.tensor_copy(c.x, x).then_inc(c.V.sem, 1)
            e(f"u{j}")
            nc.vector.tensor_copy(c.u, u).then_inc(c.V.sem, 1)
            e(f"new{j}")
            nc.vector.tensor_tensor(c.state, new, k.r.ends[:, :, bass.ds(2 * i + j, 1)].broadcast_to([P, 4, HD]),
                                    ALU.mult).then_inc(c.V.sem, 1)

    if which == "scalar":
        for j in range(2):
            e(f"out{j}")
            nc.scalar.activation(k.r.o[:, :, bass.ds(t0 + j * CH, CH)], banks[j][2], ACT.Copy)


def sample_states(k, c, eng, which):
    nc = k.nc
    v = lambda name: c.wait(eng, which, c.V, c.V.at(name))
    s = lambda name: c.wait(eng, which, c.S, c.S.at(name))
    e = lambda name: c.wait(eng, which, c.E, c.E.at(name))
    parts = [slice(0, HD), slice(HD, P)]
    cols = [slice(n * DEC_SEQ, (n + 1) * DEC_SEQ) for n in range(DEC_BATCH)]
    flat = lambda x: x.rearrange("p n v -> p (n v)")

    if which == "tensor":
        for m in range(4):
            for n in range(DEC_BATCH):
                for part in parts:
                    mm = nc.tensor.matmul(c.bank(6)[part, m, cols[n]], c.states[part, m, n, :], c.k0[part, m, cols[n]],
                                          start=True, stop=True)
        mm.then_inc(c.E.sem, 1)
        s("seen")
        accumulate(nc, c.bank(7), (c.seen, c.identity4), (c.ak, c.v1)).then_inc(c.E.sem, 1)
        v("inverse_done")
        v("x0")
        accumulate(nc, c.bank(6), (c.ti, c.x)).then_inc(c.E.sem, 1)
        v("u0")
        for m in range(4):
            for part in parts:
                nc.tensor.matmul(c.bank(0)[part, m, :], c.v1[part, m, :], c.rk[part, m, :], start=True, stop=False)
            for n in range(DEC_BATCH):
                for part in parts:
                    nc.tensor.matmul(c.bank(0)[part, m, cols[n]], c.states[part, m, n, :], c.r0[part, m, cols[n]],
                                     start=False, stop=False)
            for part in parts:
                mm = nc.tensor.matmul(c.bank(0)[part, m, :], c.u[part, m, :], c.rb[part, m, :], start=False, stop=True)
        mm.then_inc(c.E.sem, 1)
        for m in range(4):
            eng.wait_ge(c.spread, m + 1)
            if m >= 2:
                eng.wait_ge(c.taken, m - 1)
            for n, (lhs, rhs) in enumerate(((k.ident, c.states[:, m]), (c.h1[:, m, :], c.vm[:, m % 2]),
                                            (c.b1[:, m, :], c.um[:, m % 2]))):
                for part in parts:
                    left = lhs[part, part] if n == 0 else lhs[part, :]
                    mm = nc.tensor.matmul(k.ps[part, 1 + m % 2, :], left, flat(rhs)[part, :], start=n == 0, stop=n == 2)
            mm.then_inc(c.updated, 1)

    if which == "vector":
        e("x0")
        nc.vector.tensor_copy(c.x, c.bank(7)).then_inc(c.V.sem, 1)
        e("u0")
        nc.vector.tensor_copy(c.u, c.bank(6)).then_inc(c.V.sem, 1)
        v("u0")
        own = c.seqmask.rearrange("p (n o) -> p n o", o=1).broadcast_to([P, DEC_BATCH, HD])

        def take_state(m):
            eng.wait_ge(c.updated, m + 1)
            decay = k.r.ends[:, m, NCH:].rearrange("p (n o) -> p n o", o=1).broadcast_to([P, DEC_BATCH, HD])
            nc.vector.tensor_tensor(c.states[:, m], k.ps[:, 1 + m % 2, :].rearrange("p (n v) -> p n v", n=DEC_BATCH),
                                    decay, ALU.mult).then_inc(c.taken, 1)

        for m in range(4):
            if m >= 2:
                eng.wait_ge(c.updated, m - 1)
            rep = lambda x: x[:, m:m + 1, :].broadcast_to([P, DEC_BATCH, HD])
            nc.vector.tensor_tensor(c.vm[:, m % 2], rep(c.v1), own, ALU.mult)
            nc.vector.tensor_tensor(c.um[:, m % 2], rep(c.u), own, ALU.mult).then_inc(c.spread, 1)
            if m >= 1:
                take_state(m - 1)
        take_state(3)

    if which == "scalar":
        e("seen")
        nc.scalar.activation(c.seen, c.bank(6), ACT.Copy).then_inc(c.S.sem, 1)
        e("out0")
        nc.scalar.activation(k.r.o[:, :, SEQ:T], c.bank(0), ACT.Copy)


def rwkv_chunks_stage(k, sample):
    nc = k.nc
    with ExitStack() as ctx:
        spare = k.z[:, 0:4, :].rearrange("p a t -> p (a t)")
        c = Tiles()
        c.blocks = 4 if sample else 8
        c.bank = lambda b: k.bank(b, c.blocks * CH).rearrange("p (m t) -> p m t", t=CH)
        names = "r0 k0 b0 h0 v0 n nt n2 n2t t tt below ak rk rb v1 h1 b1 q qt q2 rr rt ti"
        (c.r0, c.k0, c.b0, c.h0, c.v0, c.n, c.nt, c.n2, c.n2t, c.t, c.tt, c.below, c.ak, c.rk, c.rb, c.v1, c.h1, c.b1,
         c.q, c.qt, c.q2, c.rr, c.rt, c.ti) = [
            k.sb(ctx, name, [P, c.blocks, CH])[:] if m >= 4 else
            spare[:, m * 512:m * 512 + c.blocks * CH].rearrange("p (h t) -> p h t", t=CH)
            for m, name in enumerate(names.split())]
        c.x, c.u, c.state = (k.sb(ctx, name, [P, 4, CH])[:] for name in ("x", "u", "state"))
        c.masks = k.sb(ctx, "masks", [P, 12, CH])
        c.ident2 = k.sb(ctx, "ident2", [P, CH])[:]
        c.identity4 = c.ident2.rearrange("p (o t) -> p o t", o=1).broadcast_to([P, 4, CH])
        c.chunks = lambda dst: dst.rearrange("p (c n) t -> p n c t", n=4)
        c.source = lambda src, t0: src[:, :, bass.ds(t0, c.blocks // 4 * CH)].rearrange("p n (c t) -> p n c t", t=CH)
        v_at, s_at, e_at, loaded, stored, c.passed = k.sems(ctx, "dve_step", "act_step", "pe_step", "loaded", "stored",
                                                            "passed")
        c.V = Steps(v_at, "copied masked square1 times1 square2 times2 square3 times3 inverse q r inverse_done x0 u0"
                    + ("" if sample else " state0 x1 u1 state1"), base=1)
        c.S = Steps(s_at, "copied square1 square2 square3 q q2" + (" seen" if sample else ""))
        c.E = Steps(e_at, "grams turned square1 square2 prods1 square3 prods2 prods3 q q2 inverse"
                    + (" seen x0 u0 out0" if sample else " x0 u0 new0 out0 x1 u1 new1 out1"))

        def wait(eng, which, steps, value):
            eng.wait_ge(steps.sem, value)
            if which == "tensor":
                eng.sem_inc(c.passed, 1)

        c.wait = wait
        if sample:
            c.states = k.sb(ctx, "states", [P, 4, DEC_BATCH, HD])
            more = k.z[:, 8:12, :].rearrange("p a t -> p (a t)")
            c.seen = more[:, 2048:2304].rearrange("p (m t) -> p m t", t=CH)
            c.vm, c.um = (more[:, m * 1024:(m + 1) * 1024].rearrange("p (b n v) -> p b n v", b=2, v=HD) for m in range(2))
            c.seqmask = k.sb(ctx, "seqmask", [P, DEC_BATCH])
            c.spread, c.updated, c.taken = k.sems(ctx, "spread", "updated", "taken")
        n_loads = 4 if sample else 2
        block = ctx.enter_context(nc.Block())

        def rounds(eng, which):
            if sample:
                chunk_inverse(k, c, SEQ, 0, eng, which, 1)
                sample_states(k, c, eng, which)
            else:
                with eng.Fori(0, NCH // 2) as i:
                    chunk_inverse(k, c, i * (2 * CH), i, eng, which, 0)
                    prompt_states(k, c, i * (2 * CH), i, eng, which)

        @block.sync
        def _(sp):
            sp.dma_start(c.masks.rearrange("p m t -> p (m t)"), k.d["masks"]).then_inc(loaded, 16)
            sp.dma_start(c.ident2, k.d["ident2"]).then_inc(loaded, 16)
            if sample:
                sp.dma_start(c.states.rearrange("p m n v -> p (m n v)"), k.d["states"]).then_inc(loaded, 16)
                sp.dma_start(c.seqmask[:], k.d["seqmask"]).then_inc(loaded, 16)
                sp.wait_ge(c.taken, 4)
                sp.dma_start(k.d["out_states"], c.states.rearrange("p m n v -> p (m n v)")).then_inc(stored, 16)
            else:
                sp.wait_ge(v_at, c.V.before(NCH // 2))
                sp.dma_start(k.d["out_state"], c.state.rearrange("p m v -> p (m v)")).then_inc(stored, 16)
            sp.wait_ge(stored, 16)

        @block.tensor
        def _(pe):
            pe.wait_ge(loaded, 16 * n_loads)
            rounds(pe, "tensor")

        @block.vector
        def _(dve):
            nc.vector.memset(c.state, 0.0).then_inc(v_at, 1)
            dve.wait_ge(loaded, 16 * n_loads)
            dve.wait_ge(v_at, 1)
            rounds(dve, "vector")

        @block.scalar
        def _(act):
            rounds(act, "scalar")


def rwkv_finish_stage(k):
    nc = k.nc
    o, r = k.r.o, k.r
    with ExitStack() as ctx:
        sq = k.sb(ctx, "sq", [P, 4, T])
        V = Steps(None, "centred mean")
        v_at, squared, rooted, summed, chain = k.sems(ctx, "dve_step", "squared", "rooted", "summed", "chain")
        block = ctx.enter_context(nc.Block())

        @block.tensor
        def _(pe):
            for src, ready in ((o, None), (sq, squared)):
                if ready is not None:
                    pe.wait_ge(ready, 1)
                for n in range(4):
                    for h in range(2):
                        mm = nc.tensor.matmul(k.bank(2 * n + h, TH), k.blocks[:], src[:, n, h * TH:(h + 1) * TH],
                                              start=True, stop=True)
                mm.then_inc(summed, 1)

        @block.vector
        def _(dve):
            ch = Chain(dve, chain)
            dve.wait_ge(summed, 1)
            for n in range(4):
                last = nc.vector.scalar_tensor_tensor(out=halves(o[:, n, :]), in0=k.pair(2 * n), scalar=-1.0 / HD,
                                                      in1=halves(o[:, n, :]), op0=ALU.mult, op1=ALU.add)
            last.then_inc(v_at, 1)
            dve.wait_ge(summed, 2)
            for n in range(4):
                last = nc.vector.tensor_scalar(halves(sq[:, n, :]), k.pair(2 * n), 1.0 / HD, GN_EPS, ALU.mult, ALU.add)
            last.then_inc(v_at, 1)
            dve.wait_ge(rooted, 1)
            ch.link(nc.vector.reciprocal(sq[:], sq[:]))
            ch.link(nc.vector.tensor_tensor(o[:], o[:], sq[:], ALU.mult))
            for n in range(4):
                last = nc.vector.tensor_scalar(o[:, n, :], o[:, n, :], k.par("gn_w", n), k.par("gn_b", n),
                                               ALU.mult, ALU.add)
            ch.link(last)
            ch.link(nc.vector.tensor_tensor(o[:], o[:], r.bonus[:], ALU.add))
            ch.link(nc.vector.tensor_tensor(o[:], o[:], r.g[:], ALU.mult))

        @block.scalar
        def _(act):
            act.wait_ge(v_at, V.at("centred"))
            nc.scalar.activation(sq[:], o[:], ACT.Square).then_inc(squared, 1)
            act.wait_ge(v_at, V.at("mean"))
            nc.scalar.activation(sq[:], sq[:], ACT.Sqrt).then_inc(rooted, 1)


def nsa_prepare_stage(k):
    nc = k.nc
    Z = k.z
    groups = [([ZQ, ZQ + 1, ZQ + 2, ZQ + 3], ["q_norm"] * 4, [0] * 4), ([ZK + 2, ZK + 4], ["k_norm"] * 2, [1, 2])]
    with ExitStack() as ctx:
        sq = k.sb(ctx, "sq", [P, 4, T])
        tab = k.sb(ctx, "rope", [P, 2, T])
        rot = k.sb(ctx, "rot", [P, P])
        V = Steps(None, "mean normed roped")
        E = Steps(None, "summed turned")
        v_at, e_at, squared, rooted, vt_ready, vt_out, loaded, stored, chain = k.sems(
            ctx, "dve_step", "pe_step", "squared", "rooted", "vt_ready", "vt_out", "loaded", "stored", "chain")
        block = ctx.enter_context(nc.Block())

        @block.sync
        def _(sp):
            sp.dma_start(tab.rearrange("p m t -> p (m t)"), k.d["rope"]).then_inc(loaded, 16)
            sp.dma_start(rot[:], k.d["rot"]).then_inc(loaded, 16)
            sp.dma_start(k.d["out_win"], k.d["win_rows"]).then_inc(stored, 16)
            sp.wait_ge(v_at, V.at("roped", 1))
            sp.dma_start(k.d["out_kv"], Z[:, ZK:NZ, :].rearrange("p c t -> p (c t)")).then_inc(stored, 16)
            sp.wait_ge(stored, 32)

        @block.scalar
        def _(act):
            for g, (tiles, _, _) in enumerate(groups):
                if g:
                    act.wait_ge(v_at, V.at("roped", g - 1))
                for n, z in enumerate(tiles):
                    last = nc.scalar.activation(sq[:, n, :], Z[:, z, :], ACT.Square)
                last.then_inc(squared, 1)
                act.wait_ge(v_at, V.at("mean", g))
                nc.scalar.activation(sq[:, 0:len(tiles), :], sq[:, 0:len(tiles), :], ACT.Sqrt).then_inc(rooted, 1)

        @block.tensor
        def _(pe):
            pe.wait_ge(loaded, 32)
            for g, (tiles, _, _) in enumerate(groups):
                pe.wait_ge(squared, g + 1)
                for n in range(len(tiles)):
                    for h in range(2):
                        mm = nc.tensor.matmul(k.bank(2 * n + h, TH), k.blocks[:], sq[:, n, h * TH:(h + 1) * TH],
                                              start=True, stop=True)
                mm.then_inc(e_at, 1)
                pe.wait_ge(v_at, V.at("normed", g))
                for n, z in enumerate(tiles):
                    for h in range(2):
                        mm = nc.tensor.matmul(k.bank(2 * n + h, TH), rot[:], Z[:, z, h * TH:(h + 1) * TH],
                                              start=True, stop=True)
                mm.then_inc(e_at, 1)
            for b, z in enumerate((ZK + 3, ZK + 5)):
                for tt in range(5):
                    n = min(P, T - tt * P)
                    mm = nc.tensor.transpose(k.ps[0:n, 4 + 2 * b + tt // 4, (tt % 4) * P:(tt % 4) * P + P],
                                             Z[:, z, tt * P:tt * P + n], k.ident[:])
            mm.then_inc(vt_ready, 1)

        @block.vector
        def _(dve):
            ch = Chain(dve, chain)
            dve.wait_ge(loaded, 32)
            for g, (tiles, gains, which) in enumerate(groups):
                m = len(tiles)
                dve.wait_ge(e_at, E.at("summed", g))
                for n in range(m):
                    last = nc.vector.tensor_scalar(halves(sq[:, n, :]), k.pair(2 * n), 1.0 / HD, EPS, ALU.mult, ALU.add)
                last.then_inc(v_at, 1)
                dve.wait_ge(rooted, g + 1)
                ch.link(nc.vector.reciprocal(sq[:, 0:m, :], sq[:, 0:m, :]))
                for n, z in enumerate(tiles):
                    last = nc.vector.scalar_tensor_tensor(out=Z[:, z, :], in0=Z[:, z, :], scalar=k.par(gains[n], which[n]),
                                                          in1=sq[:, n, :], op0=ALU.mult, op1=ALU.mult)
                last.then_inc(v_at, 1)
                dve.wait_ge(e_at, E.at("turned", g))
                for n in range(m):
                    last = nc.vector.tensor_tensor(halves(sq[:, n, :]), k.pair(2 * n), halves(tab[:, 1, :]), ALU.mult)
                dst = [k.qr[:, n, :] if g == 0 else Z[:, z, :] for n, z in enumerate(tiles)]
                for n, z in enumerate(tiles):
                    last = nc.vector.tensor_tensor(dst[n], Z[:, z, :], tab[:, 0, :], ALU.mult)
                ch.link(last)
                for n in range(m):
                    last = nc.vector.tensor_tensor(dst[n], dst[n], sq[:, n, :], ALU.add)
                last.then_inc(v_at, 1)
            dve.wait_ge(vt_ready, 1)
            for b, dst in enumerate((k.vs, k.vw)):
                nc.vector.tensor_copy(dst[:, 0:4, :].rearrange("p a c -> p (a c)"), k.bank(4 + 2 * b))
                last = nc.vector.tensor_copy(dst[0:TS, 4, :], k.ps[0:TS, 5 + 2 * b, 0:P])
            ch.link(last)


def compress_stage(k):
    nc = k.nc
    Z = k.z
    jobs = [("cache", 4, CH), ("cache", 4, CH), ("prompt", 1, 32)]
    with ExitStack() as ctx:
        w1 = k.sb(ctx, "w1", [P, 8, 2, 2, CMP_HIDDEN])
        w2 = k.sb(ctx, "w2", [P, 2, 2, HD])
        pos = k.sb(ctx, "pos", [P, 8, 2, 2])
        pages = k.sb(ctx, "pages", [P, 4 * PAGES, 8, 2, 2, 8])
        xp = k.sb(ctx, "xp", [P, 8, 2, 2, 32])
        bias = k.sb(ctx, "bias", [P, 4])
        second = k.sb(ctx, "second", [P, 512])
        hid = k.sb(ctx, "hid", [P, 2, 2, 512])
        sq = k.sb(ctx, "sq", [P, 256])
        rs = k.sb(ctx, "rs", [P, 256])
        weights, table, landed, parted, biased, bias_out, moved, summed, gelued, heads, squared, mean, rooted, out, chain, sums, kept \
            = k.sems(ctx, "weights", "table", "landed", "parted", "biased", "bias_out", "moved", "summed", "gelued",
                     "heads", "squared", "mean", "rooted", "out", "chain", "sums", "kept")
        block = ctx.enter_context(nc.Block())

        @block.sync
        def _(sp):
            sp.dma_start(k.table[:], k.d["page_table"]).then_inc(table, 16)
            sp.dma_start(w1.rearrange("p j e r f -> p (j e r f)"), k.d["cmp_w1"]).then_inc(weights, 16)
            sp.dma_start(w2.rearrange("p e h d -> p (e h d)"), k.d["cmp_w2"]).then_inc(weights, 16)
            sp.dma_start(pos.rearrange("p j e r -> p (j e r)"), k.d["cmp_pe"]).then_inc(weights, 16)
            sp.wait_ge(table, 16)
            for n in range(2):
                if n:
                    sp.wait_ge(parted, 4 * n)
                with sp.Fori(0, 4 * PAGES) as i:
                    page = sp.value_load(k.table[0:1, bass.ds(n * 4 * PAGES + i, 1)], min_val=0, max_val=k.n_phys - 1)
                    sp.dma_start(pages[:, bass.ds(i, 1)].rearrange("p o j e k c -> p (o j e k c)"),
                                 k.d["cmp_pages"][bass.ds(page, 1)].rearrange("o p n -> (o p) n")).then_inc(landed, 16)

        @block.tensor
        def _(pe):
            pe.wait_ge(weights, 48)
            for e in range(2):
                for f in range(2):
                    for j in range(8):
                        for r in range(2):
                            mm = nc.tensor.matmul(k.ps[:, 0, 2 * e + f:2 * e + f + 1], w1[:, j, e, r, f * P:(f + 1) * P],
                                                  pos[:, j, e, r:r + 1], start=j == 0 and r == 0, stop=j == 7 and r == 1)
            mm.then_inc(biased, 1)
            pe.wait_ge(bias_out, 1)
            for n, (kind, ns, cols) in enumerate(jobs):
                w = ns * 2 * cols
                if kind == "cache":
                    pe.wait_ge(landed, 16 * 4 * PAGES * (n + 1))
                else:
                    pe.wait_ge(moved, 1)
                for e in range(2):
                    for f in range(2):
                        b = 2 * (2 * e + f)
                        if n:
                            pe.wait_ge(out, 2 * n)
                        for r in range(2):
                            for j in range(8):
                                if kind == "cache":
                                    rhs = pages[:, :, j, e]
                                    dst = k.bank(b + r).rearrange("p (k s c) -> p s k c", k=2, c=8)
                                else:
                                    rhs = xp[:, j, e].rearrange("p k c -> p (k c)")
                                    dst = k.bank(b + r, w)
                                mm = nc.tensor.matmul(dst, w1[:, j, e, r, f * P:(f + 1) * P], rhs,
                                                      start=j == 0, stop=j == 7)
                        mm.then_inc(parted, 1)
                pe.wait_ge(gelued, 4 * (n + 1))
                half = w // 2
                for kv in range(2):
                    for f in range(2):
                        mm = nc.tensor.matmul(k.ps[kv * HD:kv * HD + HD, 0, 0:half], w2[:, 0, f, :],
                                              hid[:, 0, f, kv * half:(kv + 1) * half], start=f == 0, stop=f == 1)
                for s in range(ns):
                    for kv in range(2):
                        for f in range(2):
                            at = kv * half + s * cols
                            mm = nc.tensor.matmul(k.ps[0:cols, 1, s * P + kv * HD:s * P + kv * HD + HD],
                                                  hid[:, 1, f, at:at + cols], w2[:, 1, f, :], start=f == 0, stop=f == 1)
                mm.then_inc(heads, 1)
                pe.wait_ge(squared, n + 1)
                nc.tensor.matmul(k.bank(2, half), k.blocks[:], sq[:, 0:half], start=True, stop=True).then_inc(sums, 1)

        @block.scalar
        def _(act):
            for e in range(2):
                for kv in range(2):
                    for odd in range(2):
                        last = nc.scalar.activation(
                            xp[odd * HD:odd * HD + HD, :, e, kv, :].rearrange("p j c -> p c j"),
                            Z[kv * HD:kv * HD + HD, ZK + e, odd:SEQ:2].rearrange("p (c j) -> p c j", j=8), ACT.Copy)
            last.then_inc(moved, 1)
            act.wait_ge(bias_out, 1)
            for n, (kind, ns, cols) in enumerate(jobs):
                w = ns * 2 * cols
                for m in range(4):
                    act.wait_ge(parted, 4 * n + m + 1)
                    if 4 * n + m:
                        act.wait_ge(summed, 4 * n + m)
                    nc.scalar.activation(second[:, 0:w], k.bank(2 * m + 1, w), ACT.Identity,
                                         bias=bias[:, m:m + 1]).then_inc(kept, 1)
                    act.wait_ge(summed, 4 * n + m + 1)
                    nc.scalar.activation(hid[:, m // 2, m % 2, 0:w], hid[:, m // 2, m % 2, 0:w],
                                         ACT.Gelu_apprx_tanh).then_inc(gelued, 1)
                act.wait_ge(heads, n + 1)
                nc.scalar.activation(sq[:, 0:w // 2], k.bank(0, w // 2), ACT.Square).then_inc(squared, 1)
                act.wait_ge(mean, n + 1)
                nc.scalar.activation(rs[:, 0:w // 2], rs[:, 0:w // 2], ACT.Sqrt).then_inc(rooted, 1)

        @block.vector
        def _(dve):
            ch = Chain(dve, chain)
            dve.wait_ge(biased, 1)
            nc.vector.tensor_copy(bias[:], k.ps[:, 0, 0:4]).then_inc(bias_out, 1)
            for n, (kind, ns, cols) in enumerate(jobs):
                w = ns * 2 * cols
                for m in range(4):
                    if n and m == 0:
                        dve.wait_ge(heads, n)
                    dst = hid[:, m // 2, m % 2, 0:w].rearrange("p (s c) -> p s c", c=cols)
                    nc.vector.memset(dst[:, :, cols - 1:cols], 0.0)
                    dve.wait_ge(kept, 4 * n + m + 1)
                    nc.vector.tensor_tensor(
                        dst[:, :, 0:cols - 1], k.bank(2 * m, w).rearrange("p (s c) -> p s c", c=cols)[:, :, 0:cols - 1],
                        second[:, 0:w].rearrange("p (s c) -> p s c", c=cols)[:, :, 1:cols], ALU.add).then_inc(summed, 1)
                half = w // 2
                dve.wait_ge(heads, n + 1)
                if kind == "cache":
                    dst = k.vc[:, 4 * n:4 * n + 4, :].rearrange("p s d -> p (s d)")
                    nc.vector.tensor_copy(dst, k.ps[0:cols, 1, 0:ns * P]).then_inc(out, 1)
                else:
                    nc.vector.tensor_copy(k.vcp[:], k.ps[0:cols, 1, 0:P]).then_inc(out, 1)
                dve.wait_ge(sums, n + 1)
                nc.vector.tensor_scalar(rs[:, 0:half], k.bank(2, half), 1.0 / HD, EPS, ALU.mult, ALU.add).then_inc(mean, 1)
                dve.wait_ge(rooted, n + 1)
                ch.link(nc.vector.reciprocal(rs[:, 0:half], rs[:, 0:half]))
                dst = k.kc[:, 4 * n:4 * n + 4, :].rearrange("p s c -> p (s c)") if kind == "cache" else k.kcp[:]
                nc.vector.scalar_tensor_tensor(out=dst, in0=k.bank(0, half), scalar=k.par("k_norm", 0),
                                               in1=rs[:, 0:half], op0=ALU.mult, op1=ALU.mult).then_inc(out, 1)


def prompt_attention_stage(k):
    nc = k.nc
    Z = k.z
    units = [(qt, kv, i) for qt in range(SEQ // P) for kv in range(2) for i in range(4)]
    n_units = len(units)
    chunks = [2 * (qt + 1) + 1 for qt, _, _ in units]
    pieces = [-(-c // 4) for c in chunks]
    before = [sum(pieces[:u]) for u in range(n_units + 1)]
    CMP = 32
    with ExitStack() as ctx:
        E = k.sb(ctx, "probs", [P, 2, 2 * SEQ + CMP])
        PT = k.sb(ctx, "probs_t", [P, 2, 12, P])
        tri = k.sb(ctx, "tri", [P, P])
        cmask = k.sb(ctx, "cmask", [P, 4, CMP])
        cs = k.sb(ctx, "cmp_scores", [P, 8, CMP])
        mx = k.sb(ctx, "mx", [P, 2, 3])
        nm = k.sb(ctx, "nm", [P, 2, 3])
        sums = k.sb(ctx, "sums", [P, 2, 3])
        wts = k.sb(ctx, "wts", [P, 2, 3])
        loaded, scored, cmp_half, cmp_scored, cmp_masked, maxed, exped, weighted, turned, laid, mixed, out, chain = k.sems(
            ctx, "loaded", "scored", "cmp_half", "cmp_scored", "cmp_masked", "maxed", "exped", "weighted", "turned", "laid", "mixed",
            "out", "chain")

        def scores(u):
            qt = units[u][0]
            nk = (qt + 1) * P
            return k.bank(2 * (u % 2), nk), k.bank(2 * (u % 2) + 1, nk), cs[:, u % 8, :]

        def probs(u):
            nk = (units[u][0] + 1) * P
            return E[:, u % 2, 0:nk], E[:, u % 2, nk:2 * nk], E[:, u % 2, 2 * nk:2 * nk + CMP]

        block = ctx.enter_context(nc.Block())

        @block.sync
        def _(sp):
            sp.dma_start(tri[:], k.d["tri"]).then_inc(loaded, 16)
            sp.dma_start(cmask.rearrange("p a n -> p (a n)"), k.d["cmask"]).then_inc(loaded, 16)

        @block.tensor
        def _(pe):
            for step in range(n_units + 2):
                if step < n_units:
                    u = step
                    qt, kv, i = units[u]
                    half = slice(kv * HD, kv * HD + HD)
                    q = slice(qt * P, qt * P + P)
                    nk = (qt + 1) * P
                    if u % 8 == 0:
                        if qt:
                            pe.wait_ge(cmp_masked, qt)
                        for m in range(8):
                            mh = slice(m // 4 * HD, m // 4 * HD + HD)
                            mm = nc.tensor.matmul(k.ps[:, 4, m * CMP:(m + 1) * CMP], Z[mh, ZQ + m % 4, q], k.kcp[mh, :],
                                                  start=True, stop=True)
                            if m == 3:
                                mm.then_inc(cmp_half, 1)
                                pe.wait_ge(cmp_half, qt + 1)
                        mm.then_inc(cmp_scored, 1)
                    if u >= 2:
                        pe.wait_ge(exped, u - 1)
                    sel, win, _ = scores(u)
                    nc.tensor.matmul(sel, k.qr[half, i, q], Z[half, ZK + 2, 0:nk], start=True, stop=True)
                    nc.tensor.matmul(win, k.qr[half, i, q], Z[half, ZK + 4, 0:nk], start=True, stop=True).then_inc(scored, 1)
                if 1 <= step <= n_units:
                    u = step - 1
                    pe.wait_ge(weighted, u + 1)
                    for n in range(pieces[u]):
                        at = before[u] + n
                        if at >= 2:
                            pe.wait_ge(laid, at - 1)
                        for c in range(4 * n, min(4 * n + 4, chunks[u])):
                            w = P if c < chunks[u] - 1 else CMP
                            mm = nc.tensor.transpose(k.ps[0:w, 6 + at % 2, (c % 4) * P:(c % 4) * P + P],
                                                     E[:, u % 2, c * P:c * P + w], k.ident[:])
                        mm.then_inc(turned, 1)
                if step >= 2:
                    u = step - 2
                    qt, kv, i = units[u]
                    pe.wait_ge(laid, before[u + 1])
                    if u >= 1:
                        pe.wait_ge(out, u)
                    for c in range(chunks[u]):
                        if c == chunks[u] - 1:
                            lhs, rhs = k.vcp[:], PT[0:CMP, u % 2, c, :]
                        else:
                            v = k.vs if c <= qt else k.vw
                            lhs, rhs = v[:, c % (qt + 1), :], PT[:, u % 2, c, :]
                        mm = nc.tensor.matmul(k.bank(5, P), lhs, rhs, start=c == 0, stop=c == chunks[u] - 1)
                    mm.then_inc(mixed, 1)

        @block.scalar
        def _(act):
            for step in range(n_units + 1):
                if step < n_units:
                    u = step
                    act.wait_ge(maxed, u + 1)
                    if u >= 2:
                        act.wait_ge(turned, before[u - 1])
                    for b, (src, dst) in enumerate(zip(scores(u), probs(u))):
                        last = nc.scalar.activation(dst, src, ACT.Exp, bias=nm[:, u % 2, b:b + 1], scale=SCALE,
                                                    accum_out=sums[:, u % 2, b:b + 1])
                    last.then_inc(exped, 1)
                if step >= 1:
                    u = step - 1
                    for n in range(pieces[u]):
                        at = before[u] + n
                        act.wait_ge(turned, at + 1)
                        if n == 0 and u >= 2:
                            act.wait_ge(mixed, u - 1)
                        full = min(4, chunks[u] - 1 - 4 * n)
                        if full:
                            last = nc.scalar.activation(PT[:, u % 2, 4 * n:4 * n + full, :],
                                                        k.ps[:, 6 + at % 2, 0:full * P].rearrange("p (c q) -> p c q", q=P),
                                                        ACT.Copy)
                        if n == pieces[u] - 1:
                            last = nc.scalar.activation(PT[0:CMP, u % 2, chunks[u] - 1, :],
                                                        k.ps[0:CMP, 6 + at % 2, full * P:full * P + P], ACT.Copy)
                        last.then_inc(laid, 1)

        @block.vector
        def _(dve):
            ch = Chain(dve, chain)
            dve.wait_ge(loaded, 32)
            for step in range(n_units + 2):
                if step < n_units:
                    u = step
                    qt = units[u][0]
                    if u % 8 == 0:
                        dve.wait_ge(cmp_scored, qt + 1)
                        if u:
                            dve.wait_ge(exped, u)
                        nc.vector.tensor_tensor(cs[:], k.bank(4, 8 * CMP).rearrange("p (m n) -> p m n", n=CMP),
                                                cmask[:, qt:qt + 1, :].broadcast_to([P, 8, CMP]), ALU.add).then_inc(cmp_masked, 1)
                        dve.wait_ge(cmp_masked, qt + 1)
                    dve.wait_ge(scored, u + 1)
                    sel, win, cmp = scores(u)
                    last_keys = slice(qt * P, qt * P + P)
                    nc.vector.tensor_tensor(sel[:, last_keys], sel[:, last_keys], tri[:], ALU.add)
                    ch.link(nc.vector.tensor_tensor(win[:, last_keys], win[:, last_keys], tri[:], ALU.add))
                    for b, src in enumerate((sel, win, cmp)):
                        last = nc.vector.tensor_reduce(mx[:, u % 2, b:b + 1], src, AX.X, ALU.max)
                    ch.link(last)
                    nc.vector.tensor_scalar(nm[:, u % 2, :], mx[:, u % 2, :], NEG * 1e-10, -SCALE, ALU.max,
                                            ALU.mult).then_inc(maxed, 1)
                if 1 <= step <= n_units:
                    u = step - 1
                    qt, kv, i = units[u]
                    dve.wait_ge(exped, u + 1)
                    ch.link(nc.vector.tensor_scalar(wts[:, u % 2, :], sums[:, u % 2, :], 1e-30, None, ALU.max))
                    ch.link(nc.vector.reciprocal(wts[:, u % 2, :], wts[:, u % 2, :]))
                    g = 3 * (4 * kv + i)
                    nc.vector.tensor_tensor(wts[:, u % 2, 0:2], wts[:, u % 2, 0:2], k.gates[:, qt, g + 1:g + 3], ALU.mult)
                    ch.link(nc.vector.tensor_tensor(wts[:, u % 2, 2:3], wts[:, u % 2, 2:3], k.gates[:, qt, g:g + 1],
                                                    ALU.mult))
                    for b, dst in enumerate(probs(u)):
                        last = nc.vector.tensor_scalar(dst, dst, wts[:, u % 2, b:b + 1], None, ALU.mult)
                    last.then_inc(weighted, 1)
                if step >= 2:
                    u = step - 2
                    qt, kv, i = units[u]
                    half = slice(kv * HD, kv * HD + HD)
                    dve.wait_ge(mixed, u + 1)
                    nc.vector.tensor_copy(k.on[half, i, qt * P:qt * P + P], k.ps[half, 5, 0:P]).then_inc(out, 1)


def sample_attention_stage(k):
    nc = k.nc
    Z = k.z
    NG = DEC_BATCH // 2
    NSEL = PAST // SEL_BLOCK
    KEYS = dict(sel=(0, PAST), win=(PAST, WINDOW), seln=(PAST + WINDOW, TS), winn=(PAST + WINDOW + TS, TS),
                cmp=(PAST + WINDOW + 2 * TS, CH - 1))
    with ExitStack() as ctx:
        kv_pages = k.sb(ctx, "kv_pages", [P, 2, 2 * PAGES, 2 * P])
        wk = k.sb(ctx, "win_k", [P, 2, 2, WINDOW])
        wv = k.sb(ctx, "win_v", [P, 2, 2, 4, P])
        E = k.sb(ctx, "probs", [P, PAST + WINDOW + 2 * TS + CH])
        PT = k.sb(ctx, "probs_t", [P, 15, P])
        newmask = k.sb(ctx, "newmask", [P, NG, TS])
        winmask = k.sb(ctx, "winmask", [P, DEC_SEQ])
        pick = k.sb(ctx, "pick", [TS, NG, P])
        headmask = k.sb(ctx, "headmask", [P, NGATE])
        same = k.sb(ctx, "same", [P, P])
        iota = k.sb(ctx, "iota", [P, 14])
        mx = k.sb(ctx, "mx", [P, 5])
        nm = k.sb(ctx, "nm", [P, 3])
        sums = k.sb(ctx, "sums", [P, 5])
        wts = k.sb(ctx, "wts", [P, 3])
        pc = k.sb(ctx, "pc", [P, CH])
        imp = k.sb(ctx, "imp", [P, 14])
        pen = k.sb(ctx, "pen", [P, 14])
        one = k.sb(ctx, "one", [P, 2])
        gsel = k.sb(ctx, "gsel", [P, NGATE])
        gr = k.sb(ctx, "gr", [P, 3])
        qs = k.sb(ctx, "qs", [P, 2, DEC_BATCH, 4 * DEC_SEQ])
        V = Steps(None, "cmpmax pc maxes weighted out")
        S = Steps(None, "cmpexp exps laid1 laid2")
        PE = Steps(None, "scores imp turned1 turned2 mixed")
        v_at, s_at, e_at, loaded, landed0, landed1, chain, packed = k.sems(
            ctx, "dve_step", "act_step", "pe_step", "loaded", "landed0", "landed1", "chain", "packed")
        landed = (landed0, landed1)
        tables = [(newmask.rearrange("p g t -> p (g t)"), "newmask"), (winmask[:], "winmask"),
                  (pick.rearrange("p g t -> p (g t)"), "pick"), (headmask[:], "headmask"), (same[:], "same"),
                  (iota[:], "iota14")]
        past = k.ps[:, 0:2, :].rearrange("p b n -> p (b n)")
        win, small = k.bank(2), k.bank(3)
        near = k.sb(ctx, "near", [P, 3 * CH])
        parts = lambda t: (t[:, 0:CH - 1], t[:, CH:2 * CH], t[:, 2 * CH:3 * CH])
        cmp, seln, winn = parts(near)
        isum, grow, mix = k.ps[:, 4, 0:CH - 1], k.ps[:, 4, 128:128 + NGATE], k.ps[:, 4, 256:256 + P]
        probs = lambda name: E[:, KEYS[name][0]:KEYS[name][0] + KEYS[name][1]]
        block = ctx.enter_context(nc.Block())

        @block.sync
        def _(sp):
            for dst, name in tables:
                sp.dma_start(dst, k.d[name]).then_inc(loaded, 16)
            for g in range(NG):
                b = g % 2
                if g >= 2:
                    sp.wait_ge(e_at, PE.at("mixed", g - 2))
                with sp.Fori(0, 2 * PAGES) as i:
                    page = sp.value_load(k.table[0:1, bass.ds(g * 2 * PAGES + i, 1)], min_val=0, max_val=k.n_phys - 1)
                    sp.dma_start(kv_pages[:, b, bass.ds(i, 1), :].rearrange("p o n -> p (o n)"),
                                 k.d["sel_pages"][bass.ds(page, 1)].rearrange("o p n -> (o p) n")).then_inc(landed[b], 16)
                sp.dma_start(wk[:, b].rearrange("p s n -> p (s n)"), k.d["win_k"][g]).then_inc(landed[b], 16)
                sp.dma_start(wv[:, b].rearrange("p s c n -> p (s c n)"), k.d["win_v"][g]).then_inc(landed[b], 16)

        @block.tensor
        def _(pe):
            pe.wait_ge(loaded, 16 * len(tables))
            pe.wait_ge(packed, 2)
            for g in range(NG):
                b = g % 2
                pe.wait_ge(landed[b], (g // 2 + 1) * 16 * (2 * PAGES + 2))
                if g:
                    pe.wait_ge(s_at, S.at("exps", g - 1))
                    pe.wait_ge(v_at, V.at("out", g - 1))
                for s in range(2):
                    seq = 2 * g + s
                    for kv in range(2):
                        half = slice(kv * HD, kv * HD + HD)
                        rows = slice(32 * (2 * s + kv), 32 * (2 * s + kv) + 32)
                        qr, qn = qs[half, 0, seq, :], qs[half, 1, seq, :]
                        for n in range(2):
                            nc.tensor.matmul(past[rows, n * 512:(n + 1) * 512], qr,
                                             kv_pages[half, b, PAGES * s + 4 * n:PAGES * s + 4 * n + 4, 0:P],
                                             start=True, stop=True)
                        nc.tensor.matmul(win[rows, :], qr, wk[half, b, s, :], start=True, stop=True)
                        pcmp, pseln, pwinn = parts(small)
                        nc.tensor.matmul(pcmp[rows, :], qn, k.kc[half, seq, 0:CH - 1], start=True, stop=True)
                        nc.tensor.matmul(pseln[rows, :], qr, Z[half, ZK + 2, SEQ:T], start=True, stop=True)
                        nc.tensor.matmul(pwinn[rows, :], qr, Z[half, ZK + 4, SEQ:T], start=True, stop=True)
                nc.tensor.matmul(grow, pick[:, g, :], k.gates[0:TS, 4, :], start=True, stop=True).then_inc(e_at, 1)
                pe.wait_ge(v_at, V.at("pc", g))
                nc.tensor.matmul(isum, same[:], pc[:, 0:CH - 1], start=True, stop=True).then_inc(e_at, 1)
                pe.wait_ge(v_at, V.at("weighted", g))
                for n in range(12):
                    mm = nc.tensor.transpose(k.ps[:, 5 + n // 4, (n % 4) * P:(n % 4) * P + P], E[:, n * P:(n + 1) * P],
                                             k.ident[:])
                mm.then_inc(e_at, 1)
                pe.wait_ge(s_at, S.at("laid1", g))
                for n, name in enumerate(("seln", "winn", "cmp")):
                    mm = nc.tensor.transpose(k.ps[0:KEYS[name][1], 5, n * P:n * P + P], probs(name), k.ident[:])
                mm.then_inc(e_at, 1)
                pe.wait_ge(s_at, S.at("laid2", g))
                for s in range(2):
                    seq = 2 * g + s
                    cols = slice(CH * s, CH * s + CH)
                    terms = [(kv_pages[:, b, PAGES * s + n, P:2 * P], PT[:, n, cols]) for n in range(PAGES)]
                    terms += [(wv[:, b, s, n, :], PT[:, PAGES + n, cols]) for n in range(4)]
                    terms += [(k.vs[0:TS, 4, :], PT[0:TS, 12, cols]), (k.vw[0:TS, 4, :], PT[0:TS, 13, cols]),
                              (k.vc[0:CH - 1, seq, :], PT[0:CH - 1, 14, cols])]
                    for n, (lhs, rhs) in enumerate(terms):
                        mm = nc.tensor.matmul(mix[:, cols], lhs, rhs, start=n == 0, stop=n == len(terms) - 1)
                mm.then_inc(e_at, 1)

        @block.scalar
        def _(act):
            for g in range(NG):
                act.wait_ge(v_at, V.at("cmpmax", g))
                if g:
                    act.wait_ge(e_at, PE.at("turned2", g - 1))
                nc.scalar.activation(probs("cmp"), cmp, ACT.Exp, bias=nm[:, 0:1], scale=SCALE,
                                     accum_out=sums[:, 0:1]).then_inc(s_at, 1)
                act.wait_ge(v_at, V.at("maxes", g))
                for n, (name, src, b) in enumerate((("sel", past, 1), ("seln", seln, 1), ("win", win, 2),
                                                    ("winn", winn, 2))):
                    last = nc.scalar.activation(probs(name), src, ACT.Exp, bias=nm[:, b:b + 1], scale=SCALE,
                                                accum_out=sums[:, 1 + n:2 + n])
                last.then_inc(s_at, 1)
                act.wait_ge(e_at, PE.at("turned1", g))
                last = nc.scalar.activation(PT[:, 0:12, :].rearrange("p c q -> p (c q)"),
                                            k.ps[:, 5:8, :].rearrange("p b n -> p (b n)"), ACT.Copy)
                last.then_inc(s_at, 1)
                act.wait_ge(e_at, PE.at("turned2", g))
                nc.scalar.activation(PT[0:TS, 12:14, :].rearrange("p c q -> p (c q)"), k.ps[0:TS, 5, 0:2 * P], ACT.Copy)
                nc.scalar.activation(PT[0:CH - 1, 14, :], k.ps[0:CH - 1, 5, 2 * P:3 * P], ACT.Copy).then_inc(s_at, 1)

        @block.vector
        def _(dve):
            ch = Chain(dve, chain)
            for m, src in enumerate((k.qr, Z[:, ZQ:ZQ + 4, :])):
                for i in range(4):
                    last = nc.vector.tensor_copy(qs[:, m].rearrange("p s (i t) -> p s i t", i=4)[:, :, i, :],
                                                 src[:, i, SEQ:T].rearrange("p (s t) -> p s t", t=DEC_SEQ))
                last.then_inc(packed, 1)
            dve.wait_ge(loaded, 16 * len(tables))
            for g in range(NG):
                dve.wait_ge(e_at, PE.at("scores", g))
                for dst, src in zip(parts(near), parts(small)):
                    last = nc.vector.tensor_copy(dst, src)
                ch.link(last)
                ch.link(nc.vector.tensor_reduce(mx[:, 0:1], cmp, AX.X, ALU.max))
                nc.vector.tensor_scalar(nm[:, 0:1], mx[:, 0:1], -SCALE, None, ALU.mult).then_inc(v_at, 1)
                nc.vector.tensor_tensor(seln, seln, newmask[:, g, :], ALU.add)
                nc.vector.tensor_tensor(winn, winn, newmask[:, g, :], ALU.add)
                nc.vector.tensor_tensor(win[:, 0:DEC_SEQ], win[:, 0:DEC_SEQ], winmask[:], ALU.add)
                ch.link(nc.vector.tensor_tensor(gsel[:], grow, headmask[:], ALU.mult))
                nc.vector.tensor_reduce(gr[:], gsel.rearrange("p (h b) -> p b h", b=3), AX.X, ALU.add)
                nc.vector.tensor_reduce(mx[:, 1:2], seln, AX.X, ALU.max)
                nc.vector.tensor_reduce(mx[:, 2:3], win, AX.X, ALU.max)
                ch.link(nc.vector.tensor_reduce(mx[:, 3:4], winn, AX.X, ALU.max))
                dve.wait_ge(s_at, S.at("cmpexp", g))
                ch.link(nc.vector.tensor_scalar(wts[:, 0:1], sums[:, 0:1], 1e-30, None, ALU.max))
                ch.link(nc.vector.reciprocal(wts[:, 0:1], wts[:, 0:1]))
                nc.vector.tensor_scalar(pc[:, 0:CH - 1], probs("cmp"), wts[:, 0:1], None, ALU.mult).then_inc(v_at, 1)
                dve.wait_ge(e_at, PE.at("imp", g))
                ch.link(nc.vector.tensor_copy(pc[:, 0:CH - 1], isum))
                windows = pc[:, 3:3 + 4 * 14].rearrange("p (j c) -> p j c", c=4)
                ch.link(nc.vector.tensor_reduce(imp[:], windows, AX.X, ALU.add))
                ch.link(nc.vector.tensor_tensor(imp[:], imp[:], pc[:, 7:7 + 4 * 14:4], ALU.add))
                ch.link(nc.vector.tensor_reduce(one[:, 0:1], imp[:], AX.X, ALU.min))
                ch.link(nc.vector.tensor_scalar(pen[:], imp[:], one[:, 0:1], None, ALU.is_le))
                ch.link(nc.vector.tensor_tensor(pen[:], pen[:], iota[:], ALU.mult))
                ch.link(nc.vector.tensor_reduce(one[:, 1:2], pen[:], AX.X, ALU.max))
                ch.link(nc.vector.tensor_scalar(pen[:], iota[:], one[:, 1:2], NEG, ALU.is_equal, ALU.mult))
                blocks = past[:, SEL_BLOCK:15 * SEL_BLOCK].rearrange("p (j c) -> p j c", c=SEL_BLOCK)
                ch.link(nc.vector.tensor_tensor(blocks, blocks, pen.rearrange("p (j o) -> p j o", o=1)
                                                .broadcast_to([P, 14, SEL_BLOCK]), ALU.add))
                ch.link(nc.vector.tensor_reduce(mx[:, 4:5], past, AX.X, ALU.max))
                ch.link(nc.vector.tensor_tensor(mx[:, 0:1], mx[:, 4:5], mx[:, 1:2], ALU.max))
                ch.link(nc.vector.tensor_tensor(mx[:, 1:2], mx[:, 2:3], mx[:, 3:4], ALU.max))
                nc.vector.tensor_scalar(nm[:, 1:3], mx[:, 0:2], -SCALE, None, ALU.mult).then_inc(v_at, 1)
                dve.wait_ge(s_at, S.at("exps", g))
                nc.vector.tensor_tensor(wts[:, 1:2], sums[:, 1:2], sums[:, 2:3], ALU.add)
                ch.link(nc.vector.tensor_tensor(wts[:, 2:3], sums[:, 3:4], sums[:, 4:5], ALU.add))
                ch.link(nc.vector.tensor_scalar(wts[:, 1:3], wts[:, 1:3], 1e-30, None, ALU.max))
                ch.link(nc.vector.reciprocal(wts[:, 1:3], wts[:, 1:3]))
                ch.link(nc.vector.tensor_tensor(wts[:], wts[:], gr[:], ALU.mult))
                for name, b in (("sel", 1), ("seln", 1), ("win", 2), ("winn", 2), ("cmp", 0)):
                    last = nc.vector.tensor_scalar(probs(name), probs(name), wts[:, b:b + 1], None, ALU.mult)
                last.then_inc(v_at, 1)
                dve.wait_ge(e_at, PE.at("mixed", g))
                for kv in range(2):
                    half = slice(kv * HD, kv * HD + HD)
                    for s in range(2):
                        at = SEQ + (2 * g + s) * DEC_SEQ
                        src = mix[half, CH * s + 32 * kv:CH * s + 32 * kv + 32].rearrange("p (i t) -> p i t", i=4)
                        last = nc.vector.tensor_copy(k.on[half, :, at:at + DEC_SEQ], src)
                last.then_inc(v_at, 1)


def merge_stage(k, m_hi, m_lo):
    nc = k.nc
    out = k.z[:, 8:16, :]
    ring = 4
    with ExitStack() as ctx:
        wt = k.sb(ctx, "wt", [P, ring, KD, P])
        tmp = k.sb(ctx, "tmp", [P, T])
        arrived = k.sems(ctx, *[f"arrived{b}" for b in range(ring)])
        multiplied, gated, merged, rounded, chain = k.sems(ctx, "multiplied", "gated", "merged", "rounded", "chain")
        block = ctx.enter_context(nc.Block())

        @block.sync
        def _(sp):
            for n in range(KD):
                if n >= ring:
                    sp.wait_ge(multiplied, n - ring + 1)
                sp.dma_start(wt[:, n % ring].rearrange("p c n -> p (c n)"), k.d["w_merge"][n]).then_inc(arrived[n % ring], 16)

        @block.tensor
        def _(pe):
            for n in range(KD):
                pe.wait_ge(arrived[n % ring], 16 * (n // ring + 1))
                if n >= 2:
                    pe.wait_ge(merged, n - 1)
                for branch, src in enumerate((k.r.o, k.on)):
                    for c in range(4):
                        for h in range(2):
                            mm = nc.tensor.matmul(k.bank(4 * (n % 2) + 2 * branch + h, TH), wt[:, n % ring, 4 * branch + c, :],
                                                  src[:, c, h * TH:(h + 1) * TH], start=c == 0, stop=c == 3)
                mm.then_inc(multiplied, 1)

        @block.scalar
        def _(act):
            for n in range(KD):
                nc.scalar.activation(k.zg[:, n, :], k.zg[:, n, :], ACT.Sigmoid)
                nc.scalar.activation(k.zg[:, KD + n, :], k.zg[:, KD + n, :], ACT.Sigmoid).then_inc(gated, 1)
            for n in range(KD):
                act.wait_ge(merged, n + 1)
                nc.scalar.activation(m_hi[:, n, :], out[:, n, :], ACT.Copy).then_inc(rounded, 1)

        @block.vector
        def _(dve):
            ch = Chain(dve, chain)
            for n in range(KD):
                dve.wait_ge(gated, n + 1)
                dve.wait_ge(multiplied, n + 1)
                if n:
                    dve.wait_ge(merged, n)
                b = 4 * (n % 2)
                nc.vector.tensor_tensor(halves(out[:, n, :]), k.pair(b), halves(k.zg[:, n, :]), ALU.mult)
                ch.link(nc.vector.tensor_tensor(halves(tmp[:]), k.pair(b + 2), halves(k.zg[:, KD + n, :]), ALU.mult))
                nc.vector.tensor_tensor(out[:, n, :], out[:, n, :], tmp[:], ALU.add).then_inc(merged, 1)
            for n in range(KD):
                dve.wait_ge(rounded, n + 1)
                last = nc.vector.tensor_tensor(m_lo[:, n, :], out[:, n, :], m_hi[:, n, :].bitcast(F32), ALU.subtract)
            ch.link(last)


def choose_stage(k, q, picked):
    nc = k.nc
    NP = P
    tiles = [(tt * P, min(P, T - tt * P)) for tt in range(5)]
    HC = 2 * HEADS
    with ExitStack() as ctx:
        keys = k.sb(ctx, "keys", [P, HEADS, N_KEYS])
        sc = k.sb(ctx, "sc", [P, 2, HC, N_KEYS])
        sv = k.sb(ctx, "sv", [P, HC, TOPK])
        si = k.sb(ctx, "si", [P, HC, TOPK], U32)
        sif = k.sb(ctx, "sif", [P, HC, TOPK])
        cand = k.sb(ctx, "cand", [P, HEADS, TOPK, TOPK])
        cv = k.sb(ctx, "cv", [P, HEADS, TOPK])
        ci = k.sb(ctx, "ci", [P, HEADS, TOPK], U32)
        cj = k.sb(ctx, "cj", [P, 2, HEADS * TOPK], U32)
        cjf = k.sb(ctx, "cjf", [P, 2, HEADS * TOPK])
        hot = k.sb(ctx, "hot", [P, HEADS * TOPK, TOPK])
        num = k.sb(ctx, "num", [P, 3, HEADS * TOPK])
        ex = k.sb(ctx, "ex", [P, HEADS, TOPK])
        tot = k.sb(ctx, "tot", [P, HEADS])
        iota = k.sb(ctx, "iota", [P, TOPK])
        loaded, scored, copied, lowered, exped, chosen, turned, laid, chain = k.sems(
            ctx, "loaded", "scored", "copied", "lowered", "exped", "chosen", "turned", "laid", "chain")
        block = ctx.enter_context(nc.Block())

        @block.sync
        def _(sp):
            sp.dma_start(keys.rearrange("p h n -> p (h n)"), k.d["keys"]).then_inc(loaded, 16)
            sp.dma_start(iota[:], k.d["iota16"]).then_inc(loaded, 16)

        @block.tensor
        def _(pe):
            pe.wait_ge(loaded, 32)
            for n, (at, rows) in enumerate(tiles):
                if n:
                    pe.wait_ge(copied, n)
                for h in range(HEADS):
                    for c in range(2):
                        half = slice(c * HD, c * HD + HD)
                        mm = nc.tensor.matmul(k.ps[0:rows, 2 * c + h // 4, (h % 4) * N_KEYS:(h % 4 + 1) * N_KEYS],
                                              q[half, h, at:at + rows], keys[half, h, :], start=True, stop=True)
                mm.then_inc(scored, 1)
                pe.wait_ge(chosen, n + 1)
                if n:
                    pe.wait_ge(laid, n)
                for m in range(3):
                    mm = nc.tensor.transpose(k.ps[:, 4, m * P:m * P + rows], num[0:rows, m, :], k.ident[0:rows, 0:rows])
                mm.then_inc(turned, 1)

        @block.scalar
        def _(act):
            for n, (at, rows) in enumerate(tiles):
                act.wait_ge(scored, n + 1)
                if n:
                    act.wait_ge(lowered, n)
                nc.scalar.activation(sc[0:rows, 0].rearrange("p a n -> p (a n)"),
                                     k.ps[0:rows, 0:4, :].rearrange("p b n -> p (b n)"), ACT.Copy).then_inc(copied, 1)
                act.wait_ge(lowered, n + 1)
                nc.scalar.activation(ex[0:rows], ex[0:rows], ACT.Exp).then_inc(exped, 1)
                act.wait_ge(turned, n + 1)
                nc.scalar.activation(picked[:, :, at:at + rows],
                                     k.ps[:, 4, 0:3 * P].rearrange("p (m t) -> p m t", m=3)[:, :, 0:rows],
                                     ACT.Copy).then_inc(laid, 1)

        @block.vector
        def _(dve):
            ch = Chain(dve, chain)
            dve.wait_ge(loaded, 32)

            def top16(src, spare, val, idx, count, rows):
                for n in range(count):
                    last = nc.vector.max(val[0:rows, n, 0:8], src(n))
                ch.link(last)
                for n in range(count):
                    nc.vector.max_index(idx[0:rows, n, 0:8], val[0:rows, n, 0:8], src(n))
                    last = nc.vector.match_replace(spare(n), val[0:rows, n, 0:8], src(n), NEG)
                ch.link(last)
                for n in range(count):
                    last = nc.vector.max(val[0:rows, n, 8:16], spare(n))
                ch.link(last)
                for n in range(count):
                    last = nc.vector.max_index(idx[0:rows, n, 8:16], val[0:rows, n, 8:16], spare(n))
                ch.link(last)

            for n, (at, rows) in enumerate(tiles):
                r = slice(0, rows)
                dve.wait_ge(copied, n + 1)
                top16(lambda m: sc[r, 0, m, :], lambda m: sc[r, 1, m, :], sv, si, HC, rows)
                nc.vector.tensor_copy(sif[r], si[r])
                first = sv[r, 0:HEADS, :].rearrange("p h (j o) -> p h j o", o=1).broadcast_to([rows, HEADS, TOPK, TOPK])
                second = sv[r, HEADS:, :].rearrange("p h (o j) -> p h o j", o=1).broadcast_to([rows, HEADS, TOPK, TOPK])
                ch.link(nc.vector.tensor_tensor(cand[r], first, second, ALU.add))
                spare = sc[:, 1].rearrange("p a n -> p (a n)").rearrange("p (h m) -> p h m", h=HEADS)
                top16(lambda m: cand[r, m].rearrange("p a b -> p (a b)"), lambda m: spare[r, m, :], cv, ci, HEADS, rows)
                nc.vector.tensor_scalar(cj[r, 0], ci[r].rearrange("p h j -> p (h j)"), 4, None, ALU.logical_shift_right)
                nc.vector.tensor_scalar(cj[r, 1], ci[r].rearrange("p h j -> p (h j)"), 15, None, ALU.bitwise_and)
                ch.link(nc.vector.tensor_tensor(ex[r], cv[r], cv[r, :, 0:1].broadcast_to([rows, HEADS, TOPK]),
                                                ALU.subtract))
                nc.vector.tensor_copy(cjf[r], cj[r]).then_inc(lowered, 1)
                dve.wait_ge(lowered, n + 1)
                for c in range(2):
                    place = cjf[r, c, :].rearrange("p (a o) -> p a o", o=1).broadcast_to([rows, P, TOPK])
                    slot = iota[r].rearrange("p (o j) -> p o j", o=1).broadcast_to([rows, P, TOPK])
                    ch.link(nc.vector.tensor_tensor(hot[r], place, slot, ALU.is_equal))
                    which = sif[r, c * HEADS:(c + 1) * HEADS, :].rearrange("p h (o j) -> p h o j", o=1) \
                        .broadcast_to([rows, HEADS, TOPK, TOPK])
                    hot4 = hot[r].rearrange("p (h a) j -> p h a j", h=HEADS)
                    ch.link(nc.vector.tensor_tensor(hot4, hot4, which, ALU.mult))
                    if c == 0 and n:
                        dve.wait_ge(turned, n)
                    ch.link(nc.vector.tensor_reduce(num[r, c, :], hot[r], AX.X, ALU.add))
                dve.wait_ge(exped, n + 1)
                ch.link(nc.vector.tensor_reduce(tot[r], ex[r], AX.X, ALU.add))
                ch.link(nc.vector.reciprocal(tot[r], tot[r]))
                nc.vector.tensor_tensor(num[r, 2, :].rearrange("p (h j) -> p h j", h=HEADS), ex[r],
                                        tot[r].rearrange("p (h o) -> p h o", o=1).broadcast_to([rows, HEADS, TOPK]),
                                        ALU.mult).then_inc(chosen, 1)


def gate_matrix_stage(k, picked):
    nc = k.nc
    Q = 4
    rounds = T // (2 * TB)
    with ExitStack() as ctx:
        a = k.sb(ctx, "a", [P, TB, N_KEYS])
        b = k.sb(ctx, "b", [P, TB, N_KEYS])
        nq = TB // Q
        cur = k.sb(ctx, "cur", [P, 2, 3, TB])
        G = k.sb(ctx, "g", [P, 2, N_KEYS, TB])
        iota = k.sb(ctx, "iota", [P, N_KEYS])
        loaded, current, a_made, b_made, spread, taken, stored0, stored1, passed = k.sems(
            ctx, "loaded", "current", "a_made", "b_made", "spread", "taken", "stored0", "stored1", "passed")
        stored = (stored0, stored1)
        block = ctx.enter_context(nc.Block())

        @block.sync
        def _(sp):
            sp.dma_start(iota[:], k.d["iota128"]).then_inc(loaded, 16)
            with sp.Fori(0, rounds) as i:
                for s in range(2):
                    sp.wait_ge(taken, (i * 2 + s) * nq + nq + nq)
                    sp.dma_start(k.g_dram[bass.ds(i * 2 + s, 1)].rearrange("o p n -> (o p) n"),
                                 G[:, s].rearrange("p n t -> p (n t)")).then_inc(stored[s], 16)
            for s in range(2):
                sp.wait_ge(stored[s], 16 * (rounds + 1))

        @block.vector
        def _(dve):
            dve.sem_inc(spread, nq)
            dve.wait_ge(loaded, 16)
            with dve.Fori(0, rounds) as i:
                for s in range(2):
                    dve.wait_ge(spread, (i * 2 + s) * nq + 1)
                    nc.vector.tensor_copy(cur[:, s], picked[:, :, bass.ds(i * 2 * TB + s * TB, TB)]).then_inc(current, 1)
                    dve.wait_ge(current, i * 2 + s + 1)
                    for q in range(nq):
                        dve.wait_ge(spread, (i * 2 + s) * nq + q + 1)
                        for t in range(Q * q, Q * q + Q):
                            last = nc.vector.tensor_scalar(a[:, t, :], iota[:], cur[:, s, 0, t:t + 1], cur[:, s, 2, t:t + 1],
                                                           ALU.is_equal, ALU.mult)
                        t = Q * q + Q // 2
                        slots = iota.rearrange("p (o n) -> p o n", o=1).broadcast_to([P, Q // 2, N_KEYS])
                        keys = cur[:, s, 1, t:t + Q // 2].rearrange("p (t o) -> p t o", o=1).broadcast_to([P, Q // 2, N_KEYS])
                        nc.vector.tensor_tensor(b[:, t:t + Q // 2, :], slots, keys, ALU.is_equal).then_inc(a_made, 1)

        @block.gpsimd
        def _(pool):
            pool.wait_ge(loaded, 16)
            with pool.Fori(0, rounds) as i:
                for s in range(2):
                    pool.wait_ge(current, i * 2 + s + 1)
                    for q in range(nq):
                        pool.wait_ge(spread, (i * 2 + s) * nq + q + 1)
                        pool.sem_inc(passed, 1)
                        for t in range(Q * q, Q * q + Q // 2):
                            last = nc.gpsimd.tensor_scalar(b[:, t, :], iota[:], cur[:, s, 1, t:t + 1], None, ALU.is_equal)
                        last.then_inc(b_made, 1)

        @block.tensor
        def _(pe):
            with pe.Fori(0, rounds) as i:
                for s in range(2):
                    for q in range(nq):
                        pe.wait_ge(a_made, (i * 2 + s) * nq + q + 1)
                        pe.wait_ge(b_made, (i * 2 + s) * nq + q + 1)
                        pe.wait_ge(taken, (i * 2 + s) * nq + q + 1)
                        for t in range(Q * q, Q * q + Q):
                            mm = nc.tensor.matmul(k.ps[:, q, (t % Q) * P:(t % Q + 1) * P], b[:, t, :], a[:, t, :],
                                                  start=True, stop=True)
                        mm.then_inc(spread, 1)

        @block.scalar
        def _(act):
            act.sem_inc(taken, nq)
            for s in range(2):
                act.sem_inc(stored[s], 16)
            with act.Fori(0, rounds) as i:
                for s in range(2):
                    act.wait_ge(stored[s], i * 16 + 16)
                    for q in range(nq):
                        act.wait_ge(spread, (i * 2 + s) * nq + nq + q + 1)
                        nc.scalar.activation(G[:, s, :, Q * q:Q * q + Q].rearrange("p n t -> p t n"),
                                             k.bank(q).rearrange("p (t n) -> p t n", t=Q), ACT.Copy).then_inc(taken, 1)


def experts_stage(k, h, y):
    nc = k.nc
    EG = 4
    groups = N_KEYS // EG
    h_hi, h_lo = h
    with ExitStack() as ctx:
        u_raw = k.sb(ctx, "u_raw", [P, EG, KD, P])
        u_hi = k.sb(ctx, "u_hi", [P, 2, KD, P], F32R)
        u_lo = k.sb(ctx, "u_lo", [P, 2, KD, P], F32R)
        v_raw = k.sb(ctx, "v_raw", [P, 2, D_MODEL])
        v_hi = k.sb(ctx, "v_hi", [P, EG, D_MODEL], F32R)
        v_lo = k.sb(ctx, "v_lo", [P, EG, D_MODEL], F32R)
        G = k.sb(ctx, "g", [P, T // TB, EG, TB])
        act_t = k.sb(ctx, "act", [P, 2, T])
        w = k.sb(ctx, "w", [P, T])
        w_hi = k.sb(ctx, "w_hi", [P, EG, T], F32R)
        w_lo = k.sb(ctx, "w_lo", [P, EG, T], F32R)
        u_in = k.sems(ctx, *[f"u_in{e}" for e in range(EG)])
        v_in = k.sems(ctx, "v_in0", "v_in1")
        (g_in, u_rounded, u_parted, v_rounded, v_parted, up, gelued, gated, w_rounded, weighed, down, added,
         cleared) = k.sems(ctx, "g_in", "u_rounded", "u_parted", "v_rounded", "v_parted", "up", "gelued", "gated",
                           "w_rounded", "weighed", "down", "added", "cleared")
        U0, V0, UP0, GE0, WE0, DN0, AD0 = EG, 2, 0, 2, 2, KD, 2
        block = ctx.enter_context(nc.Block())

        @block.sync
        def _(sp):
            with sp.Fori(0, groups) as i:
                for e in range(EG):
                    sp.wait_ge(u_parted, i * EG + e + 1)
                    sp.dma_start(u_raw[:, e].rearrange("p c n -> p (c n)"),
                                 k.d["peer_u"][bass.ds(i * EG + e, 1)].rearrange("o p n -> (o p) n")).then_inc(u_in[e], 16)
                sp.wait_ge(weighed, i * EG + WE0)
                sp.dma_start(G.rearrange("p c e t -> p c (e t)"),
                             k.g_dram.rearrange("c p n -> p c n")[:, :, bass.ds(i * (EG * TB), EG * TB)]).then_inc(g_in, 16)
                for e in range(EG):
                    sp.wait_ge(v_parted, i * EG + e + 1)
                    sp.dma_start(v_raw[:, e % 2],
                                 k.d["peer_v"][bass.ds(i * EG + e, 1)].rearrange("o p n -> (o p) n")).then_inc(v_in[e % 2], 16)

        @block.tensor
        def _(pe):
            pe.sem_inc(down, DN0)
            with pe.Fori(0, groups) as i:
                for e in range(EG):
                    pe.wait_ge(u_parted, i * EG + U0 + e + 1)
                    pe.wait_ge(gelued, i * EG + e + 1)
                    for c in range(KD):
                        for n, (lhs, r) in enumerate(three_passes(u_hi[:, e % 2, c, :], u_lo[:, e % 2, c, :], h_hi, h_lo)):
                            for s in range(2):
                                mm = nc.tensor.matmul(k.bank(2 * (e % 2) + s, TH), lhs, r[:, c, s * TH:(s + 1) * TH],
                                                      start=c == 0 and n == 0, stop=c == KD - 1 and n == 2)
                    mm.then_inc(up, 1)
                pe.wait_ge(v_parted, i * EG + V0 + EG)
                for d in range(KD):
                    pe.wait_ge(added, i * KD + d + 1)
                    for e in range(EG):
                        if d == 0 and e in (0, EG - 1):
                            pe.wait_ge(weighed, i * EG + WE0 + (EG if e else EG - 1))
                        for n, (lhs, r) in enumerate(three_passes(v_hi[:, e, d * P:(d + 1) * P], v_lo[:, e, d * P:(d + 1) * P],
                                                                  w_hi, w_lo)):
                            for s in range(2):
                                mm = nc.tensor.matmul(k.bank(4 + 2 * (d % 2) + s, TH), lhs, r[:, e, s * TH:(s + 1) * TH],
                                                      start=e == 0 and n == 0, stop=e == EG - 1 and n == 2)
                    mm.then_inc(down, 1)

        def parts_ahead(last):
            return () if last else (0, 1)

        @block.scalar
        def _(act):
            def round_u(i, e, first=False):
                act.wait_ge(u_in[e], i * 16 + 16)
                if not first:
                    act.wait_ge(up, i * EG + e - 1)
                nc.scalar.activation(u_hi[:, e % 2], u_raw[:, e], ACT.Copy).then_inc(u_rounded, 1)

            def round_group(i, last):
                for e in range(EG):
                    act.wait_ge(v_in[e % 2], i * 32 + 16 * (e // 2 + 1))
                    act.wait_ge(down, i * KD + DN0)
                    nc.scalar.activation(v_hi[:, e, :], v_raw[:, e % 2, :], ACT.Copy).then_inc(v_rounded, 1)
                    act.wait_ge(up, i * EG + e + 1)
                    act.wait_ge(weighed, i * EG + e + 1)
                    nc.scalar.activation(halves(act_t[:, e % 2, :]), k.pair(2 * (e % 2)), ACT.Gelu_apprx_tanh).then_inc(gelued, 1)
                    if e < EG - 2:
                        round_u(i, e + 2)
                for e in parts_ahead(last):
                    round_u(i + 1, e)

            act.sem_inc(gelued, GE0)
            for e in range(2):
                round_u(0, e, first=True)
            with act.Fori(0, groups - 1) as i:
                round_group(i, False)
            round_group(groups - 1, True)

        @block.vector
        def _(dve):
            def part_u(i, e):
                dve.wait_ge(u_rounded, i * EG + e + 1)
                nc.vector.tensor_tensor(u_lo[:, e % 2], u_raw[:, e], u_hi[:, e % 2].bitcast(F32),
                                        ALU.subtract).then_inc(u_parted, 1)

            def round_group(i, last):
                dve.wait_ge(g_in, i * 16 + 16)
                for e in range(EG):
                    dve.wait_ge(v_rounded, i * EG + e + 1)
                    nc.vector.tensor_tensor(v_lo[:, e, :], v_raw[:, e % 2, :], v_hi[:, e, :].bitcast(F32),
                                            ALU.subtract).then_inc(v_parted, 1)
                    dve.wait_ge(gelued, i * EG + GE0 + e + 1)
                    dve.wait_ge(weighed, i * EG + WE0 + e)
                    nc.vector.tensor_tensor(w.rearrange("p (c t) -> p c t", t=TB),
                                            act_t[:, e % 2, :].rearrange("p (c t) -> p c t", t=TB), G[:, :, e, :],
                                            ALU.mult).then_inc(gated, 1)
                    dve.wait_ge(gated, i * EG + e + 1)
                    nc.vector.tensor_copy(w_hi[:, e, :], w[:]).then_inc(w_rounded, 1)
                    dve.wait_ge(w_rounded, i * EG + e + 1)
                    nc.vector.tensor_tensor(w_lo[:, e, :], w[:], w_hi[:, e, :].bitcast(F32), ALU.subtract).then_inc(weighed, 1)
                    if e < EG - 2:
                        part_u(i, e + 2)
                for e in parts_ahead(last):
                    part_u(i + 1, e)
                for d in range(KD):
                    dve.wait_ge(down, i * KD + DN0 + d + 1)
                    nc.vector.tensor_tensor(halves(y[:, d, :]), k.pair(4 + 2 * (d % 2)), halves(y[:, d, :]),
                                            ALU.add).then_inc(added, 1)

            dve.sem_inc(u_parted, U0)
            dve.sem_inc(v_parted, V0)
            dve.sem_inc(weighed, WE0)
            dve.sem_inc(added, AD0)
            nc.vector.memset(y[:], 0.0).then_inc(cleared, 1)
            dve.wait_ge(cleared, 1)
            for e in range(2):
                part_u(0, e)
            with dve.Fori(0, groups - 1) as i:
                round_group(i, False)
            round_group(groups - 1, True)


def embed_stage(k, h):
    nc = k.nc
    ring = 4
    kt = KD + 2
    with ExitStack() as ctx:
        wt = k.sb(ctx, "wt", [P, ring, kt, P])
        w_hi = k.sb(ctx, "w_hi", [P, 2, KD, P], F32R)
        w_lo = k.sb(ctx, "w_lo", [P, 2, KD, P], F32R)
        p = k.sb(ctx, "p", [P, 2, T])
        sig = k.sb(ctx, "sig", [P, 2, T])
        arrived = k.sems(ctx, *[f"arrived{b}" for b in range(ring)])
        loaded, rounded, parted, multiplied, gated, made, stored, chain = k.sems(
            ctx, "loaded", "rounded", "parted", "multiplied", "gated", "made", "stored", "chain")
        block = ctx.enter_context(nc.Block())

        @block.sync
        def _(sp):
            for n in range(KD):
                if n >= ring:
                    sp.wait_ge(multiplied, n - ring + 1)
                sp.dma_start(wt[:, n % ring].rearrange("p c n -> p (c n)"), k.d["w_ple"][n]).then_inc(arrived[n % ring], 16)
                if n == 0:
                    sp.dma_start(p.rearrange("p c t -> p (c t)"), k.d["p"]).then_inc(loaded, 16)
            for n in range(KD):
                sp.wait_ge(made, n + 1)
                sp.dma_start(k.d["out_y"][n], k.x[:, n, :]).then_inc(stored, 16)
            sp.wait_ge(stored, 16 * KD)

        @block.tensor
        def _(pe):
            pe.wait_ge(loaded, 16)
            for n in range(KD):
                pe.wait_ge(parted, n + 1)
                if n >= 2:
                    pe.wait_ge(made, n - 1)
                for c in range(KD):
                    for m, (lhs, r) in enumerate(three_passes(w_hi[:, n % 2, c, :], w_lo[:, n % 2, c, :], *h)):
                        for s in range(2):
                            mm = nc.tensor.matmul(k.bank(4 * (n % 2) + s, TH), lhs, r[:, c, s * TH:(s + 1) * TH],
                                                  start=c == 0 and m == 0, stop=c == KD - 1 and m == 2)
                for c in range(2):
                    for s in range(2):
                        mm = nc.tensor.matmul(k.bank(4 * (n % 2) + 2 + s, TH), wt[:, n % ring, KD + c, :],
                                              p[:, c, s * TH:(s + 1) * TH], start=c == 0, stop=c == 1)
                mm.then_inc(multiplied, 1)

        @block.scalar
        def _(act):
            for n in range(KD + 1):
                if n < KD:
                    act.wait_ge(arrived[n % ring], 16 * (n // ring + 1))
                    if n >= 2:
                        act.wait_ge(multiplied, n - 1)
                    nc.scalar.activation(w_hi[:, n % 2], wt[:, n % ring, 0:KD, :], ACT.Copy).then_inc(rounded, 1)
                if n:
                    act.wait_ge(multiplied, n)
                    if n >= 3:
                        act.wait_ge(made, n - 2)
                    nc.scalar.activation(halves(sig[:, (n - 1) % 2, :]), k.pair(4 * ((n - 1) % 2)), ACT.Sigmoid).then_inc(gated, 1)

        @block.vector
        def _(dve):
            ch = Chain(dve, chain)
            for n in range(KD + 1):
                if n < KD:
                    dve.wait_ge(rounded, n + 1)
                    nc.vector.tensor_tensor(w_lo[:, n % 2], wt[:, n % ring, 0:KD, :], w_hi[:, n % 2].bitcast(F32),
                                            ALU.subtract).then_inc(parted, 1)
                if n:
                    m = n - 1
                    dve.wait_ge(gated, m + 1)
                    ch.link(nc.vector.tensor_tensor(halves(sig[:, m % 2, :]), halves(sig[:, m % 2, :]),
                                                    k.pair(4 * (m % 2) + 2), ALU.mult))
                    nc.vector.tensor_tensor(k.x[:, m, :], k.x[:, m, :], sig[:, m % 2, :], ALU.add).then_inc(made, 1)


def add_stage(k, y):
    nc = k.nc
    with ExitStack() as ctx:
        added, = k.sems(ctx, "added")
        block = ctx.enter_context(nc.Block())

        @block.vector
        def _(dve):
            nc.vector.tensor_tensor(k.x[:], k.x[:], y[:, :, :], ALU.add).then_inc(added, 1)
            dve.wait_ge(added, 1)


def layer_program(nc, d, n_phys, last=99):
    k = Core(nc)
    k.d, k.n_phys = d, n_phys
    with ExitStack() as whole:
        k.ps = whole.enter_context(nc.psum_tensor("ps", [P, 8, 512], F32))
        k.x = k.sb(whole, "x", [P, KD, T])
        k.params = k.sb(whole, "params", [P, NPARAM])
        k.ones = k.sb(whole, "ones", [P, P])
        k.blocks = k.sb(whole, "blocks", [P, P])
        k.ident = k.sb(whole, "ident", [P, P])
        k.gates = k.sb(whole, "gates", [P, 5, NGATE])
        k.table = k.sb(whole, "table", [1, DEC_BATCH * PAGES], mybir.dt.int32)
        load_stage(k)
        with ExitStack() as mixing:
            k.z = k.sb(mixing, "z", [P, NZ, T])
            k.r = Tiles()
            k.r.o = k.z[:, 4:8, :]
            with ExitStack() as ctx:
                h = [k.sb(ctx, name, [P, KD, T], F32R) for name in ("h_hi", "h_lo")]
                wg = k.sb(ctx, "wg", [P, KD, NGATE])
                norm_stage(k, "attn_norm", *h)
                project_stage(k, d["w_in"], NZ, h, k.z, gates=(d["w_gates"], wg, k.gates))
            with ExitStack() as ctx:
                xs = k.sb(ctx, "xs", [P, RCOLS, T])
                k.r.kt, k.r.bt, k.r.bonus, k.r.g = (k.sb(ctx, name, [P, 4, T]) for name in ("kt", "bt", "bonus", "g"))
                k.r.ends = k.sb(ctx, "ends", [P, 4, NCH + DEC_BATCH])
                k.r.xs, k.r.rt, k.r.ht, k.r.vt = xs, xs[:, 0:4, :], xs[:, 4:8, :], xs[:, 8:12, :]
                rwkv_prepare_stage(k)
                rwkv_chunks_stage(k, sample=False)
                rwkv_chunks_stage(k, sample=True)
                rwkv_finish_stage(k)
            k.on = k.sb(mixing, "on", [P, 4, T])
            with ExitStack() as ctx:
                k.qr = k.sb(ctx, "qr", [P, 4, T])
                k.vs = k.sb(ctx, "vs", [P, 5, P])
                k.vw = k.sb(ctx, "vw", [P, 5, P])
                k.kc = k.sb(ctx, "kc", [P, DEC_BATCH, CH])
                k.vc = k.sb(ctx, "vc", [CH, DEC_BATCH, P])
                k.kcp = k.sb(ctx, "kcp", [P, 32])
                k.vcp = k.sb(ctx, "vcp", [32, P])
                compress_stage(k)
                nsa_prepare_stage(k)
                prompt_attention_stage(k)
                sample_attention_stage(k)
            k.zg = k.sb(mixing, "zg", [P, 2 * KD, T])
            with ExitStack() as ctx:
                h = [k.sb(ctx, name, [P, KD, T], F32R) for name in ("h_hi", "h_lo")]
                norm_stage(k, "attn_norm", *h)
                project_stage(k, d["w_zg"], 2 * KD, h, k.zg)
            with ExitStack() as ctx:
                m = [k.sb(ctx, name, [P, KD, T], F32R) for name in ("m_hi", "m_lo")]
                merge_stage(k, *m)
                project_stage(k, d["w_out"], KD, m, k.z[:, 8:16, :])
                add_stage(k, k.z[:, 8:16, :])
        k.clear_sems()
        k.g_dram = nc.dram_tensor("gate_matrix", (T // TB, P, N_KEYS * TB), F32).ap()
        with ExitStack() as ffn:
            h = [k.sb(ffn, name, [P, KD, T], F32R) for name in ("h_hi", "h_lo")]
            norm_stage(k, "ffn_norm", *h)
            with ExitStack() as ctx:
                picked = k.sb(ctx, "picked", [P, 3, T])
                q = k.sb(ctx, "q", [P, KD, T])
                project_stage(k, d["peer_wq"], KD, h, q)
                choose_stage(k, q, picked)
                gate_matrix_stage(k, picked)
            with ExitStack() as ctx:
                y = k.sb(ctx, "y", [P, KD, T])
                experts_stage(k, h, y)
                add_stage(k, y)
            norm_stage(k, "ple_norm", *h)
            embed_stage(k, h)



def _tiles(w):
    kk, n = w.shape
    return w.reshape(kk // P, P, n // P, P).transpose(2, 1, 0, 3).reshape(n // P, P, kk // P * P)


def _rows(w):
    c, t = w.shape
    return w.reshape(c // P, P, t).transpose(1, 0, 2).reshape(P, c // P * t)


def _constants():
    f = np.float32
    out = {}
    out["ones"] = np.ones((P, P), f)
    out["blocks"] = np.kron(np.eye(2), np.ones((HD, HD))).astype(f)
    out["ident"] = np.eye(P, dtype=f)
    keep = np.ones((P, T), f)
    keep[:, 0:SEQ:CH] = 0
    keep[:, SEQ::DEC_SEQ] = 0
    out["keep"] = keep
    t = np.arange(CH)
    t2 = np.tile(t, 2)
    masks = []
    for inner, outer in ((16, CH), (DEC_SEQ, DEC_SEQ)):
        near = t[:, None] // inner == t[None, :] // inner
        within = t[:, None] // outer == t[None, :] // outer
        lower = t[:, None] > t[None, :]
        masks += [-1.0 * (near & lower), -1.0 * (near & lower.T), -1.0 * (within & ~near & lower),
                  1.0 * (within & lower.T), 1.0 * (within & ~lower), -1.0 * (within & ~lower)]
    out["masks"] = np.stack(masks, 1).reshape(CH, 12 * CH).astype(f)
    out["masks"] = np.tile(out["masks"], (2, 1))
    out["ident2"] = np.tile(np.eye(CH, dtype=f), (2, 1))
    out["seqmask"] = (t2[:, None] // DEC_SEQ == np.arange(DEC_BATCH)[None, :]).astype(f)
    pos = np.concatenate([np.arange(SEQ), np.tile(PAST + np.arange(DEC_SEQ), DEC_BATCH)]).astype(f)
    half = HD // 2
    inv = np.power(f(10000.0), -np.arange(half, dtype=f) / f(half)).astype(f)
    ang = (pos[None, :] * inv[:, None]).astype(f).astype(np.float64)
    out["rope"] = np.concatenate([np.tile(np.cos(ang), (4, 1)), np.tile(np.sin(ang), (4, 1))], 1).astype(f)
    rot = np.zeros((P, P), f)
    for base in range(0, P, HD):
        for j in range(half):
            rot[base + half + j, base + j] = -1
            rot[base + j, base + half + j] = 1
    out["rot"] = rot
    q = np.arange(P)
    out["tri"] = np.where(q[:, None] >= q[None, :], 0, NEG).astype(f)
    n = np.arange(32)
    cm = [np.where((CMP_STRIDE * n[None, :] + 31 <= qt * P + q[:, None]) & (n[None, :] < 31), 0, NEG) for qt in range(4)]
    out["cmask"] = np.concatenate(cm, 1).astype(f)
    row = np.arange(P)
    rs, rkv, ri, rt = row // 64, row // 32 % 2, row // 8 % 4, row % 8
    col = np.arange(TS)
    out["newmask"] = np.concatenate([np.where((col[None, :] // 8 == 2 * g + rs[:, None]) & (col[None, :] % 8 <= rt[:, None]),
                                              0, NEG) for g in range(4)], 1).astype(f)
    out["winmask"] = np.where(np.arange(8)[None, :] <= rt[:, None], NEG, 0).astype(f)
    out["pick"] = np.concatenate([col[:, None] == (8 * (2 * g + rs) + rt)[None, :] for g in range(4)], 1).astype(f)
    out["headmask"] = (np.arange(NGATE)[None, :] // 3 == (4 * rkv + ri)[:, None]).astype(f)
    key = rs * 100 + rkv * 10 + rt
    out["same"] = (key[:, None] == key[None, :]).astype(f)
    out["iota14"] = np.tile(np.arange(1, 15, dtype=f), (P, 1))
    out["iota16"] = np.tile(np.arange(16, dtype=f), (P, 1))
    out["iota128"] = np.tile(np.arange(128, dtype=f), (P, 1))
    return out


def _lay_out(x_prompt, x_sample, cache_cmp_kv, cache_sel_kv, state_win_kv, state_wkv, state_shift, page_table,
             p_prompt, p_sample, attn_norm, w_in, rwkv_mu, rwkv_w0, rwkv_w_up, rwkv_a0, rwkv_a_up, rwkv_g_up,
             rwkv_k_k, rwkv_k_a, rwkv_r_k, rwkv_gn_w, rwkv_gn_b, w_rwkv_out, q_norm, k_norm, cmp_pe, cmp_w1,
             cmp_w2, w_nsa_out, w_out, ffn_norm, peer_wq, peer_keys, peer_u, peer_v, ple_norm, ple_w_gate, ple_w_in):
    d = _constants()
    n_phys = cache_cmp_kv.shape[1]
    d["x"] = _rows(np.concatenate([x_prompt[0], x_sample.reshape(TS, D_MODEL)], 0).T)
    d["p"] = _rows(np.concatenate([p_prompt[0, 0], p_sample[0].reshape(TS, PLE)], 0).T)
    params = dict(attn_norm=attn_norm[0], ffn_norm=ffn_norm[0], ple_norm=ple_norm[0], mu=rwkv_mu[0], w0=rwkv_w0[0],
                  a0=rwkv_a0[0], k_k=rwkv_k_k[0], k_a=rwkv_k_a[0], r_k=rwkv_r_k[0].reshape(-1), gn_w=rwkv_gn_w[0],
                  gn_b=rwkv_gn_b[0], q_norm=np.tile(q_norm[0], 2), k_norm=np.tile(k_norm[0], (1, 2)).reshape(-1))
    d["params"] = np.concatenate([params[n].reshape(-1, P).T for n in PARAMS], 1)
    order = np.concatenate([np.r_[i * HD:(i + 1) * HD, (4 + i) * HD:(5 + i) * HD] for i in range(4)])
    r0 = RCOLS * P
    kv_end = r0 + 512 + 6 * P
    w = w_in[0]
    d["w_in"] = _tiles(np.concatenate([w[:, :r0], w[:, r0:r0 + 512][:, order], w[:, r0 + 512:kv_end]], 1))
    d["w_zg"] = _tiles(w[:, kv_end + NGATE:])
    d["w_gates"] = _rows(w[:, kv_end:kv_end + NGATE])
    d["up"] = np.concatenate([np.concatenate([rwkv_w_up[0], rwkv_a_up[0]], 0), rwkv_g_up[0]], 1)
    d["shift"] = _rows(state_shift[0].T)
    d["states"] = state_wkv[0].reshape(DEC_BATCH, 4, 2, HD, HD).transpose(2, 4, 1, 0, 3).reshape(P, -1)
    pages = cache_cmp_kv[0].reshape(n_phys, 8, 8, 2, 2, 2, HD)
    d["cmp_pages"] = pages.transpose(0, 3, 6, 2, 4, 5, 1).reshape(n_phys, P, 256)
    sel = cache_sel_kv[0].reshape(n_phys, PAGE, 2, P)
    d["sel_pages"] = np.concatenate([sel[:, :, 0].transpose(0, 2, 1), sel[:, :, 1]], 2)
    win = state_win_kv[0].reshape(DEC_BATCH // 2, 2, WINDOW, 2, P)
    d["win_k"] = win[:, :, :, 0].transpose(0, 3, 1, 2).reshape(4, P, 2 * WINDOW)
    d["win_v"] = win[:, :, :, 1].reshape(4, 2, 4, P, P).transpose(0, 3, 1, 2, 4).reshape(4, P, 2 * 4 * P)
    d["win_rows"] = state_win_kv[0][:, DEC_SEQ:].reshape(DEC_BATCH, -1)
    d["page_table"] = page_table.reshape(1, -1)
    d["cmp_w1"] = cmp_w1[0].reshape(2, 2, 8, 2, HD, CMP_HIDDEN).transpose(3, 4, 2, 0, 1, 5).reshape(P, -1)
    d["cmp_pe"] = cmp_pe[0].reshape(2, 2, 8, 2, HD).transpose(3, 4, 2, 0, 1).reshape(P, -1)
    d["cmp_w2"] = cmp_w2[0].reshape(2, 2, P, HD).transpose(2, 0, 1, 3).reshape(P, -1)
    d["w_merge"] = np.concatenate([_tiles(w_rwkv_out[0]), _tiles(w_nsa_out[0][order])], 2)
    d["w_out"] = _tiles(w_out[0])
    d["peer_wq"] = _tiles(peer_wq[0])
    d["keys"] = peer_keys[0].transpose(1, 3, 0, 2).reshape(P, -1)
    d["peer_u"] = peer_u[0].reshape(N_KEYS, P, KD, P).transpose(0, 3, 2, 1).reshape(N_KEYS, P, KD * P)
    d["peer_v"] = peer_v[0].reshape(N_KEYS, P, D_MODEL)
    d["w_ple"] = np.concatenate([_tiles(ple_w_gate[0]), _tiles(ple_w_in[0])], 2)
    return {n: np.ascontiguousarray(a) for n, a in d.items()}, n_phys


_OUTS = dict(out_y=(KD, P, T), out_kv=(P, 6 * T), out_win=(DEC_BATCH, (WINDOW - DEC_SEQ) * 2 * P),
             out_state=(P, 4 * HD), out_states=(P, 4 * DEC_BATCH * HD), out_shift=(P, RCOLS * 9))


def kernel(**inputs):
    import concourse.bacc as _bacc
    from concourse import mybir as _mybir
    from concourse.bass_utils import run_bass_kernel_spmd as _run

    arrays, n_phys = _lay_out(**{n: np.asarray(a) for n, a in inputs.items()})
    nc = _bacc.Bacc("TRN2", target_bir_lowering=False, num_devices=1)
    d = {n: nc.dram_tensor(f"in_{n}", a.shape, _mybir.dt.from_np(a.dtype), kind="ExternalInput").ap()
         for n, a in arrays.items()}
    for n, shape in _OUTS.items():
        d[n] = nc.dram_tensor(n, shape, F32, kind="ExternalOutput").ap()
    layer_program(nc, d, n_phys)
    r = _run(nc, [{f"in_{n}": a for n, a in arrays.items()}], core_ids=[0]).results[0]

    y = r["out_y"].reshape(D_MODEL, T).T
    kv = r["out_kv"].reshape(2, HD, 3, 2, T).transpose(2, 4, 3, 0, 1)
    prompt = [np.ascontiguousarray(kv[b, :SEQ])[None, None] for b in range(3)]
    new = [np.ascontiguousarray(kv[b, SEQ:]).reshape(1, DEC_BATCH, DEC_SEQ, 2, 2, HD) for b in range(3)]
    win = np.concatenate([r["out_win"].reshape(1, DEC_BATCH, WINDOW - DEC_SEQ, 2, 2, HD), new[2]], 2)
    state = r["out_state"].reshape(2, HD, 4, HD).transpose(2, 0, 3, 1).reshape(1, 1, HEADS, HD, HD)
    states = r["out_states"].reshape(2, HD, 4, DEC_BATCH, HD).transpose(3, 2, 0, 4, 1).reshape(1, DEC_BATCH, HEADS, HD, HD)
    shift = r["out_shift"].reshape(P, RCOLS, 9).transpose(2, 1, 0).reshape(9, RCOLS * P)
    out = (y[:SEQ][None], y[SEQ:].reshape(DEC_BATCH, DEC_SEQ, D_MODEL), prompt[0], new[0], prompt[1], new[1],
           prompt[2], win, state, states, shift[None, 0:1], shift[None, 1:])
    return tuple(np.ascontiguousarray(a) for a in out)
```

```python
from contextlib import ExitStack

import numpy as np

import concourse.bass as bass
from concourse import mybir

ALU = mybir.AluOpType
ACT = mybir.ActivationFunctionType
AX = mybir.AxisListType
F32 = mybir.dt.float32
F32R = mybir.dt.float32r
U32 = mybir.dt.uint32

P = 128
D_MODEL = 1024
KD = D_MODEL // P
SEQ = 512
DEC_BATCH = 8
DEC_SEQ = 8
TS = DEC_BATCH * DEC_SEQ
T = SEQ + TS
TH = T // 2
PAST = 1024
PAGE = 128
PAGES = PAST // PAGE
HD = 64
HEADS = 8
RCOLS = 14
ZQ = 14
ZK = 18
NZ = 24
NGATE = 24
CMP_STRIDE = 16
CMP_HIDDEN = 256
SEL_BLOCK = 64
WINDOW = 512
CH = 64
TB = 32
NCH = SEQ // CH
N_KEYS = 128
TOPK = 16
PLE = 256
EPS = 1e-6
GN_EPS = 64e-5
DECAY = float(np.exp(-0.5))
SCALE = HD ** -0.5
NEG = -1e30

PARAMS = {}
for _name, _n in (("attn_norm", KD), ("ffn_norm", KD), ("ple_norm", KD), ("mu", RCOLS), ("w0", 4), ("a0", 4),
                  ("k_k", 4), ("k_a", 4), ("r_k", 4), ("gn_w", 4), ("gn_b", 4), ("q_norm", 1), ("k_norm", 3)):
    PARAMS[_name] = (sum(n for _, n in PARAMS.values()), _n)
NPARAM = sum(n for _, n in PARAMS.values())


class Tiles:
    pass


class Chain:

    def __init__(self, eng, sem, base=0):
        self.eng, self.sem, self.base, self.n = eng, sem, base, 0

    def link(self, ins):
        self.n += 1
        ins.then_inc(self.sem, 1)
        self.eng.wait_ge(self.sem, self.base + self.n)


class Steps:

    def __init__(self, sem, names, base=0):
        self.sem, self.names, self.base = sem, names.split(), base

    def at(self, name, i=0):
        return i * len(self.names) + self.base + self.names.index(name) + 1

    def before(self, i):
        return i * len(self.names) + self.base


class Core:

    def __init__(self, nc):
        self.nc = nc
        self.n = 0
        self.used = []

    def sb(self, ctx, name, shape, dt=F32):
        self.n += 1
        return ctx.enter_context(self.nc.sbuf_tensor(f"{name}_{self.n}", shape, dt))

    def sems(self, ctx, *names):
        self.n += 1
        made = [ctx.enter_context(self.nc.semaphore(f"{n}_{self.n}")) for n in names]
        self.used += made
        return made

    def clear_sems(self):
        numbers = sorted({s.num for s in self.used})
        self.used = []
        with self.nc.Block() as block:
            @block.gpsimd
            def _(pool):
                at = 0
                while at < len(numbers):
                    end = at + 1
                    while end < len(numbers) and numbers[end] == numbers[end - 1] + 1:
                        end += 1
                    pool.sem_clear(range(numbers[at], numbers[end - 1] + 1))
                    at = end

    def par(self, name, i=0, lo=0, hi=P):
        at, n = PARAMS[name]
        return self.params[lo:hi, at + i:at + i + 1]

    def bank(self, b, n=512):
        return self.ps[:, b, 0:n]

    def pair(self, b):
        return self.ps[:, b:b + 2, 0:TH]


def halves(ap):
    return ap.rearrange("p (h t) -> p h t", h=2)


def load_stage(k):
    nc = k.nc
    with ExitStack() as ctx:
        loaded, = k.sems(ctx, "loaded")
        pairs = [(k.x, k.d["x"]), (k.params, k.d["params"]), (k.ones, k.d["ones"]), (k.blocks, k.d["blocks"]),
                 (k.ident, k.d["ident"]), (k.gather, k.d["gather"]), (k.spread, k.d["spread"]), (k.table, k.d["page_table"])]
        block = ctx.enter_context(nc.Block())

        @block.sync
        def _(sp):
            for dst, src in pairs:
                sp.dma_start(dst[:] if len(dst.shape) == 2 else dst.rearrange("p c t -> p (c t)"), src).then_inc(loaded, 16)
            sp.wait_ge(loaded, 16 * len(pairs))


class WeightRing:
    SIZE = 4

    def __init__(self, k, ctx, w, rows=KD):
        self.w = w
        self.tiles = k.sb(ctx, "wt", [P, self.SIZE, rows, P])
        self.arrived = k.sems(ctx, *[f"arrived{b}" for b in range(self.SIZE)])

    def load(self, sp, n, b):
        sp.dma_start(self.tiles[:, b].rearrange("p c n -> p (c n)"), self.w[n]).then_inc(self.arrived[b], 16)

    def load_first(self, sp):
        for b in range(self.SIZE):
            self.load(sp, b, b)


def norm_stage(k, gain, hi, lo, ring=None, rs=None, again=False):
    nc = k.nc
    with ExitStack() as ctx:
        sq = k.sb(ctx, "sq", [P, KD, T])
        rs = k.sb(ctx, "rs", [P, T]) if rs is None else rs
        squared, summed, mean, rooted, chain, normed, rounded = k.sems(ctx, "squared", "summed", "mean", "rooted", "chain",
                                                                       "normed", "rounded")
        block = ctx.enter_context(nc.Block())

        @block.sync
        def _(sp):
            if ring is not None:
                ring.load_first(sp)

        @block.scalar
        def _(act):
            if not again:
                for c in range(KD):
                    nc.scalar.activation(sq[:, c, :], k.x[:, c, :], ACT.Square).then_inc(squared, 1)
                act.wait_ge(mean, 1)
                nc.scalar.activation(rs[:], rs[:], ACT.Sqrt).then_inc(rooted, 1)
            for c in range(KD):
                act.wait_ge(normed, c + 1)
                nc.scalar.activation(hi[:, c, :], sq[:, c, :], ACT.Copy).then_inc(rounded, 1)

        @block.tensor
        def _(pe):
            if not again:
                for c in range(KD):
                    pe.wait_ge(squared, c + 1)
                    for h in range(2):
                        mm = nc.tensor.matmul(k.bank(h, TH), k.ones[:], sq[:, c, h * TH:(h + 1) * TH],
                                              start=c == 0, stop=c == KD - 1)
                mm.then_inc(summed, 1)

        @block.vector
        def _(dve):
            ch = Chain(dve, chain)
            if not again:
                dve.wait_ge(summed, 1)
                nc.vector.tensor_scalar(halves(rs[:]), k.pair(0), 1.0 / D_MODEL, EPS, ALU.mult, ALU.add).then_inc(mean, 1)
                dve.wait_ge(rooted, 1)
                ch.link(nc.vector.reciprocal(rs[:], rs[:]))
            for c in range(KD):
                nc.vector.scalar_tensor_tensor(out=sq[:, c, :], in0=k.x[:, c, :], scalar=k.par(gain, c),
                                               in1=rs[:], op0=ALU.mult, op1=ALU.mult).then_inc(normed, 1)
            for c in range(KD):
                dve.wait_ge(rounded, c + 1)
                last = nc.vector.tensor_tensor(lo[:, c, :], sq[:, c, :], hi[:, c, :].bitcast(F32), ALU.subtract)
            ch.link(last)


def gather_heads(k, tiles):
    for n, tile in enumerate(tiles):
        for h in range(2):
            mm = k.nc.tensor.matmul(k.bank(h, TH), k.gather[:, n, :], tile[:, h * TH:(h + 1) * TH], start=n == 0,
                                    stop=n == len(tiles) - 1)
    return mm


def spread_heads(k, rows, count):
    for n in range(count):
        for h in range(2):
            mm = k.nc.tensor.matmul(k.bank(2 * n + h, TH), k.spread[:, n, :], rows[:, h * TH:(h + 1) * TH],
                                    start=True, stop=True)
    return mm


def three_passes(w_hi, w_lo, r_hi, r_lo):
    return (w_hi, r_hi), (w_hi, r_lo), (w_lo, r_hi)


def project_stage(k, weights, ntiles, rhs, dst, gates=None):
    nc = k.nc
    ring, wt, arrived = weights.SIZE, weights.tiles, weights.arrived
    r_hi, r_lo = rhs
    with ExitStack() as ctx:
        w_hi = k.sb(ctx, "w_hi", [P, 2, KD, P], F32R)
        w_lo = k.sb(ctx, "w_lo", [P, 2, KD, P], F32R)
        rounded, parted, multiplied, taken, gate_w, gate_mm = k.sems(ctx, "rounded", "parted", "multiplied", "taken",
                                                                     "gate_w", "gate_mm")
        block = ctx.enter_context(nc.Block())

        @block.sync
        def _(sp):
            if gates is not None:
                sp.dma_start(gates[1].rearrange("p c n -> p (c n)"), gates[0]).then_inc(gate_w, 16)
            with sp.Fori(0, ntiles // ring - 1) as i:
                for b in range(ring):
                    sp.wait_ge(parted, i * ring + ring + b + 1)
                    weights.load(sp, i * ring + ring + b, b)

        @block.vector
        def _(dve):
            dve.sem_inc(parted, ring)
            with dve.Fori(0, ntiles // ring) as i:
                for b in range(ring):
                    dve.wait_ge(arrived[b], i * 16 + 16)
                    dve.wait_ge(multiplied, i * ring + b + 1)
                    nc.vector.tensor_copy(w_hi[:, b % 2], wt[:, b]).then_inc(rounded, 1)
                    dve.wait_ge(rounded, i * ring + b + 1)
                    nc.vector.tensor_tensor(w_lo[:, b % 2], wt[:, b], w_hi[:, b % 2].bitcast(F32),
                                            ALU.subtract).then_inc(parted, 1)

        @block.tensor
        def _(pe):
            pe.sem_inc(multiplied, 2)
            with pe.Fori(0, ntiles // ring) as i:
                for b in range(ring):
                    pe.wait_ge(parted, i * ring + ring + b + 1)
                    pe.wait_ge(taken, i * ring + b + 1)
                    for c in range(KD):
                        for n, (lhs, r) in enumerate(three_passes(w_hi[:, b % 2, c, :], w_lo[:, b % 2, c, :], r_hi, r_lo)):
                            for h in range(2):
                                mm = nc.tensor.matmul(k.bank(2 * b + h, TH), lhs, r[:, c, h * TH:(h + 1) * TH],
                                                      start=c == 0 and n == 0, stop=c == KD - 1 and n == 2)
                    mm.then_inc(multiplied, 1)
            if gates is not None:
                pe.wait_ge(gate_w, 16)
                pe.wait_ge(taken, ntiles + ring)
                for tt in range(5):
                    n = min(P, T - tt * P)
                    for c in range(KD):
                        for r in (r_hi, r_lo):
                            mm = nc.tensor.matmul(k.ps[0:n, 0, tt * NGATE:(tt + 1) * NGATE],
                                                  r[:, c, tt * P:tt * P + n].bitcast(F32), gates[1][:, c, :],
                                                  start=c == 0 and r is r_hi, stop=c == KD - 1 and r is r_lo)
                mm.then_inc(gate_mm, 1)

        @block.scalar
        def _(act):
            act.sem_inc(taken, ring)
            with act.Fori(0, ntiles // ring) as i:
                for b in range(ring):
                    act.wait_ge(multiplied, i * ring + b + 3)
                    out = dst[:, bass.ds(i * 4 + b, 1), :].rearrange("p o (h t) -> p (o h) t", h=2)
                    nc.scalar.activation(out, k.pair(2 * b), ACT.Copy).then_inc(taken, 1)
            if gates is not None:
                act.wait_ge(gate_mm, 1)
                nc.scalar.activation(gates[2][:, 0:4, :].rearrange("p a n -> p (a n)"), k.ps[:, 0, 0:4 * NGATE],
                                     ACT.Sigmoid)
                nc.scalar.activation(gates[2][0:TS, 4, :], k.ps[0:TS, 0, 4 * NGATE:5 * NGATE], ACT.Sigmoid)


def rwkv_prepare_stage(k):
    nc = k.nc
    Z, r = k.z, k.r
    with ExitStack() as ctx:
        xs = r.xs
        last9 = k.sb(ctx, "last9", [P, RCOLS, 9])
        prev = k.sb(ctx, "prev", [P, RCOLS, DEC_BATCH])
        up = k.sb(ctx, "up", [P, 2, 512])
        keep = k.sb(ctx, "keep", [P, T])
        norms = k.sb(ctx, "norms", [P, T])
        V = Steps(None, "last shifted_low shifted keys2 cum a_used inverted normed prods bonus done")
        S = Steps(None, "low sw aa gg rooted decays")
        E = Steps(None, "w a g keysum unit bonussum")
        v_at, s_at, e_at, loaded, stored, chain, schain = k.sems(ctx, "dve_step", "act_step", "pe_step", "loaded",
                                                                "stored", "chain", "schain")
        sw, cum, tmp = Z[:, 0:4, :], Z[:, 4:8, :], Z[:, 8:12, :]
        kk = r.kt
        block = ctx.enter_context(nc.Block())

        @block.sync
        def _(sp):
            sp.dma_start(prev.rearrange("p c s -> p (c s)"), k.d["shift"]).then_inc(loaded, 16)
            sp.dma_start(up.rearrange("p c s -> p (c s)"), k.d["up"]).then_inc(loaded, 16)
            sp.dma_start(keep[:], k.d["keep"]).then_inc(loaded, 16)
            sp.wait_ge(v_at, V.at("last"))
            sp.dma_start(k.d["out_shift"], last9.rearrange("p c s -> p (c s)")).then_inc(stored, 16)
            sp.wait_ge(stored, 16)

        @block.vector
        def _(dve):
            ch = Chain(dve, chain)
            nc.vector.tensor_copy(last9[:], Z[:, 0:RCOLS, SEQ - 1:T:DEC_SEQ]).then_inc(v_at, 1)
            nc.vector.tensor_scalar(xs[:, :, 0:1], Z[:, 0:RCOLS, 0:1], -1.0, None, ALU.mult)
            ch.link(nc.vector.tensor_tensor(xs[:, :, 1:T], Z[:, 0:RCOLS, 0:T - 1], Z[:, 0:RCOLS, 1:T], ALU.subtract))
            dve.wait_ge(loaded, 48)
            ch.link(nc.vector.tensor_tensor(xs[:, :, SEQ:T:DEC_SEQ], prev[:], Z[:, 0:RCOLS, SEQ:T:DEC_SEQ], ALU.subtract))
            for n in (12, 13, *range(12)):
                ins = nc.vector.scalar_tensor_tensor(out=xs[:, n, :], in0=xs[:, n, :], scalar=k.par("mu", n),
                                                     in1=Z[:, n, :], op0=ALU.mult, op1=ALU.add)
                if n == 13:
                    ins.then_inc(v_at, 1)
            ins.then_inc(v_at, 1)
            dve.wait_ge(v_at, V.at("shifted"))
            for n in range(4):
                last = nc.vector.tensor_scalar(kk[:, n, :], xs[:, 4 + n, :], k.par("k_k", n), None, ALU.mult)
            ch.link(last)
            nc.vector.tensor_tensor(tmp, kk[:], kk[:], ALU.mult).then_inc(v_at, 1)
            dve.wait_ge(s_at, S.at("sw"))
            for n in range(4):
                last = nc.vector.tensor_tensor_scan(cum[:, n, :], keep[:], sw[:, n, :], 0.0, ALU.mult, ALU.add)
            ch.link(last)
            nc.vector.tensor_tensor(sw, cum, sw, ALU.subtract).then_inc(v_at, 1)
            dve.wait_ge(s_at, S.at("aa"))
            for n in range(4):
                last = nc.vector.tensor_scalar(r.bonus[:, n, :], r.bt[:, n, :], -1.0, k.par("k_a", n), ALU.add, ALU.mult)
            ch.link(last)
            nc.vector.scalar_tensor_tensor(out=r.ht, in0=r.bonus[:], scalar=1.0, in1=xs[:, 4:8, :],
                                           op0=ALU.add, op1=ALU.mult).then_inc(v_at, 1)
            dve.wait_ge(s_at, S.at("rooted"))
            ch.link(nc.vector.tensor_scalar(norms[:], norms[:], 1e-12, None, ALU.max))
            nc.vector.reciprocal(norms[:], norms[:]).then_inc(v_at, 1)
            dve.wait_ge(e_at, E.at("unit"))
            for n in range(4):
                last = nc.vector.tensor_tensor(halves(kk[:, n, :]), k.pair(2 * n), halves(kk[:, n, :]), ALU.mult)
            ch.link(last)
            nc.vector.tensor_tensor(r.bt[:], r.bt[:], kk[:], ALU.mult).then_inc(v_at, 1)
            dve.wait_ge(v_at, V.at("normed"))
            for n in range(4):
                last = nc.vector.scalar_tensor_tensor(out=tmp[:, n, :], in0=xs[:, n, :], scalar=k.par("r_k", n),
                                                      in1=r.ht[:, n, :], op0=ALU.mult, op1=ALU.mult)
            last.then_inc(v_at, 1)
            dve.wait_ge(e_at, E.at("bonussum"))
            for n in range(4):
                last = nc.vector.tensor_tensor(halves(r.bonus[:, n, :]), k.pair(2 * n), halves(xs[:, 8 + n, :]), ALU.mult)
            last.then_inc(v_at, 1)
            dve.wait_ge(s_at, S.at("decays"))
            nc.vector.tensor_copy(r.ends[:, :, 0:NCH], tmp[:, :, CH - 1:SEQ:CH])
            nc.vector.tensor_copy(r.ends[:, :, NCH:], tmp[:, :, SEQ + DEC_SEQ - 1:T:DEC_SEQ])
            nc.vector.tensor_tensor(r.rt, r.rt, tmp, ALU.mult)
            nc.vector.tensor_tensor(kk[:], kk[:], sw, ALU.mult)
            nc.vector.tensor_tensor(r.bt[:], r.bt[:], cum, ALU.mult)
            nc.vector.tensor_tensor(r.ht, r.ht, cum, ALU.mult).then_inc(v_at, 1)
            dve.wait_ge(v_at, V.at("done"))

        @block.scalar
        def _(act):
            act.wait_ge(v_at, V.at("shifted_low"))
            nc.scalar.activation(xs[0:64, 12, :], xs[0:64, 12, :], ACT.Tanh)
            nc.scalar.activation(xs[:, 13, :], xs[:, 13, :], ACT.Sigmoid).then_inc(s_at, 1)
            act.wait_ge(v_at, V.at("shifted"))
            for name, dst, bias in (("w", sw, "w0"), ("a", r.bt, "a0"), ("g", r.g, None)):
                act.wait_ge(e_at, E.at(name))
                for n in range(4):
                    if bias:
                        last = nc.scalar.activation(halves(dst[:, n, :]), k.pair(2 * n), ACT.Sigmoid, bias=k.par(bias, n))
                    else:
                        last = nc.scalar.activation(halves(dst[:, n, :]), k.pair(2 * n), ACT.Copy)
                last.then_inc(s_at, 1)
            act.wait_ge(e_at, E.at("keysum"))
            nc.scalar.activation(halves(norms[:]), k.pair(0), ACT.Sqrt).then_inc(s_at, 1)
            act.wait_ge(e_at, E.at("bonussum"))
            nc.scalar.activation(tmp, cum, ACT.Exp, scale=-DECAY).then_inc(schain, 1)
            nc.scalar.activation(sw, sw, ACT.Exp, scale=-DECAY)
            act.wait_ge(schain, 1)
            nc.scalar.activation(cum, cum, ACT.Exp, scale=DECAY).then_inc(s_at, 1)

        @block.tensor
        def _(pe):
            pe.wait_ge(loaded, 48)
            pe.wait_ge(s_at, S.at("low"))
            for name, lhs, rhs in (("w", up[0:64, 0], xs[0:64, 12, :]), ("a", up[64:128, 0], xs[64:128, 12, :]),
                                   ("g", up[:, 1], xs[:, 13, :])):
                if name != "w":
                    pe.wait_ge(s_at, S.at({"a": "sw", "g": "aa"}[name]))
                for n in range(4):
                    for h in range(2):
                        mm = nc.tensor.matmul(k.bank(2 * n + h, TH), lhs[:, n * P:(n + 1) * P],
                                              rhs[:, h * TH:(h + 1) * TH], start=True, stop=True)
                mm.then_inc(e_at, 1)
            pe.wait_ge(v_at, V.at("keys2"))
            pe.wait_ge(s_at, S.at("gg"))
            gather_heads(k, [tmp[:, n, :] for n in range(4)]).then_inc(e_at, 1)
            pe.wait_ge(v_at, V.at("inverted"))
            spread_heads(k, norms, 4).then_inc(e_at, 1)
            pe.wait_ge(v_at, V.at("prods"))
            for n in range(4):
                for h in range(2):
                    mm = nc.tensor.matmul(k.bank(2 * n + h, TH), k.blocks[:], tmp[:, n, h * TH:(h + 1) * TH],
                                          start=True, stop=True)
            mm.then_inc(e_at, 1)


def accumulate(nc, out, *pairs):
    for m in range(out.shape[1]):
        for n, (lhs, rhs) in enumerate(pairs):
            for half in range(2):
                part = slice(half * HD, half * HD + HD)
                mm = nc.tensor.matmul(out[part, m, :], lhs[part, m, :], rhs[part, m, :], start=n == 0,
                                      stop=n == len(pairs) - 1)
    return mm


def accumulate_open(nc, out, lhs, rhs, first=False, last=False):
    blocks = out.shape[1]
    for m in range(blocks):
        for half in range(2):
            part = slice(half * HD, half * HD + HD)
            mm = nc.tensor.matmul(out[part, m, :], lhs[part, m, :], rhs[part, m, :], start=first and m == 0,
                                  stop=last and m == blocks - 1)
    return mm


def chunk_inverse(k, c, t0, i, eng, which, sample):
    nc = k.nc
    mask = lambda m: c.masks[:, 6 * sample + m:6 * sample + m + 1, :].broadcast_to([P, 4, CH])
    chunks = range(c.blocks // 4)
    v = lambda name: c.wait(eng, which, c.V, c.V.at(name, i))
    s = lambda name: c.wait(eng, which, c.S, c.S.at(name, i))
    e = lambda name: c.wait(eng, which, c.E, c.E.at(name, i))
    power = lambda m: (c.n2, c.n2t) if m % 2 else (c.n, c.nt)

    if which == "tensor":
        identity = c.identity4

        def product(j, b, half, lhs, rhs):
            own = lambda tile: tile if tile is identity else c.own(tile, j)
            return accumulate(nc, c.slot(j, b, half), (own(lhs), own(rhs)))

        v("copied")
        s("copied")
        for j in chunks:
            product(j, 0, 0, c.k0, c.b0)
            product(j, 0, 1, c.b0, c.k0).then_inc(c.E.sem, 1)
        for j in chunks:
            product(j, 2, 0, c.h0, c.k0)
            product(j, 2, 1, c.h0, c.r0)
            product(j, 3, 0, c.b0, c.r0)
            product(j, 3, 1, c.b0, identity)
            product(j, 1, 0, c.v0, identity)
            product(j, 1, 1, c.h0, identity).then_inc(c.E.sem, 1)
        for j in chunks:
            v(f"masked{j}")
            product(j, 0, 0, c.nt, c.n)
            s(f"turned{j}")
            product(j, 1, 0, c.n, c.nt).then_inc(c.E.sem, 1)
        for m in range(1, 4):
            n, nt = power(m)
            if m < 3:
                for j in chunks:
                    v(f"square{m}{j}")
                    s(f"square{m}{j}")
                    mm = product(j, 0, 0, nt, n)
                    if m == 1:
                        mm = product(j, 1, 0, n, nt)
                    mm.then_inc(c.E.sem, 1)
            for j in chunks:
                v(f"times{m}{j}")
                product(j, 2, 0, n, c.tt).then_inc(c.E.sem, 1)
        for j in chunks:
            v(f"times4{j}")
            product(j, 0, 0, c.below, c.tt)
            product(j, 1, 0, c.tt, c.below)
            product(j, 2, 0, c.tt, identity).then_inc(c.E.sem, 1)
        for j in chunks:
            v(f"q{j}")
            s(f"q{j}")
            product(j, 1, 0, c.qt, c.q)
            product(j, 2, 0, c.t, c.q)
            product(j, 2, 1, c.q, c.t).then_inc(c.E.sem, 1)
        for j in chunks:
            v(f"r{j}")
            s(f"q2{j}")
            product(j, 0, 0, c.rt, c.q2).then_inc(c.E.sem, 1)

    if which == "vector":
        own = c.own
        for dst, src in ((c.k0, k.r.kt), (c.b0, k.r.bt), (c.h0, k.r.ht), (c.r0, k.r.rt)):
            last = nc.vector.tensor_copy(c.chunks(dst), c.source(src, t0))
        last.then_inc(c.V.sem, 1)
        for j in chunks:
            e(f"grams{j}")
            nc.vector.tensor_tensor(own(c.n, j), c.slot(j, 0, 0), mask(0), ALU.mult)
            nc.vector.tensor_tensor(own(c.nt, j), c.slot(j, 0, 1), mask(1), ALU.mult)
            nc.vector.tensor_tensor(own(c.below, j), c.slot(j, 0, 0), mask(2), ALU.mult).then_inc(c.V.sem, 1)
        for j in chunks:
            e(f"square1{j}")
            nc.vector.tensor_copy(own(c.n2, j), c.slot(j, 0, 0)).then_inc(c.V.sem, 1)
        for j in chunks:
            v(f"masked{j}")
            nc.vector.tensor_tensor(own(c.tt, j), own(c.nt, j), c.identity4, ALU.add)
            nc.vector.tensor_tensor(own(c.ak, j), c.slot(j, 2, 0), mask(3), ALU.mult)
            nc.vector.tensor_tensor(own(c.rk, j), c.slot(j, 2, 1), mask(4), ALU.mult)
            nc.vector.tensor_tensor(own(c.rb, j), c.slot(j, 3, 0), mask(5), ALU.mult)
            nc.vector.tensor_scalar(own(c.b1, j), c.slot(j, 3, 1), -1.0, None, ALU.mult).then_inc(c.V.sem, 1)
        for m in range(2, 5):
            if m < 4:
                for j in chunks:
                    e(f"square{m}{j}")
                    v(f"times{m - 1}{j}")
                    nc.vector.tensor_copy(own(power(m)[0], j), c.slot(j, 0, 0)).then_inc(c.V.sem, 1)
            for j in chunks:
                e(f"prods{m - 1}{j}")
                v(f"times{m - 1}{j}")
                nc.vector.tensor_tensor(own(c.tt, j), c.slot(j, 2, 0), own(c.tt, j), ALU.add).then_inc(c.V.sem, 1)
        for j in chunks:
            e(f"q{j}")
            nc.vector.tensor_copy(own(c.t, j), c.slot(j, 2, 0))
            nc.vector.tensor_copy(own(c.q, j), c.slot(j, 0, 0)).then_inc(c.V.sem, 1)
        for j in chunks:
            e(f"q2{j}")
            v(f"q{j}")
            nc.vector.tensor_tensor(own(c.rr, j), c.slot(j, 2, 0), own(c.tt, j), ALU.add)
            nc.vector.tensor_tensor(own(c.rt, j), c.slot(j, 2, 1), own(c.t, j), ALU.add).then_inc(c.V.sem, 1)
        for j in chunks:
            e(f"inverse{j}")
            v(f"r{j}")
            nc.vector.tensor_tensor(own(c.ti, j), c.slot(j, 0, 0), own(c.rr, j), ALU.add).then_inc(c.V.sem, 1)

    if which == "scalar":
        own = c.own
        if not sample:
            c.wait(eng, which, c.V, c.V.before(i))
        nc.scalar.activation(c.chunks(c.v0), c.source(k.r.vt, t0), ACT.Copy).then_inc(c.S.sem, 1)
        for j in chunks:
            e(f"turned{j}")
            nc.scalar.activation(own(c.v1, j), c.slot(j, 1, 0), ACT.Copy)
            nc.scalar.activation(own(c.h1, j), c.slot(j, 1, 1), ACT.Copy).then_inc(c.S.sem, 1)
        for m in range(1, 3):
            for j in chunks:
                e(f"square{m}{j}")
                if m == 2:
                    v(f"times1{j}")
                nc.scalar.activation(own(power(m)[1], j), c.slot(j, 1, 0), ACT.Copy).then_inc(c.S.sem, 1)
        for j in chunks:
            e(f"q{j}")
            nc.scalar.activation(own(c.qt, j), c.slot(j, 1, 0), ACT.Copy).then_inc(c.S.sem, 1)
        for j in chunks:
            e(f"q2{j}")
            nc.scalar.activation(own(c.q2, j), c.slot(j, 1, 0), ACT.Copy).then_inc(c.S.sem, 1)


def prompt_states(k, c, t0, i, eng, which):
    nc = k.nc
    v = lambda name: c.wait(eng, which, c.V, c.V.at(name, i))
    e = lambda name: c.wait(eng, which, c.E, c.E.at(name, i))
    banks = [[c.slot(j, *place) for place in ((3, 0), (3, 1), (1, 0), (2, 0))] for j in range(2)]
    part_of = c.own

    def early(j):
        x, _, out, new = banks[j]
        accumulate_open(nc, x, part_of(c.ak, j), part_of(c.v1, j), first=True)
        accumulate_open(nc, out, part_of(c.v1, j), part_of(c.rk, j), first=True)
        accumulate_open(nc, new, part_of(c.h1, j), part_of(c.v1, j), first=True)

    if which == "tensor":
        early(0)
        for j in range(2):
            x, u, out, new = banks[j]
            v(f"done{j}")
            if j:
                v("state0")
            accumulate_open(nc, x, part_of(c.k0, j), c.state, last=True).then_inc(c.E.sem, 1)
            accumulate_open(nc, out, c.state, part_of(c.r0, j))
            accumulate_open(nc, new, c.identity4, c.state)
            if j == 0:
                early(1)
            v(f"x{j}")
            accumulate(nc, u, (part_of(c.ti, j), c.x)).then_inc(c.E.sem, 1)
            v(f"u{j}")
            accumulate_open(nc, new, part_of(c.b1, j), c.u, last=True).then_inc(c.E.sem, 1)
            accumulate_open(nc, out, c.u, part_of(c.rb, j), last=True).then_inc(c.E.sem, 1)

    if which == "vector":
        for j in range(2):
            x, u, out, new = banks[j]
            e(f"x{j}")
            nc.vector.tensor_copy(c.x, x).then_inc(c.V.sem, 1)
            e(f"u{j}")
            nc.vector.tensor_copy(c.u, u).then_inc(c.V.sem, 1)
            e(f"new{j}")
            nc.vector.tensor_tensor(c.state, new, k.r.ends[:, :, bass.ds(2 * i + j, 1)].broadcast_to([P, 4, HD]),
                                    ALU.mult).then_inc(c.V.sem, 1)

    if which == "scalar":
        for j in range(2):
            e(f"out{j}")
            nc.scalar.activation(k.r.o[:, :, bass.ds(t0 + j * CH, CH)], banks[j][2], ACT.Copy)


def sample_states(k, c, eng, which):
    nc = k.nc
    v = lambda name: c.wait(eng, which, c.V, c.V.at(name))
    s = lambda name: c.wait(eng, which, c.S, c.S.at(name))
    e = lambda name: c.wait(eng, which, c.E, c.E.at(name))
    parts = [slice(0, HD), slice(HD, P)]
    cols = [slice(n * DEC_SEQ, (n + 1) * DEC_SEQ) for n in range(DEC_BATCH)]
    flat = lambda x: x.rearrange("p n v -> p (n v)")
    seen, x, u, out = (k.bank(b, 4 * CH).rearrange("p (m t) -> p m t", t=CH) for b in (4, 5, 6, 7))

    if which == "tensor":
        for m in range(4):
            for n in range(DEC_BATCH):
                for part in parts:
                    mm = nc.tensor.matmul(seen[part, m, cols[n]], c.states[part, m, n, :], c.k0[part, m, cols[n]],
                                          start=True, stop=True)
        mm.then_inc(c.E.sem, 1)
        s("seen")
        accumulate(nc, x, (c.seen, c.identity4), (c.ak, c.v1)).then_inc(c.E.sem, 1)
        v("done0")
        v("x0")
        accumulate(nc, u, (c.ti, c.x)).then_inc(c.E.sem, 1)
        v("u0")
        for m in range(4):
            for part in parts:
                nc.tensor.matmul(out[part, m, :], c.v1[part, m, :], c.rk[part, m, :], start=True, stop=False)
            for n in range(DEC_BATCH):
                for part in parts:
                    nc.tensor.matmul(out[part, m, cols[n]], c.states[part, m, n, :], c.r0[part, m, cols[n]],
                                     start=False, stop=False)
            for part in parts:
                mm = nc.tensor.matmul(out[part, m, :], c.u[part, m, :], c.rb[part, m, :], start=False, stop=True)
        mm.then_inc(c.E.sem, 1)
        for m in range(4):
            eng.wait_ge(c.spread, m + 1)
            if m >= 2:
                eng.wait_ge(c.taken, m - 1)
            for n, (lhs, rhs) in enumerate(((k.ident, c.states[:, m]), (c.h1[:, m, :], c.vm[:, m % 2]),
                                            (c.b1[:, m, :], c.um[:, m % 2]))):
                for part in parts:
                    left = lhs[part, part] if n == 0 else lhs[part, :]
                    mm = nc.tensor.matmul(k.ps[part, 1 + m % 2, :], left, flat(rhs)[part, :], start=n == 0, stop=n == 2)
            mm.then_inc(c.updated, 1)

    if which == "vector":
        e("x0")
        nc.vector.tensor_copy(c.x, x).then_inc(c.V.sem, 1)
        e("u0")
        nc.vector.tensor_copy(c.u, u).then_inc(c.V.sem, 1)
        v("u0")
        own = c.seqmask.rearrange("p (n o) -> p n o", o=1).broadcast_to([P, DEC_BATCH, HD])

        def take_state(m):
            eng.wait_ge(c.updated, m + 1)
            decay = k.r.ends[:, m, NCH:].rearrange("p (n o) -> p n o", o=1).broadcast_to([P, DEC_BATCH, HD])
            nc.vector.tensor_tensor(c.states[:, m], k.ps[:, 1 + m % 2, :].rearrange("p (n v) -> p n v", n=DEC_BATCH),
                                    decay, ALU.mult).then_inc(c.taken, 1)

        for m in range(4):
            if m >= 2:
                eng.wait_ge(c.updated, m - 1)
            rep = lambda x: x[:, m:m + 1, :].broadcast_to([P, DEC_BATCH, HD])
            nc.vector.tensor_tensor(c.vm[:, m % 2], rep(c.v1), own, ALU.mult)
            nc.vector.tensor_tensor(c.um[:, m % 2], rep(c.u), own, ALU.mult).then_inc(c.spread, 1)
            if m >= 1:
                take_state(m - 1)
        take_state(3)

    if which == "scalar":
        e("seen")
        nc.scalar.activation(c.seen, seen, ACT.Copy).then_inc(c.S.sem, 1)
        e("out0")
        nc.scalar.activation(k.r.o[:, :, SEQ:T], out, ACT.Copy)


def rwkv_chunks_stage(k, sample):
    nc = k.nc
    with ExitStack() as ctx:
        spare = k.z[:, 0:4, :].rearrange("p a t -> p (a t)")
        c = Tiles()
        c.blocks = 4 if sample else 8
        c.slot = lambda j, b, half: k.ps[:, 4 * j + b, half * 256:half * 256 + 256].rearrange("p (m t) -> p m t", t=CH)
        c.own = lambda tile, j: tile[:, 4 * j:4 * j + 4, :]
        names = "r0 k0 b0 h0 v0 n nt n2 n2t t tt below ak rk rb v1 h1 b1 q qt q2 rr rt ti"
        (c.r0, c.k0, c.b0, c.h0, c.v0, c.n, c.nt, c.n2, c.n2t, c.t, c.tt, c.below, c.ak, c.rk, c.rb, c.v1, c.h1, c.b1,
         c.q, c.qt, c.q2, c.rr, c.rt, c.ti) = [
            k.sb(ctx, name, [P, c.blocks, CH])[:] if m >= 4 else
            spare[:, m * 512:m * 512 + c.blocks * CH].rearrange("p (h t) -> p h t", t=CH)
            for m, name in enumerate(names.split())]
        c.x, c.u, c.state = (k.sb(ctx, name, [P, 4, CH])[:] for name in ("x", "u", "state"))
        c.masks = k.sb(ctx, "masks", [P, 12, CH])
        c.ident2 = k.sb(ctx, "ident2", [P, CH])[:]
        c.identity4 = c.ident2.rearrange("p (o t) -> p o t", o=1).broadcast_to([P, 4, CH])
        c.chunks = lambda dst: dst.rearrange("p (c n) t -> p n c t", n=4)
        c.source = lambda src, t0: src[:, :, bass.ds(t0, c.blocks // 4 * CH)].rearrange("p n (c t) -> p n c t", t=CH)
        v_at, s_at, e_at, loaded, stored, c.passed = k.sems(ctx, "dve_step", "act_step", "pe_step", "loaded", "stored",
                                                            "passed")
        names = lambda steps: " " + " ".join(f"{n}{j}" for n in steps.split() for j in range(c.blocks // 4)) + " "
        c.V = Steps(v_at, "copied" + names("masked square1 times1 square2 times2 square3 times3 times4 q r done")
                    + ("x0 u0" if sample else "x0 u0 state0 x1 u1 state1"), base=1)
        c.S = Steps(s_at, "copied" + names("turned square1 square2 q q2") + ("seen" if sample else ""))
        c.E = Steps(e_at, names("grams turned square1 square2 prods1 square3 prods2 prods3 q q2 inverse")
                    + ("seen x0 u0 out0" if sample else "x0 u0 new0 out0 x1 u1 new1 out1"))

        def wait(eng, which, steps, value):
            eng.wait_ge(steps.sem, value)
            if which == "tensor":
                eng.sem_inc(c.passed, 1)

        c.wait = wait
        if sample:
            c.states = k.sb(ctx, "states", [P, 4, DEC_BATCH, HD])
            more = k.z[:, 8:12, :].rearrange("p a t -> p (a t)")
            c.seen = more[:, 2048:2304].rearrange("p (m t) -> p m t", t=CH)
            c.vm, c.um = (more[:, m * 1024:(m + 1) * 1024].rearrange("p (b n v) -> p b n v", b=2, v=HD) for m in range(2))
            c.seqmask = k.sb(ctx, "seqmask", [P, DEC_BATCH])
            c.spread, c.updated, c.taken = k.sems(ctx, "spread", "updated", "taken")
        n_loads = 4 if sample else 2
        block = ctx.enter_context(nc.Block())

        def rounds(eng, which):
            if sample:
                chunk_inverse(k, c, SEQ, 0, eng, which, 1)
                sample_states(k, c, eng, which)
            else:
                with eng.Fori(0, NCH // 2) as i:
                    chunk_inverse(k, c, i * (2 * CH), i, eng, which, 0)
                    prompt_states(k, c, i * (2 * CH), i, eng, which)

        @block.sync
        def _(sp):
            sp.dma_start(c.masks.rearrange("p m t -> p (m t)"), k.d["masks"]).then_inc(loaded, 16)
            sp.dma_start(c.ident2, k.d["ident2"]).then_inc(loaded, 16)
            if sample:
                sp.dma_start(c.states.rearrange("p m n v -> p (m n v)"), k.d["states"]).then_inc(loaded, 16)
                sp.dma_start(c.seqmask[:], k.d["seqmask"]).then_inc(loaded, 16)
                sp.wait_ge(c.taken, 4)
                sp.dma_start(k.d["out_states"], c.states.rearrange("p m n v -> p (m n v)")).then_inc(stored, 16)
            else:
                sp.wait_ge(v_at, c.V.before(NCH // 2))
                sp.dma_start(k.d["out_state"], c.state.rearrange("p m v -> p (m v)")).then_inc(stored, 16)
            sp.wait_ge(stored, 16)

        @block.tensor
        def _(pe):
            pe.wait_ge(loaded, 16 * n_loads)
            rounds(pe, "tensor")

        @block.vector
        def _(dve):
            nc.vector.memset(c.state, 0.0).then_inc(v_at, 1)
            dve.wait_ge(loaded, 16 * n_loads)
            dve.wait_ge(v_at, 1)
            rounds(dve, "vector")

        @block.scalar
        def _(act):
            rounds(act, "scalar")


def rwkv_finish_stage(k):
    nc = k.nc
    o, r = k.r.o, k.r
    with ExitStack() as ctx:
        sq = k.sb(ctx, "sq", [P, 4, T])
        rs = k.sb(ctx, "rs", [P, T])
        V = Steps(None, "centred mean inverted")
        E = Steps(None, "summed squares spread")
        v_at, e_at, squared, rooted, chain = k.sems(ctx, "dve_step", "pe_step", "squared", "rooted", "chain")
        block = ctx.enter_context(nc.Block())

        @block.tensor
        def _(pe):
            for n in range(4):
                for h in range(2):
                    mm = nc.tensor.matmul(k.bank(2 * n + h, TH), k.blocks[:], o[:, n, h * TH:(h + 1) * TH],
                                          start=True, stop=True)
            mm.then_inc(e_at, 1)
            pe.wait_ge(squared, 1)
            gather_heads(k, [sq[:, n, :] for n in range(4)]).then_inc(e_at, 1)
            pe.wait_ge(v_at, V.at("inverted"))
            spread_heads(k, rs, 4).then_inc(e_at, 1)

        @block.vector
        def _(dve):
            ch = Chain(dve, chain)
            dve.wait_ge(e_at, E.at("summed"))
            for n in range(4):
                last = nc.vector.scalar_tensor_tensor(out=halves(o[:, n, :]), in0=k.pair(2 * n), scalar=-1.0 / HD,
                                                      in1=halves(o[:, n, :]), op0=ALU.mult, op1=ALU.add)
            last.then_inc(v_at, 1)
            dve.wait_ge(e_at, E.at("squares"))
            nc.vector.tensor_scalar(halves(rs[:]), k.pair(0), 1.0 / HD, GN_EPS, ALU.mult, ALU.add).then_inc(v_at, 1)
            dve.wait_ge(rooted, 1)
            nc.vector.reciprocal(rs[:], rs[:]).then_inc(v_at, 1)
            dve.wait_ge(e_at, E.at("spread"))
            for n in range(4):
                last = nc.vector.scalar_tensor_tensor(out=halves(o[:, n, :]), in0=halves(o[:, n, :]), scalar=k.par("gn_w", n),
                                                      in1=k.pair(2 * n), op0=ALU.mult, op1=ALU.mult)
            ch.link(last)
            for n in range(4):
                last = nc.vector.scalar_tensor_tensor(out=o[:, n, :], in0=o[:, n, :], scalar=k.par("gn_b", n),
                                                      in1=r.bonus[:, n, :], op0=ALU.add, op1=ALU.add)
            ch.link(last)
            ch.link(nc.vector.tensor_tensor(o[:], o[:], r.g[:], ALU.mult))

        @block.scalar
        def _(act):
            act.wait_ge(v_at, V.at("centred"))
            nc.scalar.activation(sq[:], o[:], ACT.Square).then_inc(squared, 1)
            act.wait_ge(v_at, V.at("mean"))
            nc.scalar.activation(rs[:], rs[:], ACT.Sqrt).then_inc(rooted, 1)


def nsa_prepare_stage(k):
    nc = k.nc
    Z = k.z
    groups = [([ZQ, ZQ + 1, ZQ + 2, ZQ + 3], ["q_norm"] * 4, [0] * 4), ([ZK + 2, ZK + 4], ["k_norm"] * 2, [1, 2])]
    with ExitStack() as ctx:
        sq = k.sb(ctx, "sq", [P, 4, T])
        tab = k.sb(ctx, "rope", [P, 2, T])
        rot = k.sb(ctx, "rot", [P, P])
        rs = k.sb(ctx, "rs", [P, T])
        V = Steps(None, "mean inverted normed roped")
        E = Steps(None, "summed spread turned")
        v_at, e_at, squared, rooted, vt_ready, loaded, stored, chain = k.sems(
            ctx, "dve_step", "pe_step", "squared", "rooted", "vt_ready", "loaded", "stored", "chain")
        block = ctx.enter_context(nc.Block())

        @block.sync
        def _(sp):
            sp.dma_start(tab.rearrange("p m t -> p (m t)"), k.d["rope"]).then_inc(loaded, 16)
            sp.dma_start(rot[:], k.d["rot"]).then_inc(loaded, 16)
            sp.dma_start(k.d["out_win"], k.d["win_rows"]).then_inc(stored, 16)
            sp.wait_ge(v_at, V.at("roped", 1))
            sp.dma_start(k.d["out_kv"], Z[:, ZK:NZ, :].rearrange("p c t -> p (c t)")).then_inc(stored, 16)
            sp.wait_ge(stored, 32)

        @block.scalar
        def _(act):
            for g, (tiles, _, _) in enumerate(groups):
                if g:
                    act.wait_ge(v_at, V.at("roped", g - 1))
                for n, z in enumerate(tiles):
                    last = nc.scalar.activation(sq[:, n, :], Z[:, z, :], ACT.Square)
                last.then_inc(squared, 1)
                act.wait_ge(v_at, V.at("mean", g))
                nc.scalar.activation(rs[:], rs[:], ACT.Sqrt).then_inc(rooted, 1)

        @block.tensor
        def _(pe):
            pe.wait_ge(loaded, 32)
            for g, (tiles, _, _) in enumerate(groups):
                pe.wait_ge(squared, g + 1)
                gather_heads(k, [sq[:, n, :] for n in range(len(tiles))]).then_inc(e_at, 1)
                pe.wait_ge(v_at, V.at("inverted", g))
                spread_heads(k, rs, len(tiles)).then_inc(e_at, 1)
                pe.wait_ge(v_at, V.at("normed", g))
                for n, z in enumerate(tiles):
                    for h in range(2):
                        mm = nc.tensor.matmul(k.bank(2 * n + h, TH), rot[:], Z[:, z, h * TH:(h + 1) * TH],
                                              start=True, stop=True)
                mm.then_inc(e_at, 1)
            for b, z in enumerate((ZK + 3, ZK + 5)):
                for tt in range(5):
                    n = min(P, T - tt * P)
                    mm = nc.tensor.transpose(k.ps[0:n, 4 + 2 * b + tt // 4, (tt % 4) * P:(tt % 4) * P + P],
                                             Z[:, z, tt * P:tt * P + n], k.ident[:])
            mm.then_inc(vt_ready, 1)

        @block.vector
        def _(dve):
            ch = Chain(dve, chain)
            dve.wait_ge(loaded, 32)
            for g, (tiles, gains, which) in enumerate(groups):
                m = len(tiles)
                dve.wait_ge(e_at, E.at("summed", g))
                nc.vector.tensor_scalar(halves(rs[:]), k.pair(0), 1.0 / HD, EPS, ALU.mult, ALU.add).then_inc(v_at, 1)
                dve.wait_ge(rooted, g + 1)
                nc.vector.reciprocal(rs[:], rs[:]).then_inc(v_at, 1)
                dve.wait_ge(e_at, E.at("spread", g))
                for n, z in enumerate(tiles):
                    last = nc.vector.scalar_tensor_tensor(out=halves(Z[:, z, :]), in0=halves(Z[:, z, :]),
                                                          scalar=k.par(gains[n], which[n]), in1=k.pair(2 * n),
                                                          op0=ALU.mult, op1=ALU.mult)
                last.then_inc(v_at, 1)
                dve.wait_ge(e_at, E.at("turned", g))
                for n in range(m):
                    last = nc.vector.tensor_tensor(halves(sq[:, n, :]), k.pair(2 * n), halves(tab[:, 1, :]), ALU.mult)
                dst = [k.qr[:, n, :] if g == 0 else Z[:, z, :] for n, z in enumerate(tiles)]
                for n, z in enumerate(tiles):
                    last = nc.vector.tensor_tensor(dst[n], Z[:, z, :], tab[:, 0, :], ALU.mult)
                ch.link(last)
                for n in range(m):
                    last = nc.vector.tensor_tensor(dst[n], dst[n], sq[:, n, :], ALU.add)
                last.then_inc(v_at, 1)
            dve.wait_ge(vt_ready, 1)
            for b, dst in enumerate((k.vs, k.vw)):
                nc.vector.tensor_copy(dst[:, 0:4, :].rearrange("p a c -> p (a c)"), k.bank(4 + 2 * b))
                last = nc.vector.tensor_copy(dst[0:TS, 4, :], k.ps[0:TS, 5 + 2 * b, 0:P])
            ch.link(last)


def compress_stage(k):
    nc = k.nc
    Z = k.z
    SEQS = 2
    GP = SEQS * PAGES
    groups = DEC_BATCH // SEQS
    jobs = [(1, 32)] + [(SEQS, CH)] * groups
    MAXW = SEQS * 2 * CH
    with ExitStack() as ctx:
        w1 = k.sb(ctx, "w1", [P, 8, 2, 2, CMP_HIDDEN])
        w2 = k.sb(ctx, "w2", [P, 2, 2, HD])
        pages = k.sb(ctx, "pages", [P, 2 * GP, 8, 2, 2, 8])
        xp = k.sb(ctx, "xp", [P, 8, 2, 66])
        bias = k.sb(ctx, "bias", [P, 4])
        second = k.sb(ctx, "second", [P, MAXW])
        hid = k.sb(ctx, "hid", [P, 2, 2, 2, MAXW])
        sq = k.sb(ctx, "sq", [P, MAXW // 2])
        rs = k.sb(ctx, "rs", [P, MAXW // 2])
        (weights, landed0, landed1, parted, moved, summed, gelued, heads, squared, mean, rooted, out,
         chain, sums, kept) = k.sems(ctx, "weights", "landed0", "landed1", "parted", "moved",
                                     "summed", "gelued", "heads", "squared", "mean", "rooted", "out", "chain", "sums",
                                     "kept")
        landed = (landed0, landed1)
        block = ctx.enter_context(nc.Block())

        def steps(first, tail_a, tail_b):
            for n in range(len(jobs) + 1):
                for m in range(4):
                    if n < len(jobs):
                        first(n, m)
                    if n and m == 1:
                        tail_a(n - 1)
                if n:
                    tail_b(n - 1)

        @block.sync
        def _(sp):
            sp.dma_start(xp[:, :, :, 64:66], k.d["cmp_pe"].rearrange("p (j e r) -> p j e r", j=8, e=2)).then_inc(weights, 16)
            sp.dma_start(w1.rearrange("p j e r f -> p (j e r f)"), k.d["cmp_w1"]).then_inc(weights, 16)
            sp.dma_start(w2.rearrange("p e h d -> p (e h d)"), k.d["cmp_w2"]).then_inc(weights, 16)
            for g in range(groups):
                if g >= 2:
                    sp.wait_ge(parted, 4 * g)
                with sp.Fori(0, GP) as i:
                    page = sp.value_load(k.table[0:1, bass.ds(g * GP + i, 1)], min_val=0, max_val=k.n_phys - 1)
                    sp.dma_start(pages[:, bass.ds(g % 2 * GP + i, 1)].rearrange("p o j e k c -> p (o j e k c)"),
                                 k.d["cmp_pages"][bass.ds(page, 1)].rearrange("o p n -> (o p) n")).then_inc(
                                     landed[g % 2], 16)

        @block.tensor
        def _(pe):
            pe.wait_ge(weights, 48)
            def first(n, m):
                ns, cols = jobs[n]
                w = ns * 2 * cols if n else 66
                e, f = m // 2, m % 2
                if m == 0:
                    if n:
                        g = n - 1
                        pe.wait_ge(landed[g % 2], 16 * GP * (g // 2 + 1))
                    else:
                        pe.wait_ge(moved, 1)
                if n:
                    pe.wait_ge(summed, 4 * (n - 1) + m + 1)
                for r in range(2):
                    dst = k.ps[:, m, r * MAXW:r * MAXW + w]
                    for j in range(8):
                        if n:
                            rhs = pages[:, g_slot(n):g_slot(n) + GP, j, e]
                            to = dst.rearrange("p (k s c) -> p s k c", k=2, c=8)
                        else:
                            rhs, to = xp[:, j, e, :], dst
                        mm = nc.tensor.matmul(to, w1[:, j, e, r, f * P:(f + 1) * P], rhs, start=j == 0, stop=j == 7)
                mm.then_inc(parted, 1)

            def tail_a(n):
                ns, cols = jobs[n]
                half = ns * cols
                pe.wait_ge(gelued, 4 * (n + 1))
                if n:
                    pe.wait_ge(out, 2 * n)
                for kv in range(2):
                    for f in range(2):
                        mm = nc.tensor.matmul(k.ps[kv * HD:kv * HD + HD, 4, 0:half], w2[:, 0, f, :],
                                              hid[:, n % 2, 0, f, kv * half:(kv + 1) * half], start=f == 0, stop=f == 1)
                for s in range(ns):
                    for kv in range(2):
                        for f in range(2):
                            at = kv * half + s * cols
                            mm = nc.tensor.matmul(k.ps[0:cols, 5, s * P + kv * HD:s * P + kv * HD + HD],
                                                  hid[:, n % 2, 1, f, at:at + cols], w2[:, 1, f, :], start=f == 0,
                                                  stop=f == 1)
                mm.then_inc(heads, 1)

            def tail_b(n):
                half = jobs[n][0] * jobs[n][1]
                pe.wait_ge(squared, n + 1)
                nc.tensor.matmul(k.bank(6, half), k.blocks[:], sq[:, 0:half], start=True, stop=True).then_inc(sums, 1)

            g_slot = lambda n: (n - 1) % 2 * GP
            steps(first, tail_a, tail_b)

        @block.scalar
        def _(act):
            for e in range(2):
                for kv in range(2):
                    for odd in range(2):
                        last = nc.scalar.activation(
                            xp[odd * HD:odd * HD + HD, :, e, kv * 32:kv * 32 + 32].rearrange("p j c -> p c j"),
                            Z[kv * HD:kv * HD + HD, ZK + e, odd:SEQ:2].rearrange("p (c j) -> p c j", j=8), ACT.Copy)
            last.then_inc(moved, 1)

            def first(n, m):
                w = jobs[n][0] * 2 * jobs[n][1]
                extra = 0 if n else 2
                act.wait_ge(parted, 4 * n + m + 1)
                if 4 * n + m:
                    act.wait_ge(summed, 4 * n + m)
                nc.scalar.activation(second[:, 0:w + extra], k.ps[:, m, MAXW:MAXW + w + extra],
                                     ACT.Copy).then_inc(kept, 1)
                act.wait_ge(summed, 4 * n + m + 1)
                rows = hid[:, n % 2, m // 2, m % 2, 0:w]
                nc.scalar.activation(rows, rows, ACT.Gelu_apprx_tanh, bias=bias[:, m:m + 1]).then_inc(gelued, 1)

            def tail_a(n):
                half = jobs[n][0] * jobs[n][1]
                act.wait_ge(heads, n + 1)
                nc.scalar.activation(sq[:, 0:half], k.bank(4, half), ACT.Square).then_inc(squared, 1)

            def tail_b(n):
                half = jobs[n][0] * jobs[n][1]
                act.wait_ge(mean, n + 1)
                nc.scalar.activation(rs[:, 0:half], rs[:, 0:half], ACT.Sqrt).then_inc(rooted, 1)

            steps(first, tail_a, tail_b)

        @block.vector
        def _(dve):
            ch = Chain(dve, chain)

            def first(n, m):
                ns, cols = jobs[n]
                w = ns * 2 * cols
                dst = hid[:, n % 2, m // 2, m % 2, 0:w].rearrange("p (s c) -> p s c", c=cols)
                nc.vector.memset(dst[:, :, cols - 1:cols], 0.0)
                dve.wait_ge(kept, 4 * n + m + 1)
                if n == 0:
                    nc.vector.tensor_tensor(bias[:, m:m + 1], k.ps[:, m, w:w + 1], second[:, w + 1:w + 2], ALU.add)
                nc.vector.tensor_tensor(
                    dst[:, :, 0:cols - 1], k.ps[:, m, 0:w].rearrange("p (s c) -> p s c", c=cols)[:, :, 0:cols - 1],
                    second[:, 0:w].rearrange("p (s c) -> p s c", c=cols)[:, :, 1:cols], ALU.add).then_inc(summed, 1)

            def tail_a(n):
                ns, cols = jobs[n]
                dve.wait_ge(heads, n + 1)
                if n:
                    dst = k.vc[:, SEQS * (n - 1):SEQS * n, :].rearrange("p s d -> p (s d)")
                else:
                    dst = k.vcp[:]
                nc.vector.tensor_copy(dst, k.ps[0:cols, 5, 0:ns * P]).then_inc(out, 1)

            def tail_b(n):
                half = jobs[n][0] * jobs[n][1]
                dve.wait_ge(sums, n + 1)
                nc.vector.tensor_scalar(rs[:, 0:half], k.bank(6, half), 1.0 / HD, EPS, ALU.mult, ALU.add).then_inc(mean, 1)
                dve.wait_ge(rooted, n + 1)
                ch.link(nc.vector.reciprocal(rs[:, 0:half], rs[:, 0:half]))
                dst = k.kc[:, SEQS * (n - 1):SEQS * n, :].rearrange("p s c -> p (s c)") if n else k.kcp[:]
                nc.vector.scalar_tensor_tensor(out=dst, in0=k.bank(4, half), scalar=k.par("k_norm", 0),
                                               in1=rs[:, 0:half], op0=ALU.mult, op1=ALU.mult).then_inc(out, 1)

            steps(first, tail_a, tail_b)


def prompt_attention_stage(k, cached):
    nc = k.nc
    Z = k.z
    units = [(qt, kv, i) for qt in range(SEQ // P) for kv in range(2) for i in range(4)]
    n_units = len(units)
    chunks = [2 * (qt + 1) + 1 for qt, _, _ in units]
    pieces = [-(-c // 4) for c in chunks]
    before = [sum(pieces[:u]) for u in range(n_units + 1)]
    CMP = 32
    with ExitStack() as ctx:
        E = k.sb(ctx, "probs", [P, 3, 2 * SEQ + CMP])
        PT = Z[:, 8:14, :].rearrange("p c t -> p (c t)")[:, 0:2 * 12 * P].rearrange("p (b c q) -> p b c q", b=2, q=P)
        tri = k.sb(ctx, "tri", [P, P])
        cmask = k.sb(ctx, "cmask", [P, 4, CMP])
        cs = k.sb(ctx, "cmp_scores", [P, 8, CMP])
        mx = k.sb(ctx, "mx", [P, 3, 3])
        nm = k.sb(ctx, "nm", [P, 3, 3])
        sums = k.sb(ctx, "sums", [P, 3, 3])
        wts = k.sb(ctx, "wts", [P, 3, 3])
        loaded, scored, cmp_half, cmp_scored, cmp_masked, maxed, exped, weighted, turned, laid, mixed, out, chain = k.sems(
            ctx, "loaded", "scored", "cmp_half", "cmp_scored", "cmp_masked", "maxed", "exped", "weighted", "turned", "laid", "mixed",
            "out", "chain")

        def scores(u):
            qt = units[u][0]
            nk = (qt + 1) * P
            return k.bank(2 * (u % 2), nk), k.bank(2 * (u % 2) + 1, nk), cs[:, u % 8, :]

        def probs(u):
            nk = (units[u][0] + 1) * P
            return E[:, u % 3, 0:nk], E[:, u % 3, nk:2 * nk], E[:, u % 3, 2 * nk:2 * nk + CMP]

        block = ctx.enter_context(nc.Block())

        @block.sync
        def _(sp):
            sp.dma_start(tri[:], k.d["tri"]).then_inc(loaded, 16)
            sp.dma_start(cmask.rearrange("p a n -> p (a n)"), k.d["cmask"]).then_inc(loaded, 16)
            for g in range(cached.SLOTS):
                cached.load(sp, g)

        @block.tensor
        def _(pe):
            for step in range(n_units + 3):
                if step < n_units:
                    u = step
                    qt, kv, i = units[u]
                    half = slice(kv * HD, kv * HD + HD)
                    q = slice(qt * P, qt * P + P)
                    nk = (qt + 1) * P
                    if u % 8 == 0:
                        if qt:
                            pe.wait_ge(cmp_masked, qt)
                        for m in range(8):
                            mh = slice(m // 4 * HD, m // 4 * HD + HD)
                            mm = nc.tensor.matmul(k.ps[:, 4, m * CMP:(m + 1) * CMP], Z[mh, ZQ + m % 4, q], k.kcp[mh, :],
                                                  start=True, stop=True)
                            if m == 3:
                                mm.then_inc(cmp_half, 1)
                                pe.wait_ge(cmp_half, qt + 1)
                        mm.then_inc(cmp_scored, 1)
                    if u >= 2:
                        pe.wait_ge(exped, u - 1)
                    sel, win, _ = scores(u)
                    nc.tensor.matmul(sel, k.qr[half, i, q], Z[half, ZK + 2, 0:nk], start=True, stop=True)
                    nc.tensor.matmul(win, k.qr[half, i, q], Z[half, ZK + 4, 0:nk], start=True, stop=True).then_inc(scored, 1)
                if 2 <= step <= n_units + 1:
                    u = step - 2
                    pe.wait_ge(weighted, u + 1)
                    for n in range(pieces[u]):
                        at = before[u] + n
                        if at >= 2:
                            pe.wait_ge(laid, at - 1)
                        for c in range(4 * n, min(4 * n + 4, chunks[u])):
                            w = P if c < chunks[u] - 1 else CMP
                            mm = nc.tensor.transpose(k.ps[0:w, 6 + at % 2, (c % 4) * P:(c % 4) * P + P],
                                                     E[:, u % 3, c * P:c * P + w], k.ident[:])
                        mm.then_inc(turned, 1)
                if step >= 3:
                    u = step - 3
                    qt, kv, i = units[u]
                    pe.wait_ge(laid, before[u + 1])
                    if u >= 1:
                        pe.wait_ge(out, u)
                    for c in range(chunks[u]):
                        if c == chunks[u] - 1:
                            lhs, rhs = k.vcp[:], PT[0:CMP, u % 2, c, :]
                        else:
                            v = k.vs if c <= qt else k.vw
                            lhs, rhs = v[:, c % (qt + 1), :], PT[:, u % 2, c, :]
                        mm = nc.tensor.matmul(k.bank(5, P), lhs, rhs, start=c == 0, stop=c == chunks[u] - 1)
                    mm.then_inc(mixed, 1)

        @block.scalar
        def _(act):
            for step in range(n_units + 2):
                if step < n_units:
                    u = step
                    act.wait_ge(maxed, u + 1)
                    if u >= 3:
                        act.wait_ge(turned, before[u - 2])
                    for b, (src, dst) in enumerate(zip(scores(u), probs(u))):
                        last = nc.scalar.activation(dst, src, ACT.Exp, bias=nm[:, u % 3, b:b + 1], scale=SCALE,
                                                    accum_out=sums[:, u % 3, b:b + 1])
                    last.then_inc(exped, 1)
                if step >= 2:
                    u = step - 2
                    for n in range(pieces[u]):
                        at = before[u] + n
                        act.wait_ge(turned, at + 1)
                        if n == 0 and u >= 2:
                            act.wait_ge(mixed, u - 1)
                        full = min(4, chunks[u] - 1 - 4 * n)
                        if full:
                            last = nc.scalar.activation(PT[:, u % 2, 4 * n:4 * n + full, :],
                                                        k.ps[:, 6 + at % 2, 0:full * P].rearrange("p (c q) -> p c q", q=P),
                                                        ACT.Copy)
                        if n == pieces[u] - 1:
                            last = nc.scalar.activation(PT[0:CMP, u % 2, chunks[u] - 1, :],
                                                        k.ps[0:CMP, 6 + at % 2, full * P:full * P + P], ACT.Copy)
                        last.then_inc(laid, 1)

        @block.vector
        def _(dve):
            ch = Chain(dve, chain)
            dve.wait_ge(loaded, 32)
            for step in range(n_units + 3):
                if step < n_units:
                    u = step
                    qt = units[u][0]
                    if u % 8 == 0:
                        dve.wait_ge(cmp_scored, qt + 1)
                        if u:
                            dve.wait_ge(exped, u)
                        nc.vector.tensor_tensor(cs[:], k.bank(4, 8 * CMP).rearrange("p (m n) -> p m n", n=CMP),
                                                cmask[:, qt:qt + 1, :].broadcast_to([P, 8, CMP]), ALU.add).then_inc(cmp_masked, 1)
                        dve.wait_ge(cmp_masked, qt + 1)
                    dve.wait_ge(scored, u + 1)
                    sel, win, cmp = scores(u)
                    last_keys = slice(qt * P, qt * P + P)
                    nc.vector.tensor_tensor(sel[:, last_keys], sel[:, last_keys], tri[:], ALU.add)
                    ch.link(nc.vector.tensor_tensor(win[:, last_keys], win[:, last_keys], tri[:], ALU.add))
                    for b, src in enumerate((sel, win, cmp)):
                        last = nc.vector.tensor_reduce(mx[:, u % 3, b:b + 1], src, AX.X, ALU.max)
                    ch.link(last)
                    nc.vector.tensor_scalar(nm[:, u % 3, :], mx[:, u % 3, :], NEG * 1e-10, -SCALE, ALU.max,
                                            ALU.mult).then_inc(maxed, 1)
                if 1 <= step <= n_units:
                    u = step - 1
                    qt, kv, i = units[u]
                    dve.wait_ge(exped, u + 1)
                    ch.link(nc.vector.tensor_scalar(wts[:, u % 3, :], sums[:, u % 3, :], 1e-30, None, ALU.max))
                    ch.link(nc.vector.reciprocal(wts[:, u % 3, :], wts[:, u % 3, :]))
                    g = 3 * (4 * kv + i)
                    nc.vector.tensor_tensor(wts[:, u % 3, 0:2], wts[:, u % 3, 0:2], k.gates[:, qt, g + 1:g + 3], ALU.mult)
                    ch.link(nc.vector.tensor_tensor(wts[:, u % 3, 2:3], wts[:, u % 3, 2:3], k.gates[:, qt, g:g + 1],
                                                    ALU.mult))
                    for b, dst in enumerate(probs(u)):
                        last = nc.vector.tensor_scalar(dst, dst, wts[:, u % 3, b:b + 1], None, ALU.mult)
                    last.then_inc(weighted, 1)
                if step >= 3:
                    u = step - 3
                    qt, kv, i = units[u]
                    half = slice(kv * HD, kv * HD + HD)
                    dve.wait_ge(mixed, u + 1)
                    nc.vector.tensor_copy(k.on[half, i, qt * P:qt * P + P], k.ps[half, 5, 0:P]).then_inc(out, 1)


class CachedRows:
    SLOTS = 3

    def __init__(self, k, ctx):
        self.k = k
        self.pages = k.sb(ctx, "kv_pages", [P, self.SLOTS, 2 * PAGES, 2 * P])
        self.win_k = k.sb(ctx, "win_k", [P, self.SLOTS, 2, WINDOW])
        self.win_v = k.sb(ctx, "win_v", [P, self.SLOTS, 2, 4, P])
        self.landed = k.sems(ctx, *[f"landed{b}" for b in range(self.SLOTS)])

    def load(self, sp, g):
        k, b = self.k, g % self.SLOTS
        sp.dma_start(self.win_k[:, b].rearrange("p s n -> p (s n)"), k.d["win_k"][g]).then_inc(self.landed[b], 16)
        sp.dma_start(self.win_v[:, b].rearrange("p s c n -> p (s c n)"), k.d["win_v"][g]).then_inc(self.landed[b], 16)
        with sp.Fori(0, 2 * PAGES) as i:
            page = sp.value_load(k.table[0:1, bass.ds(g * 2 * PAGES + i, 1)], min_val=0, max_val=k.n_phys - 1)
            sp.dma_start(self.pages[:, b, bass.ds(i, 1), :].rearrange("p o n -> p (o n)"),
                         k.d["sel_pages"][bass.ds(page, 1)].rearrange("o p n -> (o p) n")).then_inc(self.landed[b], 16)


def sample_attention_stage(k, cached):
    nc = k.nc
    Z = k.z
    NG = DEC_BATCH // 2
    KEYS = dict(sel=(0, PAST), win=(PAST, WINDOW), seln=(PAST + WINDOW, TS), winn=(PAST + WINDOW + TS, TS),
                cmp=(PAST + WINDOW + 2 * TS, CH - 1))
    with ExitStack() as ctx:
        kv_pages, wk, wv, landed = cached.pages, cached.win_k, cached.win_v, cached.landed
        E = k.sb(ctx, "probs", [P, 2, PAST + WINDOW + 2 * TS + CH])
        spare = Z[:, 8:12, :].rearrange("p c t -> p (c t)")
        PT = spare[:, 0:15 * P].rearrange("p (c q) -> p c q", q=P)
        newmask = k.sb(ctx, "newmask", [P, NG, TS])
        winmask = k.sb(ctx, "winmask", [P, DEC_SEQ])
        pick = k.sb(ctx, "pick", [TS, NG, P])
        headmask = k.sb(ctx, "headmask", [P, NGATE])
        same = k.sb(ctx, "same", [P, P])
        iota = k.sb(ctx, "iota", [P, 14])
        mx = k.sb(ctx, "mx", [P, 5])
        nm = k.sb(ctx, "nm", [P, 3])
        sums = k.sb(ctx, "sums", [P, 5])
        wts = k.sb(ctx, "wts", [P, 3])
        pc = k.sb(ctx, "pc", [P, CH])
        imp = k.sb(ctx, "imp", [P, 14])
        pen = k.sb(ctx, "pen", [P, 14])
        one = k.sb(ctx, "one", [P, 2])
        gsel = k.sb(ctx, "gsel", [P, NGATE])
        gr = k.sb(ctx, "gr", [P, 2, 3])
        qs = k.sb(ctx, "qs", [P, 2, DEC_BATCH, 4 * DEC_SEQ])
        def order(ahead, names):
            steps = [f"{name}/0" for name in ahead.split()]
            for g in range(NG):
                for name in names.split():
                    own = g + name.startswith("next:")
                    if own < NG:
                        steps.append(f"{name.removeprefix('next:')}/{own}")
            return Steps(None, " ".join(steps))

        V = order("cmpmax pc maxes", "weighted next:cmpmax next:pc next:maxes out")
        S = order("cmpexp exps", "laid1 next:cmpexp laid2 next:exps")
        PE = order("scores imp", "next:scores turned1 next:imp turned2 mixed")
        step = lambda steps, name, g: steps.at(f"{name}/{g}")
        v_at, s_at, e_at, loaded, chain, packed = k.sems(ctx, "dve_step", "act_step", "pe_step", "loaded", "chain",
                                                         "packed")
        tables = [(newmask.rearrange("p g t -> p (g t)"), "newmask"), (winmask[:], "winmask"),
                  (pick.rearrange("p g t -> p (g t)"), "pick"), (headmask[:], "headmask"), (same[:], "same"),
                  (iota[:], "iota14")]
        past = k.ps[:, 0:2, :].rearrange("p b n -> p (b n)")
        win, small = k.bank(2), k.bank(3)
        near = spare[:, 15 * P:15 * P + 3 * CH]
        parts = lambda t: (t[:, 0:CH - 1], t[:, CH:2 * CH], t[:, 2 * CH:3 * CH])
        cmp, seln, winn = parts(near)
        isum, grow, mix = k.ps[:, 4, 0:CH - 1], k.ps[:, 4, 128:128 + NGATE], k.ps[:, 6, 0:P]
        probs = lambda name, g: E[:, g % 2, KEYS[name][0]:KEYS[name][0] + KEYS[name][1]]
        block = ctx.enter_context(nc.Block())

        @block.sync
        def _(sp):
            for dst, name in tables:
                sp.dma_start(dst, k.d[name]).then_inc(loaded, 16)
            for g in range(cached.SLOTS, NG):
                sp.wait_ge(e_at, step(PE, "mixed", g - cached.SLOTS))
                cached.load(sp, g)

        @block.tensor
        def _(pe):
            pe.wait_ge(loaded, 16 * len(tables))
            pe.wait_ge(packed, 2)
            def scores(g):
                b = g % cached.SLOTS
                pe.wait_ge(landed[b], (g // cached.SLOTS + 1) * 16 * (2 * PAGES + 2))
                if g:
                    pe.wait_ge(s_at, step(S, "exps", g - 1))
                for s in range(2):
                    seq = 2 * g + s
                    for kv in range(2):
                        half = slice(kv * HD, kv * HD + HD)
                        rows = slice(32 * (2 * s + kv), 32 * (2 * s + kv) + 32)
                        qr, qn = qs[half, 0, seq, :], qs[half, 1, seq, :]
                        for n in range(2):
                            nc.tensor.matmul(past[rows, n * 512:(n + 1) * 512], qr,
                                             kv_pages[half, b, PAGES * s + 4 * n:PAGES * s + 4 * n + 4, 0:P],
                                             start=True, stop=True)
                        nc.tensor.matmul(win[rows, :], qr, wk[half, b, s, :], start=True, stop=True)
                        pcmp, pseln, pwinn = parts(small)
                        nc.tensor.matmul(pcmp[rows, :], qn, k.kc[half, seq, 0:CH - 1], start=True, stop=True)
                        nc.tensor.matmul(pseln[rows, :], qr, Z[half, ZK + 2, SEQ:T], start=True, stop=True)
                        nc.tensor.matmul(pwinn[rows, :], qr, Z[half, ZK + 4, SEQ:T], start=True, stop=True)
                nc.tensor.matmul(grow, pick[:, g, :], k.gates[0:TS, 4, :], start=True, stop=True).then_inc(e_at, 1)

            def importance(g):
                pe.wait_ge(v_at, step(V, "pc", g))
                nc.tensor.matmul(isum, same[:], pc[:, 0:CH - 1], start=True, stop=True).then_inc(e_at, 1)

            def turn_past(g):
                pe.wait_ge(v_at, step(V, "weighted", g))
                if g:
                    pe.wait_ge(v_at, step(V, "out", g - 1))
                for n in range(12):
                    mm = nc.tensor.transpose(k.ps[:, 5 + n // 4, (n % 4) * P:(n % 4) * P + P], E[:, g % 2, n * P:(n + 1) * P],
                                             k.ident[:])
                mm.then_inc(e_at, 1)

            def turn_rest_and_mix(g):
                pe.wait_ge(s_at, step(S, "laid1", g))
                for n, name in enumerate(("seln", "winn", "cmp")):
                    mm = nc.tensor.transpose(k.ps[0:KEYS[name][1], 5, n * P:n * P + P], probs(name, g), k.ident[:])
                mm.then_inc(e_at, 1)
                pe.wait_ge(s_at, step(S, "laid2", g))
                b = g % cached.SLOTS
                for s in range(2):
                    seq = 2 * g + s
                    cols = slice(CH * s, CH * s + CH)
                    terms = [(kv_pages[:, b, PAGES * s + n, P:2 * P], PT[:, n, cols]) for n in range(PAGES)]
                    terms += [(wv[:, b, s, n, :], PT[:, PAGES + n, cols]) for n in range(4)]
                    terms += [(k.vs[0:TS, 4, :], PT[0:TS, 12, cols]), (k.vw[0:TS, 4, :], PT[0:TS, 13, cols]),
                              (k.vc[0:CH - 1, seq, :], PT[0:CH - 1, 14, cols])]
                    for n, (lhs, rhs) in enumerate(terms):
                        mm = nc.tensor.matmul(mix[:, cols], lhs, rhs, start=n == 0, stop=n == len(terms) - 1)
                mm.then_inc(e_at, 1)

            scores(0)
            importance(0)
            for g in range(NG):
                if g + 1 < NG:
                    scores(g + 1)
                turn_past(g)
                if g + 1 < NG:
                    importance(g + 1)
                turn_rest_and_mix(g)

        @block.scalar
        def _(act):
            def exp_cmp(g):
                act.wait_ge(v_at, step(V, "cmpmax", g))
                if g >= 2:
                    act.wait_ge(e_at, step(PE, "turned2", g - 2))
                nc.scalar.activation(probs("cmp", g), cmp, ACT.Exp, bias=nm[:, 0:1], scale=SCALE,
                                     accum_out=sums[:, 0:1]).then_inc(s_at, 1)

            def exp_rest(g):
                act.wait_ge(v_at, step(V, "maxes", g))
                for n, (name, src, b) in enumerate((("sel", past, 1), ("seln", seln, 1), ("win", win, 2),
                                                    ("winn", winn, 2))):
                    last = nc.scalar.activation(probs(name, g), src, ACT.Exp, bias=nm[:, b:b + 1], scale=SCALE,
                                                accum_out=sums[:, 1 + n:2 + n])
                last.then_inc(s_at, 1)

            exp_cmp(0)
            exp_rest(0)
            for g in range(NG):
                act.wait_ge(e_at, step(PE, "turned1", g))
                nc.scalar.activation(PT[:, 0:12, :].rearrange("p c q -> p (c q)"),
                                     k.ps[:, 5:8, :].rearrange("p b n -> p (b n)"), ACT.Copy).then_inc(s_at, 1)
                if g + 1 < NG:
                    exp_cmp(g + 1)
                act.wait_ge(e_at, step(PE, "turned2", g))
                nc.scalar.activation(PT[0:TS, 12:14, :].rearrange("p c q -> p (c q)"), k.ps[0:TS, 5, 0:2 * P], ACT.Copy)
                nc.scalar.activation(PT[0:CH - 1, 14, :], k.ps[0:CH - 1, 5, 2 * P:3 * P], ACT.Copy).then_inc(s_at, 1)
                if g + 1 < NG:
                    exp_rest(g + 1)

        @block.vector
        def _(dve):
            ch = Chain(dve, chain)
            for m, src in enumerate((k.qr, Z[:, ZQ:ZQ + 4, :])):
                for i in range(4):
                    last = nc.vector.tensor_copy(qs[:, m].rearrange("p s (i t) -> p s i t", i=4)[:, :, i, :],
                                                 src[:, i, SEQ:T].rearrange("p (s t) -> p s t", t=DEC_SEQ))
                last.then_inc(packed, 1)
            dve.wait_ge(loaded, 16 * len(tables))
            def choose_blocks(g):
                dve.wait_ge(e_at, step(PE, "scores", g))
                for dst, src in zip(parts(near), parts(small)):
                    last = nc.vector.tensor_copy(dst, src)
                ch.link(last)
                ch.link(nc.vector.tensor_reduce(mx[:, 0:1], cmp, AX.X, ALU.max))
                nc.vector.tensor_scalar(nm[:, 0:1], mx[:, 0:1], -SCALE, None, ALU.mult).then_inc(v_at, 1)
                nc.vector.tensor_tensor(seln, seln, newmask[:, g, :], ALU.add)
                nc.vector.tensor_tensor(winn, winn, newmask[:, g, :], ALU.add)
                nc.vector.tensor_tensor(win[:, 0:DEC_SEQ], win[:, 0:DEC_SEQ], winmask[:], ALU.add)
                ch.link(nc.vector.tensor_tensor(gsel[:], grow, headmask[:], ALU.mult))
                nc.vector.tensor_reduce(gr[:, g % 2], gsel.rearrange("p (h b) -> p b h", b=3), AX.X, ALU.add)
                nc.vector.tensor_reduce(mx[:, 1:2], seln, AX.X, ALU.max)
                nc.vector.tensor_reduce(mx[:, 2:3], win, AX.X, ALU.max)
                ch.link(nc.vector.tensor_reduce(mx[:, 3:4], winn, AX.X, ALU.max))
                dve.wait_ge(s_at, step(S, "cmpexp", g))
                ch.link(nc.vector.tensor_scalar(wts[:, 0:1], sums[:, 0:1], 1e-30, None, ALU.max))
                ch.link(nc.vector.reciprocal(wts[:, 0:1], wts[:, 0:1]))
                nc.vector.tensor_scalar(pc[:, 0:CH - 1], probs("cmp", g), wts[:, 0:1], None, ALU.mult).then_inc(v_at, 1)
                dve.wait_ge(e_at, step(PE, "imp", g))
                ch.link(nc.vector.tensor_copy(pc[:, 0:CH - 1], isum))
                windows = pc[:, 3:3 + 4 * 14].rearrange("p (j c) -> p j c", c=4)
                ch.link(nc.vector.tensor_reduce(imp[:], windows, AX.X, ALU.add))
                ch.link(nc.vector.tensor_tensor(imp[:], imp[:], pc[:, 7:7 + 4 * 14:4], ALU.add))
                ch.link(nc.vector.tensor_reduce(one[:, 0:1], imp[:], AX.X, ALU.min))
                ch.link(nc.vector.tensor_scalar(pen[:], imp[:], one[:, 0:1], None, ALU.is_le))
                ch.link(nc.vector.tensor_tensor(pen[:], pen[:], iota[:], ALU.mult))
                ch.link(nc.vector.tensor_reduce(one[:, 1:2], pen[:], AX.X, ALU.max))
                ch.link(nc.vector.tensor_scalar(pen[:], iota[:], one[:, 1:2], NEG, ALU.is_equal, ALU.mult))
                blocks = past[:, SEL_BLOCK:15 * SEL_BLOCK].rearrange("p (j c) -> p j c", c=SEL_BLOCK)
                ch.link(nc.vector.tensor_tensor(blocks, blocks, pen.rearrange("p (j o) -> p j o", o=1)
                                                .broadcast_to([P, 14, SEL_BLOCK]), ALU.add))
                ch.link(nc.vector.tensor_reduce(mx[:, 4:5], past, AX.X, ALU.max))
                ch.link(nc.vector.tensor_tensor(mx[:, 0:1], mx[:, 4:5], mx[:, 1:2], ALU.max))
                ch.link(nc.vector.tensor_tensor(mx[:, 1:2], mx[:, 2:3], mx[:, 3:4], ALU.max))
                nc.vector.tensor_scalar(nm[:, 1:3], mx[:, 0:2], -SCALE, None, ALU.mult).then_inc(v_at, 1)

            def weigh(g):
                dve.wait_ge(s_at, step(S, "exps", g))
                nc.vector.tensor_tensor(wts[:, 1:2], sums[:, 1:2], sums[:, 2:3], ALU.add)
                ch.link(nc.vector.tensor_tensor(wts[:, 2:3], sums[:, 3:4], sums[:, 4:5], ALU.add))
                ch.link(nc.vector.tensor_scalar(wts[:, 1:3], wts[:, 1:3], 1e-30, None, ALU.max))
                ch.link(nc.vector.reciprocal(wts[:, 1:3], wts[:, 1:3]))
                ch.link(nc.vector.tensor_tensor(wts[:], wts[:], gr[:, g % 2], ALU.mult))
                for name, b in (("sel", 1), ("seln", 1), ("win", 2), ("winn", 2), ("cmp", 0)):
                    last = nc.vector.tensor_scalar(probs(name, g), probs(name, g), wts[:, b:b + 1], None, ALU.mult)
                last.then_inc(v_at, 1)

            def take_out(g):
                dve.wait_ge(e_at, step(PE, "mixed", g))
                for kv in range(2):
                    half = slice(kv * HD, kv * HD + HD)
                    for s in range(2):
                        at = SEQ + (2 * g + s) * DEC_SEQ
                        src = mix[half, CH * s + 32 * kv:CH * s + 32 * kv + 32].rearrange("p (i t) -> p i t", i=4)
                        last = nc.vector.tensor_copy(k.on[half, :, at:at + DEC_SEQ], src)
                last.then_inc(v_at, 1)

            choose_blocks(0)
            for g in range(NG):
                weigh(g)
                if g + 1 < NG:
                    choose_blocks(g + 1)
                take_out(g)


def merge_stage(k, m_hi, m_lo, w_out):
    nc = k.nc
    out = k.z[:, 8:16, :]
    ring = 4
    with ExitStack() as ctx:
        wt = k.sb(ctx, "wt", [P, ring, KD, P])
        tmp = k.sb(ctx, "tmp", [P, T])
        arrived = k.sems(ctx, *[f"arrived{b}" for b in range(ring)])
        multiplied, gated, merged, rounded, chain = k.sems(ctx, "multiplied", "gated", "merged", "rounded", "chain")
        block = ctx.enter_context(nc.Block())

        @block.sync
        def _(sp):
            for n in range(KD):
                if n >= ring:
                    sp.wait_ge(multiplied, n - ring + 1)
                sp.dma_start(wt[:, n % ring].rearrange("p c n -> p (c n)"), k.d["w_merge"][n]).then_inc(arrived[n % ring], 16)
            w_out.load_first(sp)

        @block.tensor
        def _(pe):
            for n in range(KD):
                pe.wait_ge(arrived[n % ring], 16 * (n // ring + 1))
                if n >= 2:
                    pe.wait_ge(merged, n - 1)
                for branch, src in enumerate((k.r.o, k.on)):
                    for c in range(4):
                        for h in range(2):
                            mm = nc.tensor.matmul(k.bank(4 * (n % 2) + 2 * branch + h, TH), wt[:, n % ring, 4 * branch + c, :],
                                                  src[:, c, h * TH:(h + 1) * TH], start=c == 0, stop=c == 3)
                mm.then_inc(multiplied, 1)

        @block.scalar
        def _(act):
            for n in range(KD):
                nc.scalar.activation(k.zg[:, n, :], k.zg[:, n, :], ACT.Sigmoid)
                nc.scalar.activation(k.zg[:, KD + n, :], k.zg[:, KD + n, :], ACT.Sigmoid).then_inc(gated, 1)
            for n in range(KD):
                act.wait_ge(merged, n + 1)
                nc.scalar.activation(m_hi[:, n, :], out[:, n, :], ACT.Copy).then_inc(rounded, 1)

        @block.vector
        def _(dve):
            ch = Chain(dve, chain)
            for n in range(KD):
                dve.wait_ge(gated, n + 1)
                dve.wait_ge(multiplied, n + 1)
                if n:
                    dve.wait_ge(merged, n)
                b = 4 * (n % 2)
                nc.vector.tensor_tensor(halves(out[:, n, :]), k.pair(b), halves(k.zg[:, n, :]), ALU.mult)
                ch.link(nc.vector.tensor_tensor(halves(tmp[:]), k.pair(b + 2), halves(k.zg[:, KD + n, :]), ALU.mult))
                nc.vector.tensor_tensor(out[:, n, :], out[:, n, :], tmp[:], ALU.add).then_inc(merged, 1)
            for n in range(KD):
                dve.wait_ge(rounded, n + 1)
                last = nc.vector.tensor_tensor(m_lo[:, n, :], out[:, n, :], m_hi[:, n, :].bitcast(F32), ALU.subtract)
            ch.link(last)


def choose_stage(k, q, picked):
    nc = k.nc
    WIDE = 4
    NWIDE = WIDE * TOPK
    NCAND = NWIDE + (TOPK - WIDE) * 4
    tiles = [(tt * P, min(P, T - tt * P)) for tt in range(5)]
    HC = 2 * HEADS
    with ExitStack() as ctx:
        keys = k.sb(ctx, "keys", [P, HEADS, N_KEYS])
        sc = k.sb(ctx, "sc", [P, 2, HC, N_KEYS])
        sv = k.sb(ctx, "sv", [P, HC, TOPK])
        si = k.sb(ctx, "si", [P, HC, TOPK], U32)
        sif = k.sb(ctx, "sif", [P, HC, TOPK])
        cand = k.sb(ctx, "cand", [P, HEADS, NCAND])
        cv = k.sb(ctx, "cv", [P, HEADS, TOPK])
        ci = k.sb(ctx, "ci", [P, HEADS, TOPK], U32)
        cj = k.sb(ctx, "cj", [P, 4, HEADS * TOPK], U32)
        cjf = k.sb(ctx, "cjf", [P, 4, HEADS * TOPK])
        far = k.sb(ctx, "far", [P, HEADS * TOPK])
        hot = k.sb(ctx, "hot", [P, 2, HEADS * TOPK, TOPK])
        num = k.sb(ctx, "num", [P, 3, HEADS * TOPK])
        ex = k.sb(ctx, "ex", [P, HEADS, TOPK])
        tot = k.sb(ctx, "tot", [P, HEADS])
        iota = k.sb(ctx, "iota", [P, TOPK])
        loaded, scored, copied, lowered, exped, placed, numbered, chosen, turned, laid, chain = k.sems(
            ctx, "loaded", "scored", "copied", "lowered", "exped", "placed", "numbered", "chosen", "turned", "laid",
            "chain")
        block = ctx.enter_context(nc.Block())

        @block.sync
        def _(sp):
            sp.dma_start(keys.rearrange("p h n -> p (h n)"), k.d["keys"]).then_inc(loaded, 16)
            sp.dma_start(iota[:], k.d["iota16"]).then_inc(loaded, 16)

        @block.tensor
        def _(pe):
            pe.wait_ge(loaded, 32)

            def scores(n):
                at, rows = tiles[n]
                if n:
                    pe.wait_ge(copied, n)
                for h in range(HEADS):
                    for c in range(2):
                        half = slice(c * HD, c * HD + HD)
                        mm = nc.tensor.matmul(k.ps[0:rows, 2 * c + h // 4, (h % 4) * N_KEYS:(h % 4 + 1) * N_KEYS],
                                              q[half, h, at:at + rows], keys[half, h, :], start=True, stop=True)
                mm.then_inc(scored, 1)

            scores(0)
            for n, (at, rows) in enumerate(tiles):
                if n + 1 < len(tiles):
                    scores(n + 1)
                pe.wait_ge(chosen, n + 1)
                if n:
                    pe.wait_ge(laid, n)
                for m in range(3):
                    mm = nc.tensor.transpose(k.ps[:, 4, m * P:m * P + rows], num[0:rows, m, :], k.ident[0:rows, 0:rows])
                mm.then_inc(turned, 1)

        @block.scalar
        def _(act):
            def copy_scores(n):
                rows = tiles[n][1]
                act.wait_ge(scored, n + 1)
                nc.scalar.activation(sc[0:rows, 0].rearrange("p a n -> p (a n)"),
                                     k.ps[0:rows, 0:4, :].rearrange("p b n -> p (b n)"), ACT.Copy).then_inc(copied, 1)

            copy_scores(0)
            for n, (at, rows) in enumerate(tiles):
                act.wait_ge(lowered, n + 1)
                nc.scalar.activation(ex[0:rows], ex[0:rows], ACT.Exp).then_inc(exped, 1)
                if n + 1 < len(tiles):
                    copy_scores(n + 1)
                act.wait_ge(turned, n + 1)
                nc.scalar.activation(picked[:, :, at:at + rows],
                                     k.ps[:, 4, 0:3 * P].rearrange("p (m t) -> p m t", m=3)[:, :, 0:rows],
                                     ACT.Copy).then_inc(laid, 1)

        @block.gpsimd
        def _(pool):
            for n, (at, rows) in enumerate(tiles):
                r = slice(0, rows)
                for c in range(2):
                    which = sif[r, c * HEADS:(c + 1) * HEADS, :].rearrange("p h (o j) -> p h o j", o=1) \
                        .broadcast_to([rows, HEADS, TOPK, TOPK])
                    hot4 = hot[r, c].rearrange("p (h a) j -> p h a j", h=HEADS)
                    pool.wait_ge(placed, 2 * n + c + 1)
                    nc.gpsimd.tensor_tensor(hot4, hot4, which, ALU.mult).then_inc(numbered, 1)

        @block.vector
        def _(dve):
            ch = Chain(dve, chain)
            dve.wait_ge(loaded, 32)

            def top16(src, spare, val, idx, count, rows):
                for n in range(count):
                    last = nc.vector.max(val[0:rows, n, 0:8], src(n))
                ch.link(last)
                for n in range(count):
                    nc.vector.max_index(idx[0:rows, n, 0:8], val[0:rows, n, 0:8], src(n))
                    last = nc.vector.match_replace(spare(n), val[0:rows, n, 0:8], src(n), NEG)
                ch.link(last)
                for n in range(count):
                    last = nc.vector.max(val[0:rows, n, 8:16], spare(n))
                ch.link(last)
                for n in range(count):
                    last = nc.vector.max_index(idx[0:rows, n, 8:16], val[0:rows, n, 8:16], spare(n))
                ch.link(last)

            def finish(n):
                r = slice(0, tiles[n][1])
                rows = tiles[n][1]
                dve.wait_ge(exped, n + 1)
                ch.link(nc.vector.tensor_reduce(tot[r], ex[r], AX.X, ALU.add))
                ch.link(nc.vector.reciprocal(tot[r], tot[r]))
                if n:
                    dve.wait_ge(turned, n)
                for c in range(2):
                    dve.wait_ge(numbered, 2 * n + c + 1)
                    nc.vector.tensor_reduce(num[r, c, :], hot[r, c], AX.X, ALU.add)
                nc.vector.tensor_tensor(num[r, 2, :].rearrange("p (h j) -> p h j", h=HEADS), ex[r],
                                        tot[r].rearrange("p (h o) -> p h o", o=1).broadcast_to([rows, HEADS, TOPK]),
                                        ALU.mult).then_inc(chosen, 1)

            for n, (at, rows) in enumerate(tiles):
                r = slice(0, rows)
                dve.wait_ge(copied, n + 1)
                top16(lambda m: sc[r, 0, m, :], lambda m: sc[r, 1, m, :], sv, si, HC, rows)
                if n:
                    finish(n - 1)
                nc.vector.tensor_copy(sif[r], si[r])
                for i0, i1, width in ((0, WIDE, TOPK), (WIDE, TOPK, 4)):
                    shape = [rows, HEADS, i1 - i0, width]
                    first = sv[r, 0:HEADS, i0:i1].rearrange("p h (j o) -> p h j o", o=1).broadcast_to(shape)
                    second = sv[r, HEADS:, 0:width].rearrange("p h (o j) -> p h o j", o=1).broadcast_to(shape)
                    place = slice(0, NWIDE) if i0 == 0 else slice(NWIDE, NCAND)
                    last = nc.vector.tensor_tensor(cand[r, :, place].rearrange("p h (i j) -> p h i j", j=width), first, second,
                                                   ALU.add)
                ch.link(last)
                spare = sc[:, 1].rearrange("p a n -> p (a n)")[:, 0:HEADS * NCAND].rearrange("p (h m) -> p h m", h=HEADS)
                top16(lambda m: cand[r, m, :], lambda m: spare[r, m, :], cv, ci, HEADS, rows)
                flat = ci[r].rearrange("p h j -> p (h j)")
                nc.vector.tensor_scalar(cj[r, 0], flat, 4, None, ALU.logical_shift_right)
                nc.vector.tensor_scalar(cj[r, 1], flat, 15, None, ALU.bitwise_and)
                nc.vector.tensor_scalar(cj[r, 2], flat, 2, None, ALU.logical_shift_right)
                nc.vector.tensor_scalar(cj[r, 3], flat, 3, None, ALU.bitwise_and)
                ch.link(nc.vector.tensor_tensor(ex[r], cv[r], cv[r, :, 0:1].broadcast_to([rows, HEADS, TOPK]),
                                                ALU.subtract))
                nc.vector.tensor_copy(cjf[r], cj[r]).then_inc(lowered, 1)
                dve.wait_ge(lowered, n + 1)
                ch.link(nc.vector.tensor_scalar(far[r], cjf[r, 2], float(NWIDE // 4), None, ALU.is_ge))
                ch.link(nc.vector.tensor_scalar(cjf[r, 2], cjf[r, 2], float(WIDE - NWIDE // 4), None, ALU.add))
                ch.link(nc.vector.tensor_tensor(cjf[r, 2:4], cjf[r, 2:4], cjf[r, 0:2], ALU.subtract))
                ch.link(nc.vector.tensor_tensor(cjf[r, 2:4], cjf[r, 2:4], far[r].rearrange("p (o a) -> p o a", o=1)
                                                .broadcast_to([rows, 2, HEADS * TOPK]), ALU.mult))
                ch.link(nc.vector.tensor_tensor(cjf[r, 0:2], cjf[r, 0:2], cjf[r, 2:4], ALU.add))
                for c in range(2):
                    place = cjf[r, c, :].rearrange("p (a o) -> p a o", o=1).broadcast_to([rows, P, TOPK])
                    slot = iota[r].rearrange("p (o j) -> p o j", o=1).broadcast_to([rows, P, TOPK])
                    nc.vector.tensor_tensor(hot[r, c], place, slot, ALU.is_equal).then_inc(placed, 1)
            finish(len(tiles) - 1)


class ExpertRows:
    SIZE = 4

    def __init__(self, k, ctx):
        self.k = k
        self.tiles = k.sb(ctx, "u_raw", [P, self.SIZE, KD, P])
        self.landed = k.sems(ctx, *[f"u_in{e}" for e in range(self.SIZE)])

    def load(self, sp, i, e):
        sp.dma_start(self.tiles[:, e].rearrange("p c n -> p (c n)"),
                     self.k.d["peer_u"][bass.ds(i * self.SIZE + e, 1)].rearrange("o p n -> (o p) n")).then_inc(
                         self.landed[e], 16)


def gate_matrix_stage(k, picked, experts):
    nc = k.nc
    Q = 8
    QB = 512 // N_KEYS
    rounds = T // (2 * TB)
    with ExitStack() as ctx:
        hot = k.sb(ctx, "hot", [P, 2, TB, N_KEYS])
        a, b = hot[:, 0], hot[:, 1]
        nq = TB // Q
        cur = k.sb(ctx, "cur", [P, 2, 3, TB])
        G = k.sb(ctx, "g", [P, 2, N_KEYS, TB])
        iota = k.sb(ctx, "iota", [P, N_KEYS])
        loaded, current, both_made, a_made, b_made, weighted, spread, taken, stored0, stored1, passed = k.sems(
            ctx, "loaded", "current", "both_made", "a_made", "b_made", "weighted", "spread", "taken", "stored0",
            "stored1", "passed")
        stored = (stored0, stored1)
        block = ctx.enter_context(nc.Block())

        @block.sync
        def _(sp):
            sp.dma_start(iota[:], k.d["iota128"]).then_inc(loaded, 16)
            for e in range(experts.SIZE):
                experts.load(sp, 0, e)
            with sp.Fori(0, rounds) as i:
                for s in range(2):
                    sp.wait_ge(taken, (i * 2 + s) * nq + nq + nq)
                    sp.dma_start(k.g_dram[bass.ds(i * 2 + s, 1)].rearrange("o p n -> (o p) n"),
                                 G[:, s].rearrange("p n t -> p (n t)")).then_inc(stored[s], 16)
            for s in range(2):
                sp.wait_ge(stored[s], 16 * (rounds + 1))

        @block.vector
        def _(dve):
            dve.sem_inc(spread, nq)
            dve.wait_ge(loaded, 16)
            with dve.Fori(0, rounds) as i:
                for s in range(2):
                    dve.wait_ge(spread, (i * 2 + s) * nq + 1)
                    nc.vector.tensor_copy(cur[:, s], picked[:, :, bass.ds(i * 2 * TB + s * TB, TB)]).then_inc(current, 1)
                    dve.wait_ge(current, i * 2 + s + 1)
                    for q in range(nq):
                        dve.wait_ge(spread, (i * 2 + s) * nq + q + 1)
                        t = Q * q + Q // 2
                        slots = iota.rearrange("p (o m n) -> p o m n", o=1, m=1).broadcast_to([P, 2, Q // 2, N_KEYS])
                        keys = cur[:, s, 0:2, t:t + Q // 2].rearrange("p c (t o) -> p c t o", o=1) \
                            .broadcast_to([P, 2, Q // 2, N_KEYS])
                        nc.vector.tensor_tensor(hot[:, :, t:t + Q // 2, :], slots, keys, ALU.is_equal).then_inc(both_made, 1)
                        for t in range(Q * q, Q * q + Q // 2):
                            last = nc.vector.tensor_scalar(a[:, t, :], iota[:], cur[:, s, 0, t:t + 1], cur[:, s, 2, t:t + 1],
                                                           ALU.is_equal, ALU.mult)
                        last.then_inc(a_made, 1)

        @block.gpsimd
        def _(pool):
            pool.wait_ge(loaded, 16)
            with pool.Fori(0, rounds) as i:
                for s in range(2):
                    pool.wait_ge(current, i * 2 + s + 1)
                    for q in range(nq):
                        pool.wait_ge(spread, (i * 2 + s) * nq + q + 1)
                        pool.sem_inc(passed, 1)
                        for t in range(Q * q, Q * q + Q // 2):
                            last = nc.gpsimd.tensor_scalar(b[:, t, :], iota[:], cur[:, s, 1, t:t + 1], None, ALU.is_equal)
                        last.then_inc(b_made, 1)

        @block.tensor
        def _(pe):
            with pe.Fori(0, rounds) as i:
                for s in range(2):
                    for q in range(nq):
                        pe.wait_ge(a_made, (i * 2 + s) * nq + q + 1)
                        pe.wait_ge(b_made, (i * 2 + s) * nq + q + 1)
                        pe.wait_ge(weighted, (i * 2 + s) * nq + q + 1)
                        pe.wait_ge(taken, (i * 2 + s) * nq + q + 1)
                        for t in range(Q * q, Q * q + Q):
                            mm = nc.tensor.matmul(k.ps[:, t // QB, (t % QB) * P:(t % QB + 1) * P], b[:, t, :], a[:, t, :],
                                                  start=True, stop=True)
                        mm.then_inc(spread, 1)

        @block.scalar
        def _(act):
            act.sem_inc(taken, nq)
            for s in range(2):
                act.sem_inc(stored[s], 16)
            with act.Fori(0, rounds) as i:
                for step in range(2 * nq + 1):
                    if step < 2 * nq:
                        s, q = step // nq, step % nq
                        act.wait_ge(both_made, i * 2 * nq + step + 1)
                        for t in range(Q * q + Q // 2, Q * q + Q):
                            last = nc.scalar.activation(a[:, t, :], a[:, t, :], ACT.Copy, scale=cur[:, s, 2, t:t + 1])
                        last.then_inc(weighted, 1)
                    if step:
                        s, q = (step - 1) // nq, (step - 1) % nq
                        if q == 0:
                            act.wait_ge(stored[s], i * 16 + 16)
                        act.wait_ge(spread, i * 2 * nq + step - 1 + nq + 1)
                        nc.scalar.activation(G[:, s, :, Q * q:Q * q + Q].rearrange("p n t -> p t n"),
                                             k.ps[:, Q // QB * q:Q // QB * (q + 1), :].rearrange("p b (t n) -> p (b t) n", t=QB),
                                             ACT.Copy).then_inc(taken, 1)


def experts_stage(k, h, y, experts):
    nc = k.nc
    EG = experts.SIZE
    groups = N_KEYS // EG
    h_hi, h_lo = h
    with ExitStack() as ctx:
        u_raw, u_in = experts.tiles, experts.landed
        u_hi = k.sb(ctx, "u_hi", [P, 2, KD, P], F32R)
        u_lo = k.sb(ctx, "u_lo", [P, 2, KD, P], F32R)
        v_raw = k.sb(ctx, "v_raw", [P, 2, D_MODEL])
        v_hi = k.sb(ctx, "v_hi", [P, EG, D_MODEL], F32R)
        v_lo = k.sb(ctx, "v_lo", [P, EG, D_MODEL], F32R)
        G = k.sb(ctx, "g", [P, T // TB, EG, TB])
        act_t = k.sb(ctx, "act", [P, 2, T])
        w = k.sb(ctx, "w", [P, T])
        w_hi = k.sb(ctx, "w_hi", [P, EG, T], F32R)
        w_lo = k.sb(ctx, "w_lo", [P, EG, T], F32R)
        v_in = k.sems(ctx, "v_in0", "v_in1")
        (g_in, u_rounded, u_parted, v_rounded, v_parted, up, gelued, gated, w_rounded, weighed, down, added,
         cleared) = k.sems(ctx, "g_in", "u_rounded", "u_parted", "v_rounded", "v_parted", "up", "gelued", "gated",
                           "w_rounded", "weighed", "down", "added", "cleared")
        U0, V0, GE0, WE0, DN0, AD0 = EG, 2, 2, 2, KD, 2
        block = ctx.enter_context(nc.Block())

        @block.sync
        def _(sp):
            def load_group(i):
                sp.wait_ge(weighed, i * EG + WE0)
                sp.dma_start(G.rearrange("p c e t -> p c (e t)"),
                             k.g_dram.rearrange("c p n -> p c n")[:, :, bass.ds(i * (EG * TB), EG * TB)]).then_inc(g_in, 16)
                for e in range(EG):
                    sp.wait_ge(v_parted, i * EG + e + 1)
                    sp.dma_start(v_raw[:, e % 2],
                                 k.d["peer_v"][bass.ds(i * EG + e, 1)].rearrange("o p n -> (o p) n")).then_inc(v_in[e % 2], 16)

            with sp.Fori(0, groups - 1) as i:
                load_group(i)
                for e in range(EG):
                    sp.wait_ge(u_parted, i * EG + U0 + e + 1)
                    experts.load(sp, i + 1, e)
            load_group(groups - 1)

        @block.gpsimd
        def _(pool):
            nc.gpsimd.memset(y[:], 0.0).then_inc(cleared, 1)

        @block.tensor
        def _(pe):
            pe.sem_inc(down, DN0)
            with pe.Fori(0, groups) as i:
                for e in range(EG):
                    pe.wait_ge(u_parted, i * EG + U0 + e + 1)
                    pe.wait_ge(gelued, i * EG + e + 1)
                    for c in range(KD):
                        for n, (lhs, r) in enumerate(three_passes(u_hi[:, e % 2, c, :], u_lo[:, e % 2, c, :], h_hi, h_lo)):
                            for s in range(2):
                                mm = nc.tensor.matmul(k.bank(2 * (e % 2) + s, TH), lhs, r[:, c, s * TH:(s + 1) * TH],
                                                      start=c == 0 and n == 0, stop=c == KD - 1 and n == 2)
                    mm.then_inc(up, 1)
                pe.wait_ge(v_parted, i * EG + V0 + EG)
                for d in range(KD):
                    pe.wait_ge(added, i * KD + d + 1)
                    for e in range(EG):
                        if d == 0 and e in (0, EG - 1):
                            pe.wait_ge(weighed, i * EG + WE0 + (EG if e else EG - 1))
                        for n, (lhs, r) in enumerate(three_passes(v_hi[:, e, d * P:(d + 1) * P], v_lo[:, e, d * P:(d + 1) * P],
                                                                  w_hi, w_lo)):
                            for s in range(2):
                                mm = nc.tensor.matmul(k.bank(4 + 2 * (d % 2) + s, TH), lhs, r[:, e, s * TH:(s + 1) * TH],
                                                      start=e == 0 and n == 0, stop=e == EG - 1 and n == 2)
                    mm.then_inc(down, 1)

        def parts_ahead(last):
            return () if last else (0, 1)

        @block.scalar
        def _(act):
            def round_u(i, e, first=False):
                act.wait_ge(u_in[e], i * 16 + 16)
                if not first:
                    act.wait_ge(up, i * EG + e - 1)
                nc.scalar.activation(u_hi[:, e % 2], u_raw[:, e], ACT.Copy).then_inc(u_rounded, 1)

            def round_group(i, last):
                for e in range(EG):
                    act.wait_ge(v_in[e % 2], i * 32 + 16 * (e // 2 + 1))
                    act.wait_ge(down, i * KD + DN0)
                    nc.scalar.activation(v_hi[:, e, :], v_raw[:, e % 2, :], ACT.Copy).then_inc(v_rounded, 1)
                    act.wait_ge(up, i * EG + e + 1)
                    act.wait_ge(weighed, i * EG + e + 1)
                    nc.scalar.activation(halves(act_t[:, e % 2, :]), k.pair(2 * (e % 2)), ACT.Gelu_apprx_tanh).then_inc(gelued, 1)
                    if e < EG - 2:
                        round_u(i, e + 2)
                for e in parts_ahead(last):
                    round_u(i + 1, e)

            act.sem_inc(gelued, GE0)
            for e in range(2):
                round_u(0, e, first=True)
            with act.Fori(0, groups - 1) as i:
                round_group(i, False)
            round_group(groups - 1, True)

        @block.vector
        def _(dve):
            def part_u(i, e):
                dve.wait_ge(u_rounded, i * EG + e + 1)
                nc.vector.tensor_tensor(u_lo[:, e % 2], u_raw[:, e], u_hi[:, e % 2].bitcast(F32),
                                        ALU.subtract).then_inc(u_parted, 1)

            def round_group(i, last):
                dve.wait_ge(g_in, i * 16 + 16)
                for e in range(EG):
                    dve.wait_ge(v_rounded, i * EG + e + 1)
                    nc.vector.tensor_tensor(v_lo[:, e, :], v_raw[:, e % 2, :], v_hi[:, e, :].bitcast(F32),
                                            ALU.subtract).then_inc(v_parted, 1)
                    dve.wait_ge(gelued, i * EG + GE0 + e + 1)
                    dve.wait_ge(weighed, i * EG + WE0 + e)
                    nc.vector.tensor_tensor(w.rearrange("p (c t) -> p c t", t=TB),
                                            act_t[:, e % 2, :].rearrange("p (c t) -> p c t", t=TB), G[:, :, e, :],
                                            ALU.mult).then_inc(gated, 1)
                    dve.wait_ge(gated, i * EG + e + 1)
                    nc.vector.tensor_copy(w_hi[:, e, :], w[:]).then_inc(w_rounded, 1)
                    dve.wait_ge(w_rounded, i * EG + e + 1)
                    nc.vector.tensor_tensor(w_lo[:, e, :], w[:], w_hi[:, e, :].bitcast(F32), ALU.subtract).then_inc(weighed, 1)
                    if e < EG - 2:
                        part_u(i, e + 2)
                for e in parts_ahead(last):
                    part_u(i + 1, e)
                for d in range(KD):
                    dve.wait_ge(down, i * KD + DN0 + d + 1)
                    nc.vector.tensor_tensor(halves(y[:, d, :]), k.pair(4 + 2 * (d % 2)), halves(y[:, d, :]),
                                            ALU.add).then_inc(added, 1)

            dve.sem_inc(u_parted, U0)
            dve.sem_inc(v_parted, V0)
            dve.sem_inc(weighed, WE0)
            dve.sem_inc(added, AD0)
            for e in range(2):
                part_u(0, e)
            dve.wait_ge(cleared, 1)
            with dve.Fori(0, groups - 1) as i:
                round_group(i, False)
            round_group(groups - 1, True)


def embed_stage(k, h, weights):
    nc = k.nc
    ring, wt, arrived = weights.SIZE, weights.tiles, weights.arrived
    with ExitStack() as ctx:
        w_hi = k.sb(ctx, "w_hi", [P, 2, KD, P], F32R)
        w_lo = k.sb(ctx, "w_lo", [P, 2, KD, P], F32R)
        p = k.sb(ctx, "p", [P, 2, T])
        sig = k.sb(ctx, "sig", [P, 2, T])
        loaded, rounded, parted, multiplied, gated, made, stored, chain = k.sems(
            ctx, "loaded", "rounded", "parted", "multiplied", "gated", "made", "stored", "chain")
        block = ctx.enter_context(nc.Block())

        @block.sync
        def _(sp):
            sp.dma_start(p.rearrange("p c t -> p (c t)"), k.d["p"]).then_inc(loaded, 16)
            for n in range(ring, KD):
                sp.wait_ge(multiplied, n - ring + 1)
                weights.load(sp, n, n % ring)
            for n in range(KD):
                sp.wait_ge(made, n + 1)
                sp.dma_start(k.d["out_y"][n], k.x[:, n, :]).then_inc(stored, 16)
            sp.wait_ge(stored, 16 * KD)

        @block.tensor
        def _(pe):
            pe.wait_ge(loaded, 16)
            for n in range(KD):
                pe.wait_ge(parted, n + 1)
                if n >= 2:
                    pe.wait_ge(made, n - 1)
                for c in range(KD):
                    for m, (lhs, r) in enumerate(three_passes(w_hi[:, n % 2, c, :], w_lo[:, n % 2, c, :], *h)):
                        for s in range(2):
                            mm = nc.tensor.matmul(k.bank(4 * (n % 2) + s, TH), lhs, r[:, c, s * TH:(s + 1) * TH],
                                                  start=c == 0 and m == 0, stop=c == KD - 1 and m == 2)
                for c in range(2):
                    for s in range(2):
                        mm = nc.tensor.matmul(k.bank(4 * (n % 2) + 2 + s, TH), wt[:, n % ring, KD + c, :],
                                              p[:, c, s * TH:(s + 1) * TH], start=c == 0, stop=c == 1)
                mm.then_inc(multiplied, 1)

        @block.scalar
        def _(act):
            for n in range(KD + 1):
                if n < KD:
                    act.wait_ge(arrived[n % ring], 16 * (n // ring + 1))
                    if n >= 2:
                        act.wait_ge(multiplied, n - 1)
                    nc.scalar.activation(w_hi[:, n % 2], wt[:, n % ring, 0:KD, :], ACT.Copy).then_inc(rounded, 1)
                if n:
                    act.wait_ge(multiplied, n)
                    if n >= 3:
                        act.wait_ge(made, n - 2)
                    nc.scalar.activation(halves(sig[:, (n - 1) % 2, :]), k.pair(4 * ((n - 1) % 2)), ACT.Sigmoid).then_inc(gated, 1)

        @block.vector
        def _(dve):
            ch = Chain(dve, chain)
            for n in range(KD + 1):
                if n < KD:
                    dve.wait_ge(rounded, n + 1)
                    nc.vector.tensor_tensor(w_lo[:, n % 2], wt[:, n % ring, 0:KD, :], w_hi[:, n % 2].bitcast(F32),
                                            ALU.subtract).then_inc(parted, 1)
                if n:
                    m = n - 1
                    dve.wait_ge(gated, m + 1)
                    ch.link(nc.vector.tensor_tensor(halves(sig[:, m % 2, :]), halves(sig[:, m % 2, :]),
                                                    k.pair(4 * (m % 2) + 2), ALU.mult))
                    nc.vector.tensor_tensor(k.x[:, m, :], k.x[:, m, :], sig[:, m % 2, :], ALU.add).then_inc(made, 1)


def add_stage(k, y):
    nc = k.nc
    with ExitStack() as ctx:
        added, = k.sems(ctx, "added")
        block = ctx.enter_context(nc.Block())

        @block.vector
        def _(dve):
            nc.vector.tensor_tensor(k.x[:], k.x[:], y[:, :, :], ALU.add).then_inc(added, 1)
            dve.wait_ge(added, 1)


def layer_program(nc, d, n_phys):
    k = Core(nc)
    k.d, k.n_phys = d, n_phys
    with ExitStack() as whole:
        k.ps = whole.enter_context(nc.psum_tensor("ps", [P, 8, 512], F32))
        k.x = k.sb(whole, "x", [P, KD, T])
        k.params = k.sb(whole, "params", [P, NPARAM])
        k.ones = k.sb(whole, "ones", [P, P])
        k.blocks = k.sb(whole, "blocks", [P, P])
        k.ident = k.sb(whole, "ident", [P, P])
        k.gather = k.sb(whole, "gather", [P, 4, P])
        k.spread = k.sb(whole, "spread", [P, 4, P])
        k.gates = k.sb(whole, "gates", [P, 5, NGATE])
        k.table = k.sb(whole, "table", [1, DEC_BATCH * PAGES], mybir.dt.int32)
        load_stage(k)
        with ExitStack() as mixing:
            k.z = k.sb(mixing, "z", [P, NZ, T])
            rs = k.sb(mixing, "rs", [P, T])
            k.r = Tiles()
            k.r.o = k.z[:, 4:8, :]
            with ExitStack() as ctx:
                h = [k.sb(ctx, name, [P, KD, T], F32R) for name in ("h_hi", "h_lo")]
                wg = k.sb(ctx, "wg", [P, KD, NGATE])
                ring = WeightRing(k, ctx, d["w_in"])
                norm_stage(k, "attn_norm", *h, ring=ring, rs=rs)
                project_stage(k, ring, NZ, h, k.z, gates=(d["w_gates"], wg, k.gates))
            with ExitStack() as ctx:
                xs = k.sb(ctx, "xs", [P, RCOLS, T])
                k.r.kt, k.r.bt, k.r.bonus, k.r.g = (k.sb(ctx, name, [P, 4, T]) for name in ("kt", "bt", "bonus", "g"))
                k.r.ends = k.sb(ctx, "ends", [P, 4, NCH + DEC_BATCH])
                k.r.xs, k.r.rt, k.r.ht, k.r.vt = xs, xs[:, 0:4, :], xs[:, 4:8, :], xs[:, 8:12, :]
                rwkv_prepare_stage(k)
                rwkv_chunks_stage(k, sample=False)
                rwkv_chunks_stage(k, sample=True)
                rwkv_finish_stage(k)
            k.on = k.sb(mixing, "on", [P, 4, T])
            with ExitStack() as ctx:
                k.qr = k.sb(ctx, "qr", [P, 4, T])
                k.vs = k.sb(ctx, "vs", [P, 5, P])
                k.vw = k.sb(ctx, "vw", [P, 5, P])
                k.kc = k.sb(ctx, "kc", [P, DEC_BATCH, CH])
                k.vc = k.sb(ctx, "vc", [CH, DEC_BATCH, P])
                k.kcp = k.sb(ctx, "kcp", [P, 32])
                k.vcp = k.sb(ctx, "vcp", [32, P])
                compress_stage(k)
                nsa_prepare_stage(k)
                cached = CachedRows(k, ctx)
                prompt_attention_stage(k, cached)
                sample_attention_stage(k, cached)
            k.zg = k.sb(mixing, "zg", [P, 2 * KD, T])
            with ExitStack() as ctx:
                h = [k.sb(ctx, name, [P, KD, T], F32R) for name in ("h_hi", "h_lo")]
                ring = WeightRing(k, ctx, d["w_zg"])
                norm_stage(k, "attn_norm", *h, ring=ring, rs=rs, again=True)
                project_stage(k, ring, 2 * KD, h, k.zg)
            with ExitStack() as ctx:
                m = [k.sb(ctx, name, [P, KD, T], F32R) for name in ("m_hi", "m_lo")]
                ring = WeightRing(k, ctx, d["w_out"])
                merge_stage(k, *m, w_out=ring)
                project_stage(k, ring, KD, m, k.z[:, 8:16, :])
                add_stage(k, k.z[:, 8:16, :])
        k.clear_sems()
        k.g_dram = nc.dram_tensor("gate_matrix", (T // TB, P, N_KEYS * TB), F32).ap()
        with ExitStack() as ffn:
            h = [k.sb(ffn, name, [P, KD, T], F32R) for name in ("h_hi", "h_lo")]
            with ExitStack() as chosen:
                experts = ExpertRows(k, chosen)
                with ExitStack() as ctx:
                    picked = k.sb(ctx, "picked", [P, 3, T])
                    q = k.sb(ctx, "q", [P, KD, T])
                    with ExitStack() as projecting:
                        ring = WeightRing(k, projecting, d["peer_wq"])
                        norm_stage(k, "ffn_norm", *h, ring=ring)
                        project_stage(k, ring, KD, h, q)
                    choose_stage(k, q, picked)
                    gate_matrix_stage(k, picked, experts)
                y = k.sb(chosen, "y", [P, KD, T])
                experts_stage(k, h, y, experts)
                add_stage(k, y)
            with ExitStack() as ctx:
                ring = WeightRing(k, ctx, d["w_ple"], rows=KD + PLE // P)
                norm_stage(k, "ple_norm", *h, ring=ring)
                embed_stage(k, h, ring)



def _tiles(w):
    kk, n = w.shape
    return w.reshape(kk // P, P, n // P, P).transpose(2, 1, 0, 3).reshape(n // P, P, kk // P * P)


def _rows(w):
    c, t = w.shape
    return w.reshape(c // P, P, t).transpose(1, 0, 2).reshape(P, c // P * t)


def _constants():
    f = np.float32
    out = {}
    out["ones"] = np.ones((P, P), f)
    out["blocks"] = np.kron(np.eye(2), np.ones((HD, HD))).astype(f)
    out["ident"] = np.eye(P, dtype=f)
    row, tile = np.arange(P), np.arange(4)
    head = 2 * tile[None, :, None] + row[:, None, None] // HD
    out["gather"] = (row[None, None, :] // 16 == head).reshape(P, 4 * P).astype(f)
    head = 2 * tile[None, :, None] + row[None, None, :] // HD
    out["spread"] = (row[:, None, None] == 16 * head).reshape(P, 4 * P).astype(f)
    keep = np.ones((P, T), f)
    keep[:, 0:SEQ:CH] = 0
    keep[:, SEQ::DEC_SEQ] = 0
    out["keep"] = keep
    t = np.arange(CH)
    t2 = np.tile(t, 2)
    masks = []
    for inner, outer in ((16, CH), (DEC_SEQ, DEC_SEQ)):
        near = t[:, None] // inner == t[None, :] // inner
        within = t[:, None] // outer == t[None, :] // outer
        lower = t[:, None] > t[None, :]
        masks += [-1.0 * (near & lower), -1.0 * (near & lower.T), -1.0 * (within & ~near & lower),
                  1.0 * (within & lower.T), 1.0 * (within & ~lower), -1.0 * (within & ~lower)]
    out["masks"] = np.stack(masks, 1).reshape(CH, 12 * CH).astype(f)
    out["masks"] = np.tile(out["masks"], (2, 1))
    out["ident2"] = np.tile(np.eye(CH, dtype=f), (2, 1))
    out["seqmask"] = (t2[:, None] // DEC_SEQ == np.arange(DEC_BATCH)[None, :]).astype(f)
    pos = np.concatenate([np.arange(SEQ), np.tile(PAST + np.arange(DEC_SEQ), DEC_BATCH)]).astype(f)
    half = HD // 2
    inv = np.power(f(10000.0), -np.arange(half, dtype=f) / f(half)).astype(f)
    ang = (pos[None, :] * inv[:, None]).astype(f).astype(np.float64)
    out["rope"] = np.concatenate([np.tile(np.cos(ang), (4, 1)), np.tile(np.sin(ang), (4, 1))], 1).astype(f)
    rot = np.zeros((P, P), f)
    for base in range(0, P, HD):
        for j in range(half):
            rot[base + half + j, base + j] = -1
            rot[base + j, base + half + j] = 1
    out["rot"] = rot
    q = np.arange(P)
    out["tri"] = np.where(q[:, None] >= q[None, :], 0, NEG).astype(f)
    n = np.arange(32)
    cm = [np.where((CMP_STRIDE * n[None, :] + 31 <= qt * P + q[:, None]) & (n[None, :] < 31), 0, NEG) for qt in range(4)]
    out["cmask"] = np.concatenate(cm, 1).astype(f)
    row = np.arange(P)
    rs, rkv, ri, rt = row // 64, row // 32 % 2, row // 8 % 4, row % 8
    col = np.arange(TS)
    out["newmask"] = np.concatenate([np.where((col[None, :] // 8 == 2 * g + rs[:, None]) & (col[None, :] % 8 <= rt[:, None]),
                                              0, NEG) for g in range(4)], 1).astype(f)
    out["winmask"] = np.where(np.arange(8)[None, :] <= rt[:, None], NEG, 0).astype(f)
    out["pick"] = np.concatenate([col[:, None] == (8 * (2 * g + rs) + rt)[None, :] for g in range(4)], 1).astype(f)
    out["headmask"] = (np.arange(NGATE)[None, :] // 3 == (4 * rkv + ri)[:, None]).astype(f)
    key = rs * 100 + rkv * 10 + rt
    out["same"] = (key[:, None] == key[None, :]).astype(f)
    out["iota14"] = np.tile(np.arange(1, 15, dtype=f), (P, 1))
    out["iota16"] = np.tile(np.arange(16, dtype=f), (P, 1))
    out["iota128"] = np.tile(np.arange(128, dtype=f), (P, 1))
    return out


def _lay_out(x_prompt, x_sample, cache_cmp_kv, cache_sel_kv, state_win_kv, state_wkv, state_shift, page_table,
             p_prompt, p_sample, attn_norm, w_in, rwkv_mu, rwkv_w0, rwkv_w_up, rwkv_a0, rwkv_a_up, rwkv_g_up,
             rwkv_k_k, rwkv_k_a, rwkv_r_k, rwkv_gn_w, rwkv_gn_b, w_rwkv_out, q_norm, k_norm, cmp_pe, cmp_w1,
             cmp_w2, w_nsa_out, w_out, ffn_norm, peer_wq, peer_keys, peer_u, peer_v, ple_norm, ple_w_gate, ple_w_in):
    d = _constants()
    n_phys = cache_cmp_kv.shape[1]
    d["x"] = _rows(np.concatenate([x_prompt[0], x_sample.reshape(TS, D_MODEL)], 0).T)
    d["p"] = _rows(np.concatenate([p_prompt[0, 0], p_sample[0].reshape(TS, PLE)], 0).T)
    params = dict(attn_norm=attn_norm[0], ffn_norm=ffn_norm[0], ple_norm=ple_norm[0], mu=rwkv_mu[0], w0=rwkv_w0[0],
                  a0=rwkv_a0[0], k_k=rwkv_k_k[0], k_a=rwkv_k_a[0], r_k=rwkv_r_k[0].reshape(-1), gn_w=rwkv_gn_w[0],
                  gn_b=rwkv_gn_b[0], q_norm=np.tile(q_norm[0], 2), k_norm=np.tile(k_norm[0], (1, 2)).reshape(-1))
    d["params"] = np.concatenate([params[n].reshape(-1, P).T for n in PARAMS], 1)
    order = np.concatenate([np.r_[i * HD:(i + 1) * HD, (4 + i) * HD:(5 + i) * HD] for i in range(4)])
    r0 = RCOLS * P
    kv_end = r0 + 512 + 6 * P
    w = w_in[0]
    d["w_in"] = _tiles(np.concatenate([w[:, :r0], w[:, r0:r0 + 512][:, order], w[:, r0 + 512:kv_end]], 1))
    d["w_zg"] = _tiles(w[:, kv_end + NGATE:])
    d["w_gates"] = _rows(w[:, kv_end:kv_end + NGATE])
    d["up"] = np.concatenate([np.concatenate([rwkv_w_up[0], rwkv_a_up[0]], 0), rwkv_g_up[0]], 1)
    d["shift"] = _rows(state_shift[0].T)
    d["states"] = state_wkv[0].reshape(DEC_BATCH, 4, 2, HD, HD).transpose(2, 4, 1, 0, 3).reshape(P, -1)
    pages = cache_cmp_kv[0].reshape(n_phys, 8, 8, 2, 2, 2, HD)
    d["cmp_pages"] = pages.transpose(0, 3, 6, 2, 4, 5, 1).reshape(n_phys, P, 256)
    sel = cache_sel_kv[0].reshape(n_phys, PAGE, 2, P)
    d["sel_pages"] = np.concatenate([sel[:, :, 0].transpose(0, 2, 1), sel[:, :, 1]], 2)
    win = state_win_kv[0].reshape(DEC_BATCH // 2, 2, WINDOW, 2, P)
    d["win_k"] = win[:, :, :, 0].transpose(0, 3, 1, 2).reshape(4, P, 2 * WINDOW)
    d["win_v"] = win[:, :, :, 1].reshape(4, 2, 4, P, P).transpose(0, 3, 1, 2, 4).reshape(4, P, 2 * 4 * P)
    d["win_rows"] = state_win_kv[0][:, DEC_SEQ:].reshape(DEC_BATCH, -1)
    d["page_table"] = page_table.reshape(1, -1)
    d["cmp_w1"] = cmp_w1[0].reshape(2, 2, 8, 2, HD, CMP_HIDDEN).transpose(3, 4, 2, 0, 1, 5).reshape(P, -1)
    d["cmp_pe"] = cmp_pe[0].reshape(2, 2, 8, 2, HD).transpose(3, 4, 2, 0, 1).reshape(P, -1)
    d["cmp_w2"] = cmp_w2[0].reshape(2, 2, P, HD).transpose(2, 0, 1, 3).reshape(P, -1)
    d["w_merge"] = np.concatenate([_tiles(w_rwkv_out[0]), _tiles(w_nsa_out[0][order])], 2)
    d["w_out"] = _tiles(w_out[0])
    d["peer_wq"] = _tiles(peer_wq[0])
    d["keys"] = peer_keys[0].transpose(1, 3, 0, 2).reshape(P, -1)
    d["peer_u"] = peer_u[0].reshape(N_KEYS, P, KD, P).transpose(0, 3, 2, 1).reshape(N_KEYS, P, KD * P)
    d["peer_v"] = peer_v[0].reshape(N_KEYS, P, D_MODEL)
    d["w_ple"] = np.concatenate([_tiles(ple_w_gate[0]), _tiles(ple_w_in[0])], 2)
    return {n: np.ascontiguousarray(a) for n, a in d.items()}, n_phys


_OUTS = dict(out_y=(KD, P, T), out_kv=(P, 6 * T), out_win=(DEC_BATCH, (WINDOW - DEC_SEQ) * 2 * P),
             out_state=(P, 4 * HD), out_states=(P, 4 * DEC_BATCH * HD), out_shift=(P, RCOLS * 9))


def kernel(**inputs):
    import concourse.bacc as _bacc
    from concourse import mybir as _mybir
    from concourse.bass_utils import run_bass_kernel_spmd as _run

    arrays, n_phys = _lay_out(**{n: np.asarray(a) for n, a in inputs.items()})
    nc = _bacc.Bacc("TRN2", target_bir_lowering=False, num_devices=1)
    d = {n: nc.dram_tensor(f"in_{n}", a.shape, _mybir.dt.from_np(a.dtype), kind="ExternalInput").ap()
         for n, a in arrays.items()}
    for n, shape in _OUTS.items():
        d[n] = nc.dram_tensor(n, shape, F32, kind="ExternalOutput").ap()
    layer_program(nc, d, n_phys)
    r = _run(nc, [{f"in_{n}": a for n, a in arrays.items()}], core_ids=[0]).results[0]

    y = r["out_y"].reshape(D_MODEL, T).T
    kv = r["out_kv"].reshape(2, HD, 3, 2, T).transpose(2, 4, 3, 0, 1)
    prompt = [np.ascontiguousarray(kv[b, :SEQ])[None, None] for b in range(3)]
    new = [np.ascontiguousarray(kv[b, SEQ:]).reshape(1, DEC_BATCH, DEC_SEQ, 2, 2, HD) for b in range(3)]
    win = np.concatenate([r["out_win"].reshape(1, DEC_BATCH, WINDOW - DEC_SEQ, 2, 2, HD), new[2]], 2)
    state = r["out_state"].reshape(2, HD, 4, HD).transpose(2, 0, 3, 1).reshape(1, 1, HEADS, HD, HD)
    states = r["out_states"].reshape(2, HD, 4, DEC_BATCH, HD).transpose(3, 2, 0, 4, 1).reshape(1, DEC_BATCH, HEADS, HD, HD)
    shift = r["out_shift"].reshape(P, RCOLS, 9).transpose(2, 1, 0).reshape(9, RCOLS * P)
    out = (y[:SEQ][None], y[SEQ:].reshape(DEC_BATCH, DEC_SEQ, D_MODEL), prompt[0], new[0], prompt[1], new[1],
           prompt[2], win, state, states, shift[None, 0:1], shift[None, 1:])
    return tuple(np.ascontiguousarray(a) for a in out)
```
